# Optimizing a Trainium2 kernel written in Bass

```python
import jax, jax.numpy as jnp
from jax import lax
import numpy as np

D_MODEL = 1024
BATCH = 1
SEQ = 512
DEPTH = 1

PLE_DIM = 256
D_CONV = 512
CONV_A_WIDTH = 3
N_HEADS = 4
HEAD_K = 128
HEAD_V = 128
D_DN_K = N_HEADS * HEAD_K
D_DN_V = N_HEADS * HEAD_V
CONV_DN_WIDTH = 3
CHUNK = 64
D_FF = 4 * D_MODEL
EPS = 1e-6

SPLITS = (D_CONV, D_CONV, D_CONV, 2 * D_DN_K + D_DN_V, D_DN_V,
          N_HEADS, N_HEADS, N_HEADS, N_HEADS, D_MODEL, D_MODEL)
D_IN_PROJ = sum(SPLITS)

kernel_name = "hybrid_gated_conv_deltanet_encoder_block"

def _split_points():
    pts, acc = [], 0
    for w in SPLITS[:-1]:
        acc += w
        pts.append(acc)
    return pts

def rms_norm(x, g):
    xf = x.astype(jnp.float32)
    y = xf * lax.rsqrt(jnp.mean(xf * xf, axis=-1, keepdims=True) + EPS)
    return (y * g.astype(jnp.float32)).astype(x.dtype)

def l2_norm(x):
    return x * lax.rsqrt(jnp.sum(x * x, axis=-1, keepdims=True) + EPS)

def dwconv_centred(x, w):
    k = w.shape[0]
    r = k // 2
    s = x.shape[1]
    xp = jnp.pad(x, ((0, 0), (r, r), (0, 0)))
    return sum(xp[:, j:j + s, :] * w[j] for j in range(k))

def gated_delta_rule(q, k, v, g, beta):
    b, s, h, dk = q.shape
    dv = v.shape[-1]
    n = s // CHUNK

    def chunks(t):
        return t.reshape(b, n, CHUNK, h, -1).transpose(0, 3, 1, 2, 4)

    q, k, v = chunks(q), chunks(k), chunks(v)
    g = jnp.cumsum(g.reshape(b, n, CHUNK, h).transpose(0, 3, 1, 2), axis=-1)
    beta = beta.reshape(b, n, CHUNK, h).transpose(0, 3, 1, 2)

    tri = jnp.tril(jnp.ones((CHUNK, CHUNK), dtype=bool))
    strict = jnp.tril(jnp.ones((CHUNK, CHUNK), dtype=bool), -1)
    decay = jnp.exp(jnp.where(tri, g[..., :, None] - g[..., None, :], -jnp.inf))

    kb = k * beta[..., None]
    vb = v * beta[..., None]
    a = jnp.where(strict, jnp.einsum('bhncd,bhnjd->bhncj', kb, k) * decay, 0.0)
    eye = jnp.eye(CHUNK, dtype=jnp.float32)
    t_inv = lax.linalg.triangular_solve(eye + a, jnp.broadcast_to(eye, a.shape),
                                        left_side=True, lower=True, unit_diagonal=True)
    u = t_inv @ vb
    w = t_inv @ (kb * jnp.exp(g)[..., None])
    intra = jnp.einsum('bhncd,bhnjd->bhncj', q, k) * decay

    def step(state, inp):
        q_c, k_c, u_c, w_c, g_c, a_c = inp
        v_new = u_c - w_c @ state
        o = (q_c * jnp.exp(g_c)[..., None]) @ state + a_c @ v_new
        g_last = g_c[..., -1]
        state = state * jnp.exp(g_last)[..., None, None] + jnp.einsum(
            'bhcd,bhce->bhde', k_c * jnp.exp(g_last[..., None] - g_c)[..., None], v_new)
        return state, o

    xs = tuple(jnp.moveaxis(t, 2, 0) for t in (q, k, u, w, g, intra))
    state0 = jnp.zeros((b, h, dk, dv), jnp.float32)
    _, o = lax.scan(step, state0, xs)
    return o.transpose(1, 0, 3, 2, 4).reshape(b, s, h, dv)

def setup_inputs(seed: int = 0) -> dict:
    key = jax.random.key(seed)
    ks = jax.random.split(key, 24)
    L = DEPTH
    f32 = jnp.float32

    def dense(k, fan_in, fan_out):
        return jax.random.normal(k, (L, fan_in, fan_out), f32) * fan_in ** -0.5

    def gain(k, n):
        return 1.0 + 0.02 * jax.random.normal(k, (L, n), f32)

    a_log_f = jnp.log(jax.random.uniform(ks[5], (L, N_HEADS), f32, 1.0, 16.0))
    a_log_b = jnp.log(jax.random.uniform(ks[6], (L, N_HEADS), f32, 1.0, 16.0))

    def dt_bias(k):
        u = jax.random.uniform(k, (L, N_HEADS), f32)
        dt = jnp.exp(u * (jnp.log(0.1) - jnp.log(0.001)) + jnp.log(0.001))
        return dt + jnp.log(-jnp.expm1(-dt))

    return {
        "x": jax.random.normal(ks[0], (BATCH, SEQ, D_MODEL), f32),
        "p": jax.random.normal(ks[1], (DEPTH, BATCH, SEQ, PLE_DIM), f32),
        "g_mix": gain(ks[2], D_MODEL),
        "w_in": dense(ks[3], D_MODEL, D_IN_PROJ),
        "conv_a": jax.random.normal(ks[4], (L, CONV_A_WIDTH, D_CONV), f32) * CONV_A_WIDTH ** -0.5,
        "conv_qkv": jax.random.normal(ks[7], (L, CONV_DN_WIDTH, 2 * D_DN_K + D_DN_V), f32) * CONV_DN_WIDTH ** -0.5,
        "a_log_f": a_log_f,
        "a_log_b": a_log_b,
        "dt_bias_f": dt_bias(ks[8]),
        "dt_bias_b": dt_bias(ks[9]),
        "g_dn_norm": gain(ks[10], HEAD_V),
        "w_a_out": dense(ks[11], D_CONV, D_MODEL),
        "w_dn_out": dense(ks[12], D_DN_V, D_MODEL),
        "w_o": dense(ks[13], D_MODEL, D_MODEL),
        "g_ffn": gain(ks[14], D_MODEL),
        "w_ff1": dense(ks[15], D_MODEL, D_FF),
        "w_ff2": dense(ks[16], D_FF, D_MODEL),
        "g_ple": gain(ks[17], D_MODEL),
        "w_ple_gate": dense(ks[18], D_MODEL, D_MODEL),
        "w_ple_proj": dense(ks[19], PLE_DIM, D_MODEL),
        "g_final": 1.0 + 0.02 * jax.random.normal(ks[20], (D_MODEL,), f32),
    }

def reference(x, p, g_mix, w_in, conv_a, conv_qkv, a_log_f, a_log_b, dt_bias_f, dt_bias_b,
              g_dn_norm, w_a_out, w_dn_out, w_o, g_ffn, w_ff1, w_ff2, g_ple, w_ple_gate,
              w_ple_proj, g_final):
    b, s, _ = x.shape
    f32 = jnp.float32
    h = x
    for i in range(DEPTH):
        n = rms_norm(h, g_mix[i])
        proj = n @ w_in[i]
        (b_a, c_a, x_a, qkv, z, beta_f, beta_b, alpha_f, alpha_b,
         gate_a, gate_dn) = jnp.split(proj, _split_points(), axis=-1)

        y_a = c_a * dwconv_centred(b_a * x_a, conv_a[i])

        qkv = jax.nn.silu(dwconv_centred(qkv, conv_qkv[i]))
        q, k, v = jnp.split(qkv, [D_DN_K, 2 * D_DN_K], axis=-1)
        q = l2_norm(q.reshape(b, s, N_HEADS, HEAD_K).astype(f32)) * HEAD_K ** -0.5
        k = l2_norm(k.reshape(b, s, N_HEADS, HEAD_K).astype(f32))
        v = v.reshape(b, s, N_HEADS, HEAD_V).astype(f32)
        g_f = -jnp.exp(a_log_f[i].astype(f32)) * jax.nn.softplus(alpha_f.astype(f32) + dt_bias_f[i].astype(f32))
        g_b = -jnp.exp(a_log_b[i].astype(f32)) * jax.nn.softplus(alpha_b.astype(f32) + dt_bias_b[i].astype(f32))
        bt_f = jax.nn.sigmoid(beta_f.astype(f32))
        bt_b = jax.nn.sigmoid(beta_b.astype(f32))
        flip = lambda t: jnp.flip(t, axis=1)
        o = gated_delta_rule(q, k, v, g_f, bt_f) + flip(
            gated_delta_rule(flip(q), flip(k), flip(v), flip(g_b), flip(bt_b)))
        o = rms_norm(o, g_dn_norm[i]) * jax.nn.silu(z.reshape(b, s, N_HEADS, HEAD_V).astype(f32))
        y_dn = o.reshape(b, s, D_DN_V).astype(h.dtype)

        merged = (jax.nn.sigmoid(gate_a) * (y_a @ w_a_out[i])
                  + jax.nn.sigmoid(gate_dn) * (y_dn @ w_dn_out[i]))
        h = h + merged @ w_o[i]

        n2 = rms_norm(h, g_ffn[i])
        h = h + jnp.square(jax.nn.relu(n2 @ w_ff1[i])) @ w_ff2[i]

        gate_p = jax.nn.sigmoid(rms_norm(h, g_ple[i]) @ w_ple_gate[i])
        h = h + gate_p * (p[i] @ w_ple_proj[i])
    return rms_norm(h, g_final)


_drawn_inputs = setup_inputs


def setup_inputs(seed=0):
    import zlib

    import numpy as np

    out = dict(_drawn_inputs(seed))
    spreads = {}
    factors = {'g_mix': 2.929,
     'a_log_f': 24.317,
     'g_dn_norm': 35.199,
     'g_ffn': 13.674,
     'g_ple': 200.0,
     'g_final': 25.949,
     'dt_bias_f': 51.32,
     'w_ple_gate': 24.48,
     'p': 8.0,
     'w_ple_proj': 8.0}
    for name, (base, spread) in spreads.items():
        noise = np.random.default_rng([zlib.crc32(name.encode()), seed]).standard_normal(out[name].shape)
        drawn = base * np.exp(spread * noise) if base else spread * noise
        out[name] = __import__('jax').numpy.asarray(drawn.astype(out[name].dtype))
    for name, factor in factors.items():
        out[name] = (out[name] * factor).astype(out[name].dtype)
    return out
```

```python
from contextlib import ExitStack

import numpy as np

import concourse.bass as bass
from concourse import mybir

ALU = mybir.AluOpType
ACT = mybir.ActivationFunctionType
F32 = mybir.dt.float32
F32R = mybir.dt.float32r
BF16 = mybir.dt.bfloat16

P = 128
TOK = 512
D = 1024
KD = D // P
H = 4
NC = TOK // P
LEVELS = 7
D_FF = 4 * D
EPS = 1e-6
DIRS = 2

SLAB = 2048
UNITS = 16
S_K, S_V, S_Q = 0, 2, 4
S_BXC = 6
S_WA = 12
S_GA = 14
S_Z = 18
S_GD = 20
S_WD = 24
S_WO = 26
S_FF = 30
FF_GROUPS = 4
FF_SLABS = 8
S_PP = S_FF + FF_GROUPS * FF_SLABS
S_PG = S_PP + 1
N_SLABS = S_PG + 4
RING = 2
SQ = 3

C_GMIX, C_GFFN, C_GPLE, C_GFIN = 0, 8, 16, 24
C_CONVA = 32
C_CONVQ = C_CONVA + 12
C_GDN = C_CONVQ + 36
C_ALOG = C_GDN + 1
C_DTB = C_ALOG + 8
C_W16 = C_DTB + 8
N_COLS = C_W16 + KD * 16 + 7


def tiles_of(s):
    if s in (S_WA, S_WA + 1, S_WD, S_WD + 1):
        return 4
    return 8 if s == S_PP else 2


def first_tile(s):
    return sum(tiles_of(r) for r in range(s))


WINDOW0 = S_BXC
WINDOW = 3 * UNITS
DECAY_AT = {2: 0, 4: 1}
PRODUCTS_AT = {9: 0, 12: 1}
LEVEL_AT = {15: [("v", 0, 0)], 16: [("v", 0, 1)],
            45: [("v", 6, 0)], 46: [("v", 6, 1)], 47: [("x", 6, 0), ("x", 6, 1)]}
for _l, _b in enumerate((18, 24, 29, 35, 40), 1):
    LEVEL_AT[_b] = [("v", _l, 0)]
    LEVEL_AT[_b + 1] = [("v", _l, 1)]
    LEVEL_AT[_b + 3] = [("x", _l, 0)]
    LEVEL_AT[_b + 4] = [("x", _l, 1)]
SCAN_AT = {3: ("read", 0), 10: ("solve", 0), 17: ("write", 0), 23: ("read", 1), 31: ("solve", 1), 38: ("write", 1)}


def window_of(s, j):
    t = (s - WINDOW0) * UNITS + j
    if 0 <= t < (NC + 1) * WINDOW:
        return t // WINDOW, t % WINDOW
    return None, None


def chunk_of(n, d):
    return n if d == 0 else NC - 1 - n


def pair(n, d):
    return DIRS * n + d + 1


def level(n, l, d):
    return (n * LEVELS + l) * DIRS + d + 1


def upper(n, l, d):
    return (n * (LEVELS - 1) + l - 1) * DIRS + d + 1


def encoder_block(nc, x_t, p_t, stream, cols_in, masks_in, levels_in, out):
    with ExitStack() as ctx:
        def sb(name, shape, dt=F32):
            return ctx.enter_context(nc.sbuf_tensor(name, shape, dt))

        def sem(name):
            return ctx.enter_context(nc.semaphore(name))

        raw = sb("raw", [P, RING, SLAB])
        w_hi = sb("w_hi", [P, RING, SLAB], F32R)
        w_lo = sb("w_lo", [P, RING, SLAB], F32R)
        act_hi = sb("act_hi", [P, KD, TOK], F32R)
        act_lo = sb("act_lo", [P, KD, TOK], F32R)
        y_hi = sb("y_hi", [P, H, TOK], F32R)
        y_lo = sb("y_lo", [P, H, TOK], F32R)
        cols = sb("cols", [P, N_COLS])
        masks = sb("masks", [P, 6, P])
        lmask = sb("lmask", [P, DIRS * LEVELS, P], BF16)
        beta = sb("beta", [P, NC, DIRS * H])
        gate = sb("gate", [P, NC, DIRS * H])
        e_cols = sb("e_cols", [P, 3, DIRS, NC, H])
        neg_run = sb("neg_run", [P, DIRS, NC, H])
        c1 = sb("c1", [P, NC, DIRS, H])
        k_cols = sb("k_cols", [P, 5, NC * H])
        q_sq = sb("q_sq", [P, NC * H])
        o_sq = sb("o_sq", [P, NC * H])
        norm_t = sb("norm_t", [P, 6, NC * H])

        KB = 256
        arena_stack = ExitStack()
        arena = arena_stack.enter_context(nc.sbuf_tensor("arena", [P, 102 * KB], F32))

        def carve(start_kb, *shape):
            flat = arena[:, start_kb * KB:start_kb * KB + int(np.prod(shape))]
            names = " ".join(f"a{i}" for i in range(len(shape)))
            sizes = {f"a{i}": shape[i] for i in range(1, len(shape))}
            return flat.rearrange(f"p ({names}) -> p {names}", **sizes) if len(shape) > 1 else flat

        x_in = carve(0, KD, TOK)
        n_f = carve(16, 4, TOK)
        sq_in = carve(24, SQ, TOK)
        diag0 = carve(32, TOK)
        rb0 = carve(34, TOK)
        tiny = carve(65, 6, NC * DIRS * H)
        ba = carve(66, NC, 16)
        k_t = carve(0, H, TOK)
        q_t = carve(8, H, TOK)
        k_tok = carve(16, NC, H, P)
        v_tok = carve(24, NC, H, P)
        decay = carve(32, 2, DIRS, H, P)
        inv_t = carve(40, 2, DIRS, H, P)
        inv = carve(48, DIRS, H, P)
        a_t = carve(52, DIRS, H, P)
        v_buf = carve(56, DIRS, H, P)
        r_buf = carve(60, DIRS, H, P)
        w_buf = carve(64, DIRS, H, P)
        w_dec = carve(68, DIRS, H, P)
        state = carve(72, DIRS, H, P)
        sq_qk = carve(36, 2, TOK)
        sig_a = carve(76, TOK)
        v_t = carve(78, H, TOK)
        o_acc = carve(78, NC, H, P)
        conv_t = carve(86, 2, TOK)
        b_sb = carve(90, 2, TOK)
        bx = carve(94, 2, TOK)
        ya = carve(98, 2, TOK)
        mixed = carve(86, KD, TOK)
        z_silu = carve(48, H, TOK)
        sig_d = carve(0, KD, TOK)
        o_junk = carve(32, P)
        yd_f = carve(56, 2, TOK)
        mg_f = carve(60, 2, TOK)
        h_t = carve(64, KD, TOK)
        relu_t = carve(80, 2, TOK)
        hid_f = carve(84, 2, TOK)
        rb = carve(88, TOK)
        diag = carve(90, TOK)
        sq_t = carve(92, SQ, TOK)
        p_in = carve(98, 2, TOK)
        ple = carve(32, KD, TOK)
        sig_p = carve(48, 2, TOK)
        arena_stack.close()
        f_hi = sb("f_hi", [P, KD, TOK], F32R)
        f_lo = sb("f_lo", [P, KD, TOK], F32R)
        hid_hi = sb("hid_hi", [P, 8, TOK], F32R)
        hid_lo = sb("hid_lo", [P, 8, TOK], F32R)
        w16_hi = sb("w16_hi", [P, KD * 16], F32R)
        w16_lo = sb("w16_lo", [P, KD * 16], F32R)
        sb("arena_rest", [P, 37 * KB])

        ident, incl_f, incl_b, strict_f, strict_b, ones = (masks[:, i, :] for i in range(6))
        incl = (incl_f, incl_b)
        strict = (strict_f, strict_b)

        dense = ctx.enter_context(nc.psum_tensor("dense", [P, 4, TOK], F32))
        extra = ctx.enter_context(nc.psum_tensor("extra", [P, 4, TOK], F32))

        cols_in_s, masks_in_s, levels_in_s = sem("cols_landed"), sem("masks_landed"), sem("levels_landed")
        x_in_s = [sem(f"x_landed{i}") for i in range(4)]
        x2_in_s, p_in_s, out_s = sem("x_again_landed"), sem("p_landed"), sem("out_stored")
        raw_s = [sem(f"raw_landed{i}") for i in range(RING)]
        hi_s, lo_s, tile_s = sem("w_hi_made"), sem("w_lo_made"), sem("tile_done")
        read_s = [sem(f"tile_read{i}") for i in range(4)]
        sq_s, sqsum_s, ms_s, root_s = sem("square_made"), sem("square_summed"), sem("mean_made"), sem("root_made")
        diag_s, rbps_s, rb_s = sem("diag_made"), sem("rstd_spread"), sem("rstd_copied")
        nf_s, nhi_s, nlo_s = sem("norm_made"), sem("norm_hi_made"), sem("norm_lo_made")
        w16h_s, w16l_s, ba_s, bac_s = sem("w16_hi_made"), sem("w16_lo_made"), sem("ba_done"), sem("ba_copied")
        beta_s, abs_s, exp_s, aexp_s = sem("beta_made"), sem("alpha_abs"), sem("alpha_exp"), sem("a_exp")
        g_s, gsum_s, ecol_s = sem("gate_made"), sem("gate_sums"), sem("decay_columns")
        ksq_s, kroot_s, qsq_s = sem("k_sq_made"), sem("k_root"), sem("q_sq_made")
        tap_s, silu_s, qksq_s, ss_s, tr_s = (sem("centre_tap"), sem("silu_made"), sem("qk_squared"),
                                             sem("qk_summed"), sem("kv_transposed"))
        kcopy_s, vcopy_s = sem("k_tok_made"), sem("v_tok_made")
        yd_s, yh_s, yl_s = sem("y_dn_made"), sem("y_hi_made"), sem("y_lo_made")
        siga_s, sigau_s, mg_s = sem("gate_a_made"), sem("gate_a_applied"), sem("merged")
        gm_s, dsum_s, dexp_s, dmask_s = sem("decay_rhs"), sem("decay_sums"), sem("decay_exp"), sem("decay_masked")
        prod_s, at_s = sem("kk_qk_done"), sem("a_made")
        v_s, vm_s, xvx_s, xu_s = sem("ax_done"), sem("ax_masked"), sem("xax_done"), sem("inverse_updated")
        sread_s, r_s, qs_s = sem("state_read"), sem("r_made"), sem("qs_added")
        xr_s, w_s, wd_s = sem("solved"), sem("w_made"), sem("w_decayed")
        in_s, ds_s, oadd_s, st_s = sem("intra_done"), sem("ds_done"), sem("o_added"), sem("state_made")
        osq_s, omean_s, oroot_s, onorm_s, otr_s = (sem("o_squared"), sem("o_mean"), sem("o_root"),
                                                   sem("o_normed"), sem("o_transposed"))
        hp_s = sem("ple_added")
        hh_s, hf_s, hl_s = sem("hid_hi_made"), sem("hid_squared"), sem("hid_lo_made")
        ph_s, pl_s, gp_s, fin_s = sem("p_hi_made"), sem("p_lo_made"), sem("ple_gate"), sem("final_made")
        dv_s = sem("vector_steps")
        ac_s = sem("scalar_steps")

        FF_T0 = first_tile(S_FF)
        assert FF_T0 % 4 == 0 and S_FF % RING == 0 and FF_SLABS % RING == 0

        def bank(u):
            return dense[:, u % 4, :]

        def split_view(t, s, nk=KD):
            return t[:, s % RING, :].rearrange("p (k n) -> p k n", k=nk)

        def conv_col(i, tap):
            at = C_CONVQ + tap * 3 * H + (i + H if i < 2 * H else i - 2 * H)
            return cols[:, at:at + 1]

        def over_heads(m):
            return m.unsqueeze(1).broadcast_to([P, H, P])

        def half(m, l, side):
            return m.rearrange("p h (b two s) -> p h b two s", two=2, s=1 << l)[:, :, :, side, :]

        def half1(m, l, side):
            return m.rearrange("p (b two s) -> p b two s", two=2, s=1 << l)[:, :, side, :]

        def wait_read(eng, u):
            eng.wait_ge(read_s[u % 4], u // 4 + 1)

        def tile_ends(s, j):
            nk = UNITS // tiles_of(s)
            return j // nk if j % nk == nk - 1 else None

        block = ctx.enter_context(nc.Block())

        @block.sync
        def _(sp):
            for i in range(4):
                sp.dma_start(x_in[:, 2 * i:2 * i + 2, :], x_t[:, 2 * i:2 * i + 2, :]).then_inc(x_in_s[i], 16)
            sp.dma_start(masks[:], masks_in).then_inc(masks_in_s, 16)
            sp.dma_start(cols[:], cols_in).then_inc(cols_in_s, 16)
            for s in range(RING):
                sp.dma_start(raw[:, s, :], stream[s]).then_inc(raw_s[s], 16)
            sp.dma_start(lmask[:], levels_in).then_inc(levels_in_s, 16)

            def slab_pair(i):
                for r in range(RING):
                    sp.wait_ge(lo_s, i * RING + (r + 1 - RING))
                    sp.dma_start(raw[:, r, :], stream[bass.ds(i * RING + r, 1)].rearrange("s p n -> p (s n)"))\
                      .then_inc(raw_s[r], 16)

            with sp.Fori(1, S_WD // RING) as i:
                slab_pair(i)
            sp.wait_ge(otr_s, H)
            sp.dma_start(h_t, x_t).then_inc(x2_in_s, 16)
            with sp.Fori(S_WD // RING, S_FF // RING) as i:
                slab_pair(i)
            sp.wait_ge(mg_s, KD)
            sp.dma_start(p_in, p_t).then_inc(p_in_s, 16)
            with sp.Fori(S_FF // RING, S_PP // RING) as i:
                slab_pair(i)
            for s in range(S_PP, N_SLABS):
                sp.wait_ge(lo_s, s + 1 - RING)
                sp.dma_start(raw[:, s % RING, :], stream[s]).then_inc(raw_s[s % RING], 16)
            for m in range(0, KD, 2):
                sp.wait_ge(fin_s, m + 2)
                sp.dma_start(out[:, m:m + 2, :], h_t[:, m:m + 2, :]).then_inc(out_s, 16)
            sp.wait_ge(out_s, 16 * (KD // 2))

        @block.tensor
        def _(pe):
            mm = nc.tensor.matmul

            def three(o, wh, wl, ah, al, first, last):
                mm(o, wh, ah, start=first, stop=False)
                mm(o, wh, al, start=False, stop=False)
                return mm(o, wl, ah, start=False, stop=last)

            def unit(s, j, src):
                nk = UNITS // tiles_of(s)
                m, k = divmod(j, nk)
                wh, wl = split_view(w_hi, s, nk), split_view(w_lo, s, nk)
                if j == 0:
                    pe.wait_ge(hi_s, s + 1)
                    pe.wait_ge(lo_s, s + 1)
                u = first_tile(s) + m
                if k == 0 and u >= 4:
                    pe.wait_ge(read_s[u % 4], u // 4)
                ah, al = src
                last = three(bank(u), wh[:, k, m * P:(m + 1) * P], wl[:, k, m * P:(m + 1) * P],
                             ah[:, k, :], al[:, k, :], k == 0, k == nk - 1)
                if k == nk - 1:
                    last.then_inc(tile_s, 1)

            def norm_sum(r, k, sq):
                i = r * KD + k
                pe.wait_ge(sq_s, i + 1)
                for c in range(NC):
                    last = mm(extra[:, c, 0:1], sq[:, i % SQ, c * P:(c + 1) * P], ones[:, 0:1],
                              start=k == 0, stop=k == KD - 1)
                last.then_inc(sqsum_s, 1)

            def norm_spread(r, dg):
                pe.wait_ge(diag_s, r + 1)
                mm(extra[:, 0, :], ones, dg, start=True, stop=True).then_inc(rbps_s, 1)

            def small_projection():
                pe.wait_ge(w16h_s, 1)
                pe.wait_ge(w16l_s, 1)
                pe.wait_ge(rb_s, 1)
                wh = w16_hi[:].rearrange("p (k n) -> p k n", k=KD)
                wl = w16_lo[:].rearrange("p (k n) -> p k n", k=KD)
                for c in range(NC):
                    t = slice(c * P, (c + 1) * P)
                    o = extra[:, 0, 16 * c:16 * c + 16]
                    for k in range(KD):
                        mm(o, act_hi[:, k, t], wh[:, k, :], start=k == 0, stop=False)
                        mm(o, act_lo[:, k, t], wh[:, k, :], start=False, stop=False)
                        last = mm(o, act_hi[:, k, t], wl[:, k, :], start=False, stop=k == KD - 1)
                last.then_inc(ba_s, 1)

            def gate_sums():
                pe.wait_ge(g_s, 1)
                for q, lhs in enumerate((incl, strict, (ones, ones))):
                    for d in range(DIRS):
                        at = (q * DIRS + d) * NC * H
                        last = mm(extra[:, 1, at:at + NC * H].rearrange("p (c h) -> p c h", c=NC),
                                  lhs[d], gate[:, :, d * H:(d + 1) * H], start=True, stop=True)
                last.then_inc(gsum_s, 1)

            def square_sums(i, h, which):
                pe.wait_ge(qksq_s, i + 1)
                for c in range(NC):
                    last = mm(extra[:, which, c * H + h:c * H + h + 1], sq_qk[:, i % 2, c * P:(c + 1) * P], ones[:, 0:1],
                              start=True, stop=True)
                last.then_inc(ss_s, 1)

            def to_tokens(i, src, h):
                pe.wait_ge(silu_s, i + 1)
                if 2 <= i < 6:
                    pe.wait_ge(kcopy_s, i - 1)
                elif i >= 6:
                    pe.wait_ge(vcopy_s, i - 5)
                for c in range(NC):
                    last = nc.tensor.transpose(extra[:, 2 + i % 2, c * P:(c + 1) * P],
                                               src[:, h, c * P:(c + 1) * P], ident)
                last.then_inc(tr_s, 1)

            def qkv_aux(i):
                h = i % H
                if i < H:
                    if i == 0:
                        pe.wait_ge(bac_s, 1)
                    square_sums(i, h, 0)
                    to_tokens(i, k_t, h)
                elif i < 2 * H:
                    to_tokens(i, v_t, h)
                else:
                    if i == 2 * H:
                        pe.wait_ge(vcopy_s, 4)
                    square_sums(i - H, h, 3)

            def decay_sums(n, d):
                pe.wait_ge(gm_s, pair(n, d))
                if n == 0:
                    pe.wait_ge(ksq_s if d == 0 else ecol_s, 1)
                else:
                    pe.wait_ge(xu_s, level(n - 1, LEVELS - 1, d))
                mm(extra[:, d, :], strict[d], v_buf[:, d].rearrange("p h n -> p (h n)"),
                   start=True, stop=True).then_inc(dsum_s, 1)

            def products(n, d):
                t = slice(chunk_of(n, d) * P, (chunk_of(n, d) + 1) * P)
                if d == 0:
                    pe.wait_ge(dexp_s, pair(n, 1))
                    pe.wait_ge(silu_s, 12)
                else:
                    pe.wait_ge(at_s, pair(n, 0))
                for h in range(H):
                    mm(extra[:, 0, h * P:(h + 1) * P], k_t[:, h, t], k_t[:, h, t], start=True, stop=True)
                for h in range(H):
                    last = mm(extra[:, 1, h * P:(h + 1) * P], k_t[:, h, t], q_t[:, h, t], start=True, stop=True)
                last.then_inc(prod_s, 1)

            def level_v(n, l, d):
                if l == 0:
                    pe.wait_ge(at_s, pair(n, 1))
                else:
                    pe.wait_ge(xu_s, level(n, l - 1, d))
                for h in range(H):
                    rhs = ident if l == 0 else inv[:, d, h, :]
                    last = mm(extra[:, d, h * P:(h + 1) * P], a_t[:, d, h, :], rhs, start=True, stop=True)
                last.then_inc(v_s, 1)

            def level_x(n, l, d):
                pe.wait_ge(vm_s, upper(n, l, d))
                xt = inv_t[:, n % 2, d]
                for h in range(H):
                    if l < LEVELS - 1:
                        mm(extra[:, d, h * 64:(h + 1) * 64].rearrange("p (b s) -> p b s", s=1 << l),
                           xt[:, h, :], half1(v_buf[:, d, h, :], l, d), start=True, stop=True)
                    last = mm(extra[:, d, 256 + h * 64:256 + (h + 1) * 64].rearrange("p (b s) -> p b s", s=1 << l),
                              v_buf[:, d, h, :], half1(xt[:, h, :], l, 1 - d), start=True, stop=True)
                last.then_inc(xvx_s, 1)

            def scan_read(n, d):
                t = slice(chunk_of(n, d) * P, (chunk_of(n, d) + 1) * P)
                pe.wait_ge(st_s, pair(n - 1, 1))
                if d == 0:
                    pe.wait_ge(oadd_s, pair(n - 1, 1))
                else:
                    pe.wait_ge(oadd_s, pair(n, 0))
                    if n < NC - 1:
                        pe.wait_ge(st_s, pair(n, 0))
                    else:
                        pe.wait_ge(w_s, pair(n, 0))
                for h in range(H):
                    mm(extra[:, 2, h * P:(h + 1) * P], k_t[:, h, t], state[:, d, h, :], start=True, stop=True)
                for h in range(H):
                    last = mm(extra[:, 3, h * P:(h + 1) * P], q_t[:, h, t], state[:, d, h, :], start=True, stop=True)
                last.then_inc(sread_s, 1)

            def scan_solve(n, d):
                pe.wait_ge(xu_s, level(n, LEVELS - 1, d))
                if n > 0:
                    pe.wait_ge(r_s, pair(n - 1, d))
                elif d == 0:
                    pe.wait_ge(vcopy_s, 4)
                else:
                    pe.wait_ge(st_s, pair(0, 0))
                for h in range(H):
                    rhs = r_buf[:, d, h, :] if n > 0 else v_tok[:, chunk_of(n, d), h, :]
                    last = mm(extra[:, 2, h * P:(h + 1) * P], inv_t[:, n % 2, d, h, :], rhs, start=True, stop=True)
                last.then_inc(xr_s, 1)

            def scan_write(n, d):
                pe.wait_ge(w_s, pair(n, d))
                if n > 0:
                    pe.wait_ge(qs_s, pair(n - 1, d))
                elif d == 0:
                    pe.wait_ge(qsq_s, 1)
                else:
                    pe.wait_ge(oadd_s, pair(0, 0))
                for h in range(H):
                    last = mm(extra[:, 3, h * P:(h + 1) * P], decay[:, n % 2, d, h, :], w_buf[:, d, h, :],
                              start=True, stop=True)
                last.then_inc(in_s, 1)
                if n < NC - 1:
                    pe.wait_ge(wd_s, pair(n, d))
                    for h in range(H):
                        last = mm(extra[:, 2, h * P:(h + 1) * P], k_tok[:, chunk_of(n, d), h, :], w_dec[:, d, h, :],
                                  start=True, stop=True)
                    last.then_inc(ds_s, 1)

            pe.wait_ge(masks_in_s, 16)
            for k in range(KD):
                norm_sum(0, k, sq_in)
            norm_spread(0, diag0)
            n_src, y_src, f_src, hid_src = (act_hi, act_lo), (y_hi, y_lo), (f_hi, f_lo), (hid_hi, hid_lo)
            for s in range(S_FF):
                for j in range(UNITS):
                    if s == 0 and j < KD:
                        pe.wait_ge(nhi_s, j + 1)
                        pe.wait_ge(nlo_s, j + 1)
                    if s == S_WA and j < H:
                        pe.wait_ge(yh_s, j + 1)
                        pe.wait_ge(yl_s, j + 1)
                    if s == S_WD and j < H:
                        pe.wait_ge(yh_s, H + j + 1)
                        pe.wait_ge(yl_s, H + j + 1)
                    if s == S_WO and j < KD:
                        pe.wait_ge(nhi_s, KD + j + 1)
                        pe.wait_ge(nlo_s, KD + j + 1)
                    unit(s, j, y_src if tiles_of(s) == 4 else n_src)
                    if (s, j) == (0, UNITS - 1):
                        small_projection()
                    if s > S_WO and j in (4, 12):
                        if (s, j) == (S_WO + 1, 4):
                            pe.wait_ge(yd_s, H)
                        norm_sum(1, 2 * (s - S_WO - 1) + (j == 12), sq_t)
                    if 1 <= s <= 6 and j in (4, 12):
                        qkv_aux(2 * (s - 1) + (j == 12))
                    if (s, j) == (3, 8):
                        gate_sums()
                    n, t = window_of(s, j)
                    if n is not None and n < NC:
                        if t in DECAY_AT:
                            decay_sums(n, DECAY_AT[t])
                        if t in PRODUCTS_AT:
                            products(n, PRODUCTS_AT[t])
                        for what, l, d in LEVEL_AT.get(t, ()):
                            (level_v if what == "v" else level_x)(n, l, d)
                    if n is not None and n > 0 and t in SCAN_AT:
                        what, d = SCAN_AT[t]
                        if what == "read" and n > 1:
                            scan_read(n - 1, d)
                        if what == "solve":
                            scan_solve(n - 1, d)
                        if what == "write":
                            scan_write(n - 1, d)
                    if (s, j) == (22, 6):
                        pe.wait_ge(onorm_s, 1)
                        for h in range(H):
                            for c in range(NC):
                                last = nc.tensor.transpose(extra[:, h, c * P:(c + 1) * P], o_acc[:, c, h, :], ident)
                            last.then_inc(otr_s, 1)

            def ff_group(i, first):
                for b in range(FF_SLABS):
                    pe.wait_ge(hi_s, i * FF_SLABS + (S_FF + b + 1))
                    pe.wait_ge(lo_s, i * FF_SLABS + (S_FF + b + 1))
                    wh, wl = split_view(w_hi, b), split_view(w_lo, b)
                    ah, al = f_src if b < FF_SLABS // 2 else hid_src
                    for m in range(2):
                        u = 2 * b + m
                        pe.wait_ge(read_s[u % 4], i * 4 + (FF_T0 + u) // 4)
                        for k in range(KD):
                            if first and u == 0:
                                pe.wait_ge(nhi_s, 2 * KD + k + 1)
                                pe.wait_ge(nlo_s, 2 * KD + k + 1)
                            if u == FF_SLABS:
                                pe.wait_ge(hh_s, i * 8 + (k + 1))
                                pe.wait_ge(hl_s, i * 8 + (k + 1))
                            last = three(bank(u), wh[:, k, m * P:(m + 1) * P], wl[:, k, m * P:(m + 1) * P],
                                         ah[:, k, :], al[:, k, :], k == 0, k == KD - 1)
                        last.then_inc(tile_s, 1)
                        if first and u == 0:
                            norm_sum(1, KD - 2, sq_t)
                            norm_sum(1, KD - 1, sq_t)
                        if first and u == 1:
                            norm_spread(1, diag)

            ff_group(0, True)
            with pe.Fori(1, FF_GROUPS) as i:
                ff_group(i, False)

            for k in range(2):
                pe.wait_ge(ph_s, k + 1)
                pe.wait_ge(pl_s, k + 1)
            for j in range(UNITS):
                unit(S_PP, j, y_src)
                if j % 2 == 1:
                    if j == 1:
                        pe.wait_ge(rb_s, 2)
                    norm_sum(2, j // 2, sq_t)
            for s in range(S_PG, N_SLABS):
                for j in range(UNITS):
                    if s == S_PG and j < KD:
                        pe.wait_ge(nhi_s, 3 * KD + j + 1)
                        pe.wait_ge(nlo_s, 3 * KD + j + 1)
                    unit(s, j, n_src)
                    if (s, j) == (S_PG, 7):
                        norm_spread(2, diag)
                    if s > S_PG and j in (4, 12):
                        if (s, j) == (S_PG + 1, 4):
                            pe.wait_ge(rb_s, 3)
                        norm_sum(3, 2 * (s - S_PG - 1) + (j == 12), sq_t)
            norm_sum(3, KD - 2, sq_t)
            norm_sum(3, KD - 1, sq_t)
            norm_spread(3, diag)

        @block.scalar
        def _(act):
            A = nc.scalar.activation

            def split_hi(s, wait=None):
                act.wait_ge(raw_s[s % RING], 16 * (s // RING + 1))
                if s >= RING:
                    act.wait_ge(tile_s, first_tile(s - RING + 1))
                A(w_hi[:, s % RING, :], raw[:, s % RING, :], ACT.Copy).then_inc(hi_s, 1)

            def square(r, k, sq, src):
                i = r * KD + k
                if i >= SQ:
                    act.wait_ge(sqsum_s, i - SQ + 1)
                A(sq[:, i % SQ, :], src, ACT.Square).then_inc(sq_s, 1)

            def norm_root(r):
                act.wait_ge(ms_s, r + 1)
                A(norm_t[:, 1, 0:NC], norm_t[:, 0, 0:NC], ACT.Sqrt).then_inc(root_s, 1)

            def norm_copy(r, to):
                act.wait_ge(rbps_s, r + 1)
                A(to, extra[:, 0, :], ACT.Copy).then_inc(rb_s, 1)

            def qkv_tile(i):
                u = i
                act.wait_ge(tile_s, u + 1)
                A(conv_t[:, i % 2, :], bank(u), ACT.Copy, scale=conv_col(i, 1)).then_inc(tap_s, 1)
                wait_read(act, u)
                to = (k_t, v_t, q_t)[i // H][:, i % H, :]
                A(to, conv_t[:, i % 2, :], ACT.Silu).then_inc(silu_s, 1)
                if i // H != 1:
                    c = i if i < H else i - H
                    act.wait_ge(silu_s, i + 1)
                    if c > 1:
                        act.wait_ge(ss_s, c - 1)
                    A(sq_qk[:, c % 2, :], to, ACT.Square).then_inc(qksq_s, 1)

            def finish_tile(s, m):
                u = first_tile(s) + m
                if s < S_BXC:
                    qkv_tile(u)
                elif s < S_WA and (s - S_BXC) % 3 == 0:
                    act.wait_ge(tile_s, u + 1)
                    if s > S_BXC:
                        wait_read(act, first_tile(S_BXC + 1) + m)
                    A(b_sb[:, m, :], bank(u), ACT.Copy).then_inc(read_s[u % 4], 1)
                elif s < S_WA and (s - S_BXC) % 3 == 2:
                    i = 2 * ((s - S_BXC) // 3) + m
                    wait_read(act, u)
                    A(y_hi[:, i, :], ya[:, m, :], ACT.Copy).then_inc(yh_s, 1)
                elif S_WA <= s < S_GA:
                    act.wait_ge(tile_s, u + 1)
                    if s == S_WA and m == 0:
                        act.wait_ge(yl_s, H)
                    A(mixed[:, u - first_tile(S_WA), :], bank(u), ACT.Copy).then_inc(read_s[u % 4], 1)
                elif S_GA <= s < S_Z:
                    i = u - first_tile(S_GA)
                    act.wait_ge(tile_s, u + 1)
                    if i > 0:
                        act.wait_ge(sigau_s, i)
                    A(sig_a, bank(u), ACT.Sigmoid).then_inc(read_s[u % 4], 1)
                elif S_Z <= s < S_GD:
                    act.wait_ge(tile_s, u + 1)
                    if s == S_Z and m == 0:
                        act.wait_ge(xu_s, level(NC - 1, LEVELS - 1, 1))
                    A(z_silu[:, u - first_tile(S_Z), :], bank(u), ACT.Silu).then_inc(read_s[u % 4], 1)
                elif S_GD <= s < S_WD:
                    act.wait_ge(tile_s, u + 1)
                    if s == S_GD and m == 0:
                        act.wait_ge(sread_s, pair(NC - 2, 1))
                    A(sig_d[:, u - first_tile(S_GD), :], bank(u), ACT.Sigmoid).then_inc(read_s[u % 4], 1)
                elif S_WD <= s < S_WO:
                    i = u - first_tile(S_WD)
                    act.wait_ge(mg_s, i + 1)
                    act.wait_ge(tile_s, first_tile(S_WD))
                    A(act_hi[:, i, :], mg_f[:, i % 2, :], ACT.Copy).then_inc(nhi_s, 1)
                elif S_WO <= s < S_FF:
                    i = u - first_tile(S_WO)
                    wait_read(act, u)
                    A(f_hi[:, i, :], h_t[:, i, :], ACT.Copy, scale=cols[:, C_GFFN + i:C_GFFN + i + 1])\
                        .then_inc(nhi_s, 1)
                    square(1, i, sq_t, h_t[:, i, :])

            for k in range(KD):
                act.wait_ge(x_in_s[k // 2], 16)
                square(0, k, sq_in, x_in[:, k, :])
            split_hi(0)
            norm_root(0)
            act.wait_ge(cols_in_s, 16)
            A(w16_hi[:], cols[:, C_W16:C_W16 + KD * 16], ACT.Copy).then_inc(w16h_s, 1)
            norm_copy(0, rb0)
            for k in range(KD):
                act.wait_ge(nf_s, k + 1)
                A(act_hi[:, k, :], n_f[:, k % 4, :], ACT.Copy).then_inc(nhi_s, 1)

            for s in range(S_FF):
                for j in range(UNITS):
                    if j == 0:
                        split_hi(s + 1)
                    m = tile_ends(s, j)
                    if m is not None:
                        finish_tile(s, m)
                    if (s, j) == (1, 2):
                        act.wait_ge(bac_s, 1)
                        A(beta[:], ba[:, :, 0:8], ACT.Sigmoid).then_inc(beta_s, 1)
                        A(tiny[:, 5, 0:8], cols[:, C_ALOG:C_ALOG + 8], ACT.Exp).then_inc(aexp_s, 1)
                        act.wait_ge(abs_s, 1)
                        A(tiny[:, 1, :], tiny[:, 0, :], ACT.Exp, scale=-1.0).then_inc(exp_s, 1)
                    if 1 <= s <= 2 and j in (4, 12):
                        i = 2 * (s - 1) + (j == 12)
                        act.wait_ge(tr_s, i + 1)
                        A(k_tok[:, :, i, :], extra[:, 2 + i % 2, :].rearrange("p (c n) -> p c n", c=NC), ACT.Copy)\
                            .then_inc(kcopy_s, 1)
                    if (s, j) == (2, 13):
                        act.wait_ge(ksq_s, 1)
                        A(k_cols[:, 1, :], k_cols[:, 0, :], ACT.Sqrt).then_inc(kroot_s, 1)
                    if (s, j) == (3, 9):
                        act.wait_ge(gsum_s, 1)
                        A(e_cols[:].rearrange("p q d c h -> p (q d c h)"), extra[:, 1, 0:3 * DIRS * NC * H], ACT.Exp)\
                            .then_inc(ecol_s, 1)
                    n, t = window_of(s, j)
                    if n is not None and n < NC and t in DECAY_AT:
                        d = DECAY_AT[t]
                        act.wait_ge(dsum_s, pair(n, d))
                        if n >= 2:
                            act.wait_ge(in_s, pair(n - 2, d))
                        A(decay[:, n % 2, d].rearrange("p h n -> p (h n)"), extra[:, d, :], ACT.Exp)\
                            .then_inc(dexp_s, 1)
                    if n is not None and n > 0 and t in SCAN_AT and SCAN_AT[t][0] == "solve":
                        d = SCAN_AT[t][1]
                        act.wait_ge(xr_s, pair(n - 1, d))
                        if n > 1:
                            act.wait_ge(wd_s, pair(n - 2, d))
                            act.wait_ge(in_s, pair(n - 2, d))
                        for h in range(H):
                            last = A(w_buf[:, d, h, :], extra[:, 2, h * P:(h + 1) * P], ACT.Copy,
                                     scale=c1[:, chunk_of(n - 1, d), d, h:h + 1])
                        last.then_inc(w_s, 1)
                    if (s, j) == (20, 10):
                        act.wait_ge(oadd_s, pair(NC - 1, 1))
                        for c in range(NC):
                            for h in range(H):
                                if c + h:
                                    act.wait_ge(ac_s, c * H + h)
                                last = A(o_junk, o_acc[:, c, h, :], ACT.Square,
                                         accum_out=o_sq[:, c * H + h:c * H + h + 1])
                                last.then_inc(ac_s, 1)
                    if (s, j) == (21, 3):
                        act.wait_ge(omean_s, 1)
                        A(norm_t[:, 1, :], norm_t[:, 0, :], ACT.Sqrt).then_inc(oroot_s, 1)
                    if (s, j) == (22, 7):
                        for h in range(H):
                            act.wait_ge(yd_s, h + 1)
                            A(y_hi[:, h, :], yd_f[:, h % 2, :], ACT.Copy).then_inc(yh_s, 1)

            def ff_group(i, first):
                for b in range(FF_SLABS):
                    r = (b + 1) % RING
                    act.wait_ge(raw_s[r], i * (16 * FF_SLABS // RING) + 16 * ((S_FF + b + 1) // RING + 1))
                    act.wait_ge(tile_s, i * 16 + (FF_T0 + 2 * b))
                    A(w_hi[:, r, :], raw[:, r, :], ACT.Copy).then_inc(hi_s, 1)
                    if first and b == 0:
                        norm_root(1)
                        norm_copy(1, rb)
                    if first and b == 2:
                        act.wait_ge(p_in_s, 16)
                        for k in range(2):
                            A(y_hi[:, k, :], p_in[:, k, :], ACT.Copy).then_inc(ph_s, 1)
                    if b < FF_SLABS // 2:
                        for m in range(2):
                            u = 2 * b + m
                            act.wait_ge(read_s[u % 4], i * 4 + ((FF_T0 + u) // 4 + 1))
                            if not first:
                                act.wait_ge(tile_s, i * 16 + FF_T0)
                            A(hid_hi[:, 2 * b + m, :], relu_t[:, m, :], ACT.Square).then_inc(hh_s, 1)
                            if not first or b > 0:
                                act.wait_ge(hl_s, i * 8 + (2 * b + m - 1))
                            A(hid_f[:, m, :], relu_t[:, m, :], ACT.Square).then_inc(hf_s, 1)

            ff_group(0, True)
            with act.Fori(1, FF_GROUPS) as i:
                ff_group(i, False)

            for k in range(KD):
                wait_read(act, first_tile(S_PP) - KD + k)
                A(act_hi[:, k, :], h_t[:, k, :], ACT.Copy, scale=cols[:, C_GPLE + k:C_GPLE + k + 1])\
                    .then_inc(nhi_s, 1)
                square(2, k, sq_t, h_t[:, k, :])
                u = first_tile(S_PP) + k
                act.wait_ge(tile_s, u + 1)
                A(ple[:, k, :], bank(u), ACT.Copy).then_inc(read_s[u % 4], 1)
                if k == 0:
                    split_hi(S_PG)
            split_hi(S_PG + 1)
            norm_root(2)
            norm_copy(2, rb)
            for s in range(S_PG, N_SLABS):
                if S_PG < s < N_SLABS - 1:
                    split_hi(s + 1)
                for m in range(2):
                    i = 2 * (s - S_PG) + m
                    wait_read(act, first_tile(s) + m)
                    A(sig_p[:, m, :], sig_p[:, m, :], ACT.Sigmoid).then_inc(gp_s, 1)
                    act.wait_ge(hp_s, i + 1)
                    square(3, i, sq_t, h_t[:, i, :])
            norm_root(3)
            norm_copy(3, rb)

        @block.vector
        def _(dve):
            V = nc.vector
            steps = [0]

            def link(ins):
                steps[0] += 1
                ins.then_inc(dv_s, 1)
                dve.wait_ge(dv_s, steps[0])

            def split_lo(s):
                dve.wait_ge(hi_s, s + 1)
                V.tensor_tensor(w_lo[:, s % RING, :], raw[:, s % RING, :], w_hi[:, s % RING, :].bitcast(F32),
                                ALU.subtract).then_inc(lo_s, 1)

            def rsqrt_steps(x, root, rec, t, to):
                link(V.reciprocal(rec, root))
                link(V.tensor_tensor(t, rec, rec, ALU.mult))
                link(V.tensor_tensor(t, t, x, ALU.mult))
                link(V.tensor_scalar(t, t, -0.5, 1.5, ALU.mult, ALU.add))
                link(V.tensor_tensor(to, rec, t, ALU.mult))

            def norm_mean(r):
                dve.wait_ge(sqsum_s, (r + 1) * KD)
                V.tensor_scalar(norm_t[:, 0, 0:NC], extra[:, :, 0:1].rearrange("p c o -> p (c o)"), 1.0 / D, EPS, ALU.mult, ALU.add)\
                    .then_inc(ms_s, 1)

            def norm_diag(r, dg):
                dve.wait_ge(root_s, r + 1)
                x, root, rec, t, to = (norm_t[:, i, 0:NC] for i in range(5))
                rsqrt_steps(x, root, rec, t, to)
                for c in range(NC):
                    last = V.tensor_scalar(dg[:, c * P:(c + 1) * P], ident, norm_t[:, 4, c:c + 1], None, ALU.mult)
                last.then_inc(diag_s, 1)

            def qkv_tile(i):
                dve.wait_ge(tap_s, i + 1)
                c = conv_t[:, i % 2, :]
                link(V.scalar_tensor_tensor(c[:, 1:TOK], bank(i)[:, 0:TOK - 1], conv_col(i, 0), c[:, 1:TOK],
                                            ALU.mult, ALU.add))
                V.scalar_tensor_tensor(c[:, 0:TOK - 1], bank(i)[:, 1:TOK], conv_col(i, 2), c[:, 0:TOK - 1],
                                       ALU.mult, ALU.add).then_inc(read_s[i % 4], 1)

            def finish_tile(s, m):
                u = first_tile(s) + m
                if s < S_BXC:
                    qkv_tile(u)
                elif s < S_WA:
                    g, what = divmod(s - S_BXC, 3)
                    i = 2 * g + m
                    if what == 1:
                        dve.wait_ge(tile_s, u + 1)
                        wait_read(dve, first_tile(s - 1) + m)
                        V.tensor_tensor(bx[:, m, :], b_sb[:, m, :], bank(u), ALU.mult).then_inc(read_s[u % 4], 1)
                        wait_read(dve, u)
                        if g:
                            dve.wait_ge(yh_s, m + 1)
                            dve.wait_ge(yl_s, m + 1)
                        taps = [cols[:, C_CONVA + 4 * q + i:C_CONVA + 4 * q + i + 1] for q in range(3)]
                        y = ya[:, m, :]
                        link(V.tensor_scalar(y, bx[:, m, :], taps[1], None, ALU.mult))
                        link(V.scalar_tensor_tensor(y[:, 1:TOK], bx[:, m, 0:TOK - 1], taps[0], y[:, 1:TOK],
                                                    ALU.mult, ALU.add))
                        link(V.scalar_tensor_tensor(y[:, 0:TOK - 1], bx[:, m, 1:TOK], taps[2], y[:, 0:TOK - 1],
                                                    ALU.mult, ALU.add))
                    if what == 2:
                        dve.wait_ge(tile_s, u + 1)
                        V.tensor_tensor(ya[:, m, :], ya[:, m, :], bank(u), ALU.mult).then_inc(read_s[u % 4], 1)
                        dve.wait_ge(yh_s, i + 1)
                        V.tensor_tensor(y_lo[:, i, :], ya[:, m, :], y_hi[:, i, :].bitcast(F32), ALU.subtract)\
                            .then_inc(yl_s, 1)
                elif S_GA <= s < S_Z:
                    i = u - first_tile(S_GA)
                    wait_read(dve, u)
                    wait_read(dve, first_tile(S_WA) + i)
                    V.tensor_tensor(mixed[:, i, :], mixed[:, i, :], sig_a, ALU.mult).then_inc(sigau_s, 1)
                elif S_WD <= s < S_WO:
                    i = u - first_tile(S_WD)
                    dve.wait_ge(tile_s, u + 1)
                    if i >= 2:
                        dve.wait_ge(nhi_s, KD + i - 1)
                        dve.wait_ge(nlo_s, KD + i - 1)
                    if i == 0:
                        for q in range(4):
                            wait_read(dve, first_tile(S_WD) - 1 - q)
                    V.tensor_tensor(mg_f[:, i % 2, :], bank(u), sig_d[:, i, :], ALU.mult).then_inc(read_s[u % 4], 1)
                    wait_read(dve, u)
                    V.tensor_tensor(mg_f[:, i % 2, :], mg_f[:, i % 2, :], mixed[:, i, :], ALU.add).then_inc(mg_s, 1)
                    dve.wait_ge(nhi_s, KD + i + 1)
                    V.tensor_tensor(act_lo[:, i, :], mg_f[:, i % 2, :], act_hi[:, i, :].bitcast(F32), ALU.subtract)\
                        .then_inc(nlo_s, 1)
                elif S_WO <= s < S_FF:
                    i = u - first_tile(S_WO)
                    dve.wait_ge(tile_s, u + 1)
                    dve.wait_ge(x2_in_s, 16)
                    V.tensor_tensor(h_t[:, i, :], h_t[:, i, :], bank(u), ALU.add).then_inc(read_s[u % 4], 1)
                    dve.wait_ge(nhi_s, 2 * KD + i + 1)
                    V.scalar_tensor_tensor(f_lo[:, i, :], h_t[:, i, :], cols[:, C_GFFN + i:C_GFFN + i + 1],
                                           f_hi[:, i, :].bitcast(F32), ALU.mult, ALU.subtract).then_inc(nlo_s, 1)

            def spread(col):
                return col.unsqueeze(2).broadcast_to([P, col.shape[1], P])

            def heads_of(flat):
                return flat.rearrange("p (h n) -> p h n", h=H)

            def norm_lo(k):
                dve.wait_ge(nhi_s, k + 1)
                V.tensor_tensor(act_lo[:, k, :], n_f[:, k % 4, :], act_hi[:, k, :].bitcast(F32), ALU.subtract)\
                    .then_inc(nlo_s, 1)

            def log_decays():
                dve.wait_ge(ba_s, 1)
                V.tensor_copy(ba[:].rearrange("p c n -> p (c n)"), extra[:, 0, 0:NC * 16]).then_inc(bac_s, 1)
                dve.wait_ge(bac_s, 1)
                x, e, r, t, y, q = (tiny[:, i, :] for i in range(6))
                al = gate[:].rearrange("p c n -> p (c n)")
                dt = cols[:, C_DTB:C_DTB + 8].unsqueeze(1).broadcast_to([P, NC, 8])
                link(V.tensor_tensor(gate[:], ba[:, :, 8:16], dt, ALU.add))
                V.scalar_tensor_tensor(x, al, -1.0, al, ALU.mult, ALU.max).then_inc(abs_s, 1)
                dve.wait_ge(exp_s, 1)
                link(V.tensor_scalar(r, e, 2.0, None, ALU.add))
                link(V.reciprocal(t, r))
                link(V.tensor_tensor(t, t, e, ALU.mult))
                link(V.tensor_tensor(y, t, t, ALU.mult))
                link(V.tensor_scalar(r, y, 1.0 / 17, None, ALU.mult))
                for odd in (15, 13, 11, 9, 7, 5, 3):
                    link(V.scalar_tensor_tensor(r, r, 1.0 / odd, y, ALU.add, ALU.mult))
                link(V.scalar_tensor_tensor(r, r, 1.0, t, ALU.add, ALU.mult))
                link(V.tensor_scalar(al, al, 0.0, None, ALU.max))
                link(V.scalar_tensor_tensor(al, r, 2.0, al, ALU.mult, ALU.add))
                dve.wait_ge(aexp_s, 1)
                ea = tiny[:, 5, 0:8].unsqueeze(1).broadcast_to([P, NC, 8])
                V.scalar_tensor_tensor(gate[:], gate[:], -1.0, ea, ALU.mult, ALU.mult).then_inc(g_s, 1)
                dve.wait_ge(g_s, 1)

            def key_columns():
                dve.wait_ge(ss_s, H)
                sq, root, rec, length, inv_sq = (k_cols[:, i, :] for i in range(5))
                V.tensor_scalar(sq, extra[:, 0, 0:NC * H], EPS, None, ALU.add).then_inc(ksq_s, 1)
                dve.wait_ge(ksq_s, 1)
                link(V.reciprocal(inv_sq, sq))
                dve.wait_ge(kroot_s, 1)
                link(V.reciprocal(rec, root))
                link(V.tensor_tensor(rec, rec, sq, ALU.mult))
                link(V.tensor_tensor(rec, rec, root, ALU.add))
                link(V.tensor_scalar(length, rec, 0.5, None, ALU.mult))
                dve.wait_ge(beta_s, 1)
                for d in range(DIRS):
                    link(V.tensor_tensor(c1[:, :, d, :], beta[:, :, d * H:(d + 1) * H],
                                         inv_sq.rearrange("p (c h) -> p c h", c=NC), ALU.mult))

            def decay_rhs(n, d):
                if n > 0:
                    dve.wait_ge(xvx_s, upper(n - 1, LEVELS - 1, d))
                for h in range(H):
                    last = V.tensor_scalar(v_buf[:, d, h, :], incl[d], gate[:, chunk_of(n, d), d * H + h:d * H + h + 1],
                                           None, ALU.mult)
                last.then_inc(gm_s, 1)

            def make_a(n, d):
                dve.wait_ge(prod_s, pair(n, d))
                dve.wait_ge(dmask_s, pair(n, d))
                for h in range(H):
                    last = V.scalar_tensor_tensor(a_t[:, d, h, :], extra[:, 0, h * P:(h + 1) * P],
                                                  c1[:, chunk_of(n, d), d, h:h + 1], decay[:, n % 2, d, h, :],
                                                  ALU.mult, ALU.mult)
                link(last)
                V.tensor_tensor(decay[:, n % 2, d], decay[:, n % 2, d], heads_of(extra[:, 1, :]), ALU.mult)\
                    .then_inc(at_s, 1)

            def first_level(n, d):
                dve.wait_ge(v_s, level(n, 0, d))
                link(V.tensor_tensor(v_buf[:, d], heads_of(extra[:, d, :]), over_heads(lmask[:, d * LEVELS, :]),
                                     ALU.mult))
                if n >= 2:
                    dve.wait_ge(xr_s, pair(n - 2, d))
                link(V.tensor_tensor(inv_t[:, n % 2, d], a_t[:, d], over_heads(lmask[:, (1 - d) * LEVELS, :]),
                                     ALU.mult))
                link(V.tensor_tensor(inv[:, d], over_heads(ident), v_buf[:, d], ALU.subtract))
                V.tensor_tensor(inv_t[:, n % 2, d], over_heads(ident), inv_t[:, n % 2, d], ALU.subtract)\
                    .then_inc(xu_s, 1)

            def update_inverse(n, l, d):
                dve.wait_ge(xvx_s, upper(n, l, d))
                if l < LEVELS - 1:
                    x = half(inv[:, d], l, d)
                    V.tensor_tensor(x, x, extra[:, d, 0:256].rearrange("p (h b s) -> p h b s", h=H, s=1 << l),
                                    ALU.subtract)
                x = half(inv_t[:, n % 2, d], l, 1 - d)
                V.tensor_tensor(x, x, extra[:, d, 256:512].rearrange("p (h b s) -> p h b s", h=H, s=1 << l),
                                ALU.subtract).then_inc(xu_s, 1)

            def scan_read(n, d):
                dve.wait_ge(sread_s, pair(n - 1, d))
                c = chunk_of(n, d)
                for h in range(H):
                    last = V.scalar_tensor_tensor(r_buf[:, d, h, :], extra[:, 2, h * P:(h + 1) * P],
                                                  neg_run[:, d, c, h:h + 1], v_tok[:, c, h, :], ALU.mult, ALU.add)
                last.then_inc(r_s, 1)
                for h in range(H):
                    run = e_cols[:, 0, d, c, h:h + 1]
                    if n < NC // 2:
                        last = V.tensor_scalar(o_acc[:, c, h, :], extra[:, 3, h * P:(h + 1) * P], run, None, ALU.mult)
                    else:
                        last = V.scalar_tensor_tensor(o_acc[:, c, h, :], extra[:, 3, h * P:(h + 1) * P], run,
                                                      o_acc[:, c, h, :], ALU.mult, ALU.add)
                last.then_inc(qs_s, 1)

            def scan_decay(n, d):
                dve.wait_ge(w_s, pair(n, d))
                if n > 0:
                    dve.wait_ge(ds_s, pair(n - 1, d))
                for h in range(H):
                    last = V.tensor_scalar(w_dec[:, d, h, :], w_buf[:, d, h, :],
                                           e_cols[:, 1, d, chunk_of(n, d), h:h + 1], None, ALU.mult)
                last.then_inc(wd_s, 1)

            def scan_write(n, d):
                c = chunk_of(n, d)
                dve.wait_ge(in_s, pair(n, d))
                if n == 0:
                    V.tensor_copy(o_acc[:, c], heads_of(extra[:, 3, :])).then_inc(oadd_s, 1)
                else:
                    dve.wait_ge(qs_s, pair(n - 1, d))
                    V.tensor_tensor(o_acc[:, c], o_acc[:, c], heads_of(extra[:, 3, :]), ALU.add).then_inc(oadd_s, 1)
                if n < NC - 1:
                    dve.wait_ge(ds_s, pair(n, d))
                    if n == 0:
                        V.tensor_copy(state[:, d], heads_of(extra[:, 2, :])).then_inc(st_s, 1)
                    else:
                        for h in range(H):
                            last = V.scalar_tensor_tensor(state[:, d, h, :], state[:, d, h, :],
                                                          e_cols[:, 2, d, c, h:h + 1], extra[:, 2, h * P:(h + 1) * P],
                                                          ALU.mult, ALU.add)
                        last.then_inc(st_s, 1)

            def output_norm():
                dve.wait_ge(ac_s, NC * H)
                dve.wait_ge(qsq_s, 1)
                link(V.tensor_scalar(norm_t[:, 5, :], q_sq[:], EPS, EPS * P, ALU.add, ALU.mult))
                V.scalar_tensor_tensor(norm_t[:, 0, :], o_sq[:], 1.0 / P, norm_t[:, 5, :], ALU.mult, ALU.add)\
                    .then_inc(omean_s, 1)
                dve.wait_ge(oroot_s, 1)
                x, root, rec, t, to = (norm_t[:, i, :] for i in range(5))
                rsqrt_steps(x, root, rec, t, to)
                flat = o_acc.rearrange("p c h n -> p (c h) n")
                V.tensor_tensor(flat, flat, spread(norm_t[:, 4, :]), ALU.mult).then_inc(onorm_s, 1)

            norm_mean(0)
            dve.wait_ge(masks_in_s, 16)
            norm_diag(0, diag0)
            dve.wait_ge(rb_s, 1)
            dve.wait_ge(cols_in_s, 16)
            for k in range(KD):
                if k >= 4:
                    dve.wait_ge(nhi_s, k - 3)
                V.scalar_tensor_tensor(n_f[:, k % 4, :], x_in[:, k, :], cols[:, C_GMIX + k:C_GMIX + k + 1], rb0,
                                       ALU.mult, ALU.mult).then_inc(nf_s, 1)
                if k == 0:
                    split_lo(0)
                if k > 0:
                    norm_lo(k - 1)
            norm_lo(KD - 1)
            dve.wait_ge(w16h_s, 1)
            V.tensor_tensor(w16_lo[:], cols[:, C_W16:C_W16 + KD * 16], w16_hi[:].bitcast(F32), ALU.subtract)\
                .then_inc(w16l_s, 1)

            for s in range(S_FF):
                for j in range(UNITS):
                    if j == 0:
                        split_lo(s + 1)
                    m = tile_ends(s, j)
                    if m is not None:
                        finish_tile(s, m)
                    if (s, j) == (1, 1):
                        log_decays()
                    if (s, j) == (2, 13):
                        key_columns()
                    if (s, j) == (3, 9):
                        dve.wait_ge(ecol_s, 1)
                        link(V.tensor_scalar(neg_run[:], e_cols[:, 0], -1.0, None, ALU.mult))
                    if 3 <= s <= 4 and j in (4, 12):
                        i = 2 * (s - 1) + (j == 12)
                        dve.wait_ge(tr_s, i + 1)
                        V.tensor_tensor(v_tok[:, :, i - H, :], extra[:, 2 + i % 2, :].rearrange("p (c n) -> p c n", c=NC),
                                        spread(k_cols[:, 3, :].rearrange("p (c h) -> p c h", c=NC)[:, :, i - H]),
                                        ALU.mult).then_inc(vcopy_s, 1)
                    if (s, j) == (6, 13):
                        dve.wait_ge(ss_s, 2 * H)
                        V.tensor_copy(q_sq[:], extra[:, 3, 0:NC * H]).then_inc(qsq_s, 1)
                    n, t = window_of(s, j)
                    if n is not None and n < NC:
                        if t == 0:
                            decay_rhs(n, 0)
                            decay_rhs(n, 1)
                        if t in PRODUCTS_AT:
                            make_a(n, PRODUCTS_AT[t])
                        for what, l, d in LEVEL_AT.get(t, ()):
                            if what == "v" and l == 0:
                                first_level(n, d)
                            elif what == "v":
                                dve.wait_ge(v_s, level(n, l, d))
                                V.tensor_tensor(v_buf[:, d], heads_of(extra[:, d, :]),
                                                over_heads(lmask[:, d * LEVELS + l, :]), ALU.mult).then_inc(vm_s, 1)
                            else:
                                update_inverse(n, l, d)
                    if n is not None and n > 0 and t in SCAN_AT:
                        what, d = SCAN_AT[t]
                        if what == "read" and n > 1:
                            scan_read(n - 1, d)
                        if what == "solve" and n < NC:
                            scan_decay(n - 1, d)
                        if what == "write":
                            scan_write(n - 1, d)
                    if (s, j) == (21, 2):
                        output_norm()
                    if (s, j) == (22, 7):
                        for h in range(H):
                            dve.wait_ge(otr_s, h + 1)
                            wait_read(dve, first_tile(S_Z) + h)
                            if h >= 2:
                                dve.wait_ge(yh_s, H + h - 1)
                                dve.wait_ge(yl_s, H + h - 1)
                            V.scalar_tensor_tensor(yd_f[:, h % 2, :], extra[:, h, :], cols[:, C_GDN:C_GDN + 1],
                                                   z_silu[:, h, :], ALU.mult, ALU.mult).then_inc(yd_s, 1)
                            dve.wait_ge(yh_s, H + h + 1)
                            V.tensor_tensor(y_lo[:, h, :], yd_f[:, h % 2, :], y_hi[:, h, :].bitcast(F32), ALU.subtract)\
                                .then_inc(yl_s, 1)

            def ff_group(i, first):
                for b in range(FF_SLABS):
                    r = (b + 1) % RING
                    dve.wait_ge(hi_s, i * FF_SLABS + (S_FF + b + 2))
                    V.tensor_tensor(w_lo[:, r, :], raw[:, r, :], w_hi[:, r, :].bitcast(F32), ALU.subtract)\
                        .then_inc(lo_s, 1)
                    if first and b == 0:
                        norm_mean(1)
                        norm_diag(1, diag)
                        dve.wait_ge(rb_s, 2)
                    if first and b == 2:
                        for k in range(2):
                            dve.wait_ge(ph_s, k + 1)
                            V.tensor_tensor(y_lo[:, k, :], p_in[:, k, :], y_hi[:, k, :].bitcast(F32), ALU.subtract)\
                                .then_inc(pl_s, 1)
                    for m in range(2):
                        u = 2 * b + m
                        dve.wait_ge(tile_s, i * 16 + (FF_T0 + u + 1))
                        if b < FF_SLABS // 2:
                            if not first or b > 0:
                                dve.wait_ge(hf_s, i * 8 + (u - 1))
                            V.scalar_tensor_tensor(relu_t[:, m, :], bank(u), 0.0, rb, ALU.max, ALU.mult)\
                                .then_inc(read_s[u % 4], 1)
                            dve.wait_ge(hf_s, i * 8 + (u + 1))
                            V.tensor_tensor(hid_lo[:, u, :], hid_f[:, m, :], hid_hi[:, u, :].bitcast(F32), ALU.subtract)\
                                .then_inc(hl_s, 1)
                        else:
                            V.tensor_tensor(h_t[:, u - 8, :], h_t[:, u - 8, :], bank(u), ALU.add)\
                                .then_inc(read_s[u % 4], 1)

            ff_group(0, True)
            with dve.Fori(1, FF_GROUPS) as i:
                ff_group(i, False)

            for k in range(KD):
                dve.wait_ge(nhi_s, 3 * KD + k + 1)
                V.scalar_tensor_tensor(act_lo[:, k, :], h_t[:, k, :], cols[:, C_GPLE + k:C_GPLE + k + 1],
                                       act_hi[:, k, :].bitcast(F32), ALU.mult, ALU.subtract).then_inc(nlo_s, 1)
                if k == 0:
                    split_lo(S_PG)
            split_lo(S_PG + 1)
            norm_mean(2)
            norm_diag(2, diag)
            dve.wait_ge(rb_s, 3)
            for s in range(S_PG, N_SLABS):
                if S_PG < s < N_SLABS - 1:
                    split_lo(s + 1)
                for m in range(2):
                    i = 2 * (s - S_PG) + m
                    u = first_tile(s) + m
                    dve.wait_ge(tile_s, u + 1)
                    V.tensor_tensor(sig_p[:, m, :], bank(u), rb, ALU.mult).then_inc(read_s[u % 4], 1)
                    dve.wait_ge(gp_s, i + 1)
                    wait_read(dve, first_tile(S_PP) + i)
                    link(V.tensor_tensor(sig_p[:, m, :], sig_p[:, m, :], ple[:, i, :], ALU.mult))
                    V.tensor_tensor(h_t[:, i, :], h_t[:, i, :], sig_p[:, m, :], ALU.add).then_inc(hp_s, 1)
            norm_mean(3)
            norm_diag(3, diag)
            dve.wait_ge(rb_s, 4)
            for k in range(KD):
                V.scalar_tensor_tensor(h_t[:, k, :], h_t[:, k, :], cols[:, C_GFIN + k:C_GFIN + k + 1], rb,
                                       ALU.mult, ALU.mult).then_inc(fin_s, 1)

        @block.gpsimd
        def _(pool):
            for n in range(NC):
                for d in range(DIRS):
                    pool.wait_ge(dexp_s, pair(n, d))
                    m = decay[:, n % 2, d]
                    sign = 1 - 2 * d
                    nc.gpsimd.affine_select(out=m, in_=m, compare_op=ALU.is_ge, fill=0.0, base=0,
                                            pattern=[[0, H], [sign, P]], channel_multiplier=-sign).then_inc(dmask_s, 1)


def _slabs(w, nk, width):
    rows, n = w.shape
    return w.reshape(nk, P, n // width, width).transpose(2, 1, 0, 3).reshape(n // width, P, nk * width)


def _features(a):
    return np.ascontiguousarray(a.T.reshape(-1, P, TOK).transpose(1, 0, 2))


def _masks():
    i = np.arange(P)
    row, col = i[:, None], i[None, :]
    m = np.stack([row == col, row <= col, row >= col, row > col, row < col, row >= 0 * col], axis=1)
    levels = []
    for d in range(DIRS):
        for l in range(LEVELS):
            same = row >> (l + 1) == col >> (l + 1)
            later, earlier = (row, col) if d == 0 else (col, row)
            levels.append(same & ((later >> l) % 2 == 1) & ((earlier >> l) % 2 == 0))
    return m.astype(np.float32), np.stack(levels, axis=1)


def kernel(**inputs):
    import ml_dtypes
    import concourse.bacc as bacc
    from concourse.bass_utils import run_bass_kernel_spmd

    a = {n: np.asarray(v) for n, v in inputs.items()}
    w_in = a["w_in"][0]
    b_at, c_at, x_at, q_at, k_at, v_at, z_at = (512 * i for i in range(7))
    ga_at = z_at + 512 + 16
    gd_at = ga_at + D

    def part(at, n):
        return _slabs(w_in[:, at:at + n], KD, 256)

    bxc = [part(at + 256 * g, 256) for g in range(2) for at in (b_at, x_at, c_at)]
    ff = []
    w1, w2 = a["w_ff1"][0], a["w_ff2"][0]
    for g in range(FF_GROUPS):
        ff += [_slabs(w1[:, D * g:D * (g + 1)], KD, 256), _slabs(w2[D * g:D * (g + 1)], KD, 256)]
    stream = np.concatenate(
        [part(k_at, 512), part(v_at, 512), part(q_at, 512), *bxc,
         _slabs(a["w_a_out"][0], H, 512), part(ga_at, D), part(z_at, 512), part(gd_at, D),
         _slabs(a["w_dn_out"][0], H, 512), _slabs(a["w_o"][0], KD, 256), *ff,
         _slabs(a["w_ple_proj"][0], 2, 1024), _slabs(a["w_ple_gate"][0], KD, 256)])
    assert stream.shape == (N_SLABS, P, SLAB)

    cols = np.zeros((P, N_COLS), np.float32)

    def put(at, m):
        cols[:, at:at + m.shape[1]] = m

    put(C_GMIX, a["g_mix"][0].reshape(KD, P).T)
    put(C_GFFN, a["g_ffn"][0].reshape(KD, P).T)
    put(C_GPLE, a["g_ple"][0].reshape(KD, P).T)
    put(C_GFIN, a["g_final"].reshape(KD, P).T)
    put(C_CONVA, a["conv_a"][0].reshape(3 * H, P).T)
    put(C_CONVQ, a["conv_qkv"][0].reshape(3 * 3 * H, P).T)
    put(C_GDN, a["g_dn_norm"][0].reshape(1, P).T)
    for at, f, b in ((C_ALOG, "a_log_f", "a_log_b"), (C_DTB, "dt_bias_f", "dt_bias_b")):
        put(at, np.broadcast_to(a[f], (P, H)))
        put(at + H, np.broadcast_to(a[b], (P, H)))
    put(C_W16, w_in[:, z_at + 512:ga_at].reshape(KD, P, 16).transpose(1, 0, 2).reshape(P, KD * 16))
    masks, levels = _masks()

    arrays = {"x_in_dram": _features(a["x"][0]), "p_in_dram": _features(a["p"][0, 0]), "stream": stream,
              "cols_in": cols, "masks_in": masks, "levels_in": levels.astype(ml_dtypes.bfloat16)}
    nc = bacc.Bacc("TRN2", target_bir_lowering=False, num_devices=1)
    args = [nc.dram_tensor(n, v.shape, mybir.dt.from_np(v.dtype), kind="ExternalInput").ap()
            for n, v in arrays.items()]
    args.append(nc.dram_tensor("out_t", (P, KD, TOK), F32, kind="ExternalOutput").ap())
    encoder_block(nc, *args)
    got = run_bass_kernel_spmd(nc, [arrays], core_ids=[0]).results[0]["out_t"]
    return np.asarray(got).transpose(2, 1, 0).reshape(1, TOK, D)
```

```python
from contextlib import ExitStack

import numpy as np

import concourse.bass as bass
from concourse import mybir

ALU = mybir.AluOpType
ACT = mybir.ActivationFunctionType
F32 = mybir.dt.float32
F32R = mybir.dt.float32r
BF16 = mybir.dt.bfloat16

P = 128
TOK = 512
D = 1024
KD = D // P
H = 4
NC = TOK // P
LEVELS = 7
D_FF = 4 * D
EPS = 1e-6
DIRS = 2

SLAB = 2048
UNITS = 16
S_K, S_Q, S_V = 0, 2, 4
S_BXC = 6
S_WA = 12
S_GA = 14
S_Z = 18
S_GD = 20
S_WD = 24
S_WO = 26
S_FF = 30
FF_GROUPS = 4
FF_SLABS = 8
S_PP = S_FF + FF_GROUPS * FF_SLABS
S_PG = S_PP + 1
N_SLABS = S_PG + 4
RING = 2
HI_PARTS, LO_PARTS = 2, 4
SQ = 3

C_GMIX, C_GFFN, C_GPLE, C_GFIN = 0, 8, 16, 24
C_CONVA = 32
C_CONVQ = C_CONVA + 12
C_GDN = C_CONVQ + 36
C_ALOG = C_GDN + 1
C_DTB = C_ALOG + 8
C_PARITY = C_DTB + 8
C_W16 = C_PARITY + 2 * LEVELS
N_COLS = C_W16 + KD * 16


def tiles_of(s):
    if s in (S_WA, S_WA + 1, S_WD, S_WD + 1):
        return 4
    return 8 if s == S_PP else 2


def first_tile(s):
    return sum(tiles_of(r) for r in range(s))


ORDER = [c for n in range(NC // 2) for c in (n, NC - 1 - n)]
DELTA = {}


def _put(unit, *what):
    DELTA.setdefault(unit, []).append(what)


INV0, INV_UNITS = 4 * UNITS + 4, 48
for _i in range(NC):
    _b = INV0 + _i * INV_UNITS
    _put(_b - 3, "gates", _i)
    _put(_b, "decay", _i)
    _put(_b + 1, "kk", _i)
    _put(_b + 4, "make_k", _i)
    _put(_b + 4, "qk", _i)
    _put(_b + 6, "make_p", _i)
    _put(_b + 8, "turn", _i, 0)
    for _l in range(1, LEVELS):
        _v = _b + 6 + 6 * _l
        _put(_v, "ax", _i, _l)
        _put(_v + 2, "xax", _i, _l)
        _put(_v + 4, "turn", _i, _l)
_b = INV0 + 2 * INV_UNITS + 2
for _at, _what, _d in ((-1, "tri", 0), (0, "solve", 0), (5, "write", 0), (6, "tri", 1), (9, "solve", 1), (14, "write", 1)):
    _put(_b + _at, _what, 0, _d)
for _n in range(1, NC):
    _b = INV0 + NC * INV_UNITS + 1 + 13 * (_n - 1)
    for _at, _what, _d in ((0, "tri", 0), (0, "read", 0), (1, "tri", 1), (1, "read", 1), (3, "solve", 0), (5, "solve", 1),
                           (7, "write", 0), (9, "write", 1)):
        _put(_b + _at, _what, _n, _d)


def chunk_of(n, d):
    return n if d == 0 else NC - 1 - n


def pair(n, d):
    return DIRS * n + d + 1


def level(i, l):
    return i * LEVELS + l + 1


def upper(i, l):
    return i * (LEVELS - 1) + l


def encoder_block(nc, x_t, p_t, stream, cols_in, masks_in, levels_in, out):
    with ExitStack() as ctx:
        def sb(name, shape, dt=F32):
            return ctx.enter_context(nc.sbuf_tensor(name, shape, dt))

        def sem(name):
            return ctx.enter_context(nc.semaphore(name))

        raw = sb("raw", [P, RING, SLAB])
        w_hi = sb("w_hi", [P, RING, SLAB], F32R)
        w_lo = sb("w_lo", [P, RING, SLAB], F32R)
        act_hi = sb("act_hi", [P, KD, TOK], F32R)
        act_lo = sb("act_lo", [P, KD, TOK], F32R)
        cols = sb("cols", [P, N_COLS])
        masks = sb("masks", [P, 6, P])
        lmask = sb("lmask", [P, 2 * LEVELS - 1, P], BF16)
        beta = sb("beta", [P, NC, DIRS * H])
        gate = sb("gate", [P, NC, DIRS * H])
        e_cols = sb("e_cols", [P, 3, DIRS, NC, H])
        neg_run = sb("neg_run", [P, DIRS, NC, H])
        c1 = sb("c1", [P, NC, DIRS, H])
        c1_end = sb("c1_end", [P, NC, DIRS, H])
        c_lvl = sb("c_lvl", [P, LEVELS, NC * H])
        k_cols = sb("k_cols", [P, 5, NC * H])
        q_sq = sb("q_sq", [P, NC * H])
        o_sq = sb("o_sq", [P, NC * H])
        norm_t = sb("norm_t", [P, 6, NC * H])

        KB = 256
        arena_stack = ExitStack()
        arena = arena_stack.enter_context(nc.sbuf_tensor("arena", [P, 118 * KB], F32))

        def carve(start_kb, *shape):
            flat = arena[:, start_kb * KB:start_kb * KB + int(np.prod(shape))]
            names = " ".join(f"a{i}" for i in range(len(shape)))
            sizes = {f"a{i}": shape[i] for i in range(1, len(shape))}
            return flat.rearrange(f"p ({names}) -> p {names}", **sizes) if len(shape) > 1 else flat

        x_in = carve(0, KD, TOK)
        n_f = carve(16, 4, TOK)
        sq_in = carve(24, SQ, TOK)
        acc0 = carve(30, TOK)
        rb0 = carve(34, TOK)
        norm0 = carve(36, 3, TOK)
        tiny = carve(65, 6, NC * DIRS * H)
        ba = carve(66, NC, 16)
        ba_t = carve(68, TOK)
        k_t = carve(0, H, TOK)
        q_t = carve(8, H, TOK)
        k_tok = carve(16, NC, H, P)
        v_tok = carve(24, NC, H, P)
        inv_t = carve(32, NC, H, P)
        qk = carve(40, NC, H, P)
        sq_qk = carve(44, 2, TOK)
        a_t = carve(48, H, P)
        z_t = carve(50, H, P)
        decay = carve(50, H, P)
        inv = carve(52, H, P)
        y = carve(54, H, P)
        ax = carve(56, H, P)
        gate_b = carve(56, H, P)
        gate_f = carve(58, H, P)
        tri_x = (carve(60, H, P), carve(48, H, P))
        tri_qk = (carve(62, H, P), carve(50, H, P))
        r_buf = carve(52, DIRS, H, P)
        w_buf = carve(64, DIRS, H, P)
        w_dec = carve(68, DIRS, H, P)
        state = carve(72, DIRS, H, P)
        sig_a = carve(76, TOK)
        v_t = carve(78, H, TOK)
        o_acc = carve(78, NC, H, P)
        conv_t = carve(86, 2, TOK)
        b_sb = carve(90, 2, TOK)
        bx = carve(94, 2, TOK)
        ya = carve(98, 2, TOK)
        mixed = carve(86, KD, TOK)
        z_silu = carve(110, H, TOK)
        sig_d = carve(0, KD, TOK)
        o_junk = carve(32, P)
        yd_f = carve(56, 2, TOK)
        mg_f = carve(60, 2, TOK)
        h_t = carve(64, KD, TOK)
        relu_t = carve(80, 2, TOK)
        hid_f = carve(84, 2, TOK)
        rb = carve(88, TOK)
        acc = carve(90, TOK)
        sq_t = carve(92, SQ, TOK)
        p_in = carve(98, 2, TOK)
        ple = carve(32, KD, TOK)
        sig_p = carve(48, 2, TOK)
        arena_stack.close()
        f_hi = sb("f_hi", [P, KD, TOK], F32R)
        f_lo = sb("f_lo", [P, KD, TOK], F32R)
        hid_hi = sb("hid_hi", [P, 8, TOK], F32R)
        hid_lo = sb("hid_lo", [P, 8, TOK], F32R)
        w16_hi = sb("w16_hi", [P, KD * 16], F32R)
        w16_lo = sb("w16_lo", [P, KD * 16], F32R)
        sb("arena_rest", [P, 37 * KB])
        y_hi = sb("y_hi", [P, H, TOK], F32R)
        y_lo = sb("y_lo", [P, H, TOK], F32R)

        ident, incl_f, incl_b, strict_f, strict_b, ones = (masks[:, i, :] for i in range(6))
        off = [lmask[:, l, :] for l in range(LEVELS)]
        tri = [None] + [lmask[:, LEVELS + l, :] for l in range(LEVELS - 1)]
        incl = (incl_f, incl_b)
        strict = (strict_f, strict_b)

        dense = ctx.enter_context(nc.psum_tensor("dense", [P, 4, TOK], F32))
        extra = ctx.enter_context(nc.psum_tensor("extra", [P, 4, TOK], F32))

        cols_in_s, masks_in_s, levels_in_s = sem("cols_landed"), sem("masks_landed"), sem("levels_landed")
        x_in_s = [sem(f"x_landed{i}") for i in range(4)]
        x2_in_s, p_in_s, out_s = sem("x_again_landed"), sem("p_landed"), sem("out_stored")
        raw_s = [sem(f"raw_landed{i}") for i in range(RING)]
        hi_s, lo_s, tile_s = sem("w_hi_made"), sem("w_lo_made"), sem("tile_done")
        read_s = [sem(f"tile_read{i}") for i in range(4)]
        sq_s, acc_s, sqsum_s = sem("square_made"), sem("square_added"), sem("squares_summed")
        ms_s, root_s, rb_s = sem("mean_made"), sem("root_made"), sem("rstd_made")
        nf_s, nhi_s, nlo_s = sem("norm_made"), sem("norm_hi_made"), sem("norm_lo_made")
        w16h_s, w16l_s, ba_s, bat_s = sem("w16_hi_made"), sem("w16_lo_made"), sem("ba_done"), sem("ba_t_copied")
        batr_s, bac_s = sem("ba_transposed"), sem("ba_copied")
        beta_s, abs_s, exp_s, aexp_s = sem("beta_made"), sem("alpha_abs"), sem("alpha_exp"), sem("a_exp")
        g_s, gsum_s, ecol_s = sem("gate_made"), sem("gate_sums"), sem("decay_columns")
        ksq_s, kroot_s, qsq_s = sem("k_sq_made"), sem("k_root"), sem("q_sq_made")
        tap_s, silu_s, qksq_s, ss_s, tr_s = (sem("centre_tap"), sem("silu_made"), sem("qk_squared"),
                                             sem("qk_summed"), sem("kv_transposed"))
        kcopy_s, vcopy_s = sem("k_tok_made"), sem("v_tok_made")
        yd_s, yh_s, yl_s = sem("y_dn_made"), sem("y_hi_made"), sem("y_lo_made")
        siga_s, sigau_s, mg_s = sem("gate_a_made"), sem("gate_a_applied"), sem("merged")
        gm_s, dsum_s, dexp_s = sem("gates_spread"), sem("decay_sums"), sem("decay_exp")
        kk_s, qk_s, p_s = sem("kk_done"), sem("qk_done"), sem("qk_decayed")
        v_s, vm_s, xvx_s, xu_s = sem("ax_done"), sem("ax_masked"), sem("xax_done"), sem("inverse_updated")
        turn_s, xt_s, z_s, y_s = sem("inverse_turned"), sem("turned_copied"), sem("z_made"), sem("y_made")
        trix_s, triqk_s = sem("x_half_made"), sem("qk_half_made")
        sread_s, r_s, qs_s = sem("state_read"), sem("r_made"), sem("qs_added")
        xr_s, w_s, wd_s = sem("solved"), sem("w_made"), sem("w_decayed")
        in_s, ds_s, oadd_s, st_s = sem("intra_done"), sem("ds_done"), sem("o_added"), sem("state_made")
        osq_s, omean_s, oroot_s, onorm_s, otr_s = (sem("o_squared"), sem("o_mean"), sem("o_root"),
                                                   sem("o_normed"), sem("o_transposed"))
        hp_s = sem("ple_added")
        hh_s, hf_s, hl_s = sem("hid_hi_made"), sem("hid_squared"), sem("hid_lo_made")
        ph_s, pl_s, gp_s, fin_s = sem("p_hi_made"), sem("p_lo_made"), sem("ple_gate"), sem("final_made")
        dv_s = sem("vector_steps")
        ac_s = sem("scalar_steps")

        FF_T0 = first_tile(S_FF)
        assert FF_T0 % 4 == 0 and S_FF % RING == 0 and FF_SLABS % RING == 0

        def bank(u):
            return dense[:, u % 4, :]

        def split_view(t, s, nk=KD):
            return t[:, s % RING, :].rearrange("p (k n) -> p k n", k=nk)

        def conv_col(i, tap):
            at = C_CONVQ + tap * 3 * H + (i + H if i < H else i - H if i < 2 * H else i)
            return cols[:, at:at + 1]

        def over_heads(m):
            return m.unsqueeze(1).broadcast_to([P, H, P])

        def heads_of(flat):
            return flat.rearrange("p (h n) -> p h n", h=H)

        def part(t, slot, q, parts):
            return t[:, slot, q * SLAB // parts:(q + 1) * SLAB // parts]

        def scan_banks(n, d):
            return (0, 1) if n > 0 and d == 0 else (2, 3)

        def slot_of(n, d):
            return d if n > 0 else 0

        def wait_read(eng, u):
            eng.wait_ge(read_s[u % 4], u // 4 + 1)

        def tile_ends(s, j):
            nk = UNITS // tiles_of(s)
            return j // nk if j % nk == nk - 1 else None

        block = ctx.enter_context(nc.Block())

        @block.sync
        def _(sp):
            for i in range(4):
                sp.dma_start(x_in[:, 2 * i:2 * i + 2, :], x_t[:, 2 * i:2 * i + 2, :]).then_inc(x_in_s[i], 16)
            sp.dma_start(masks[:], masks_in).then_inc(masks_in_s, 16)
            sp.dma_start(cols[:], cols_in).then_inc(cols_in_s, 16)
            for s in range(RING):
                sp.dma_start(raw[:, s, :], stream[s]).then_inc(raw_s[s], 16)
            sp.dma_start(lmask[:], levels_in).then_inc(levels_in_s, 16)

            def slab_pair(i):
                for r in range(RING):
                    sp.wait_ge(lo_s, i * (RING * LO_PARTS) + LO_PARTS * (r + 1 - RING))
                    sp.dma_start(raw[:, r, :], stream[bass.ds(i * RING + r, 1)].rearrange("s p n -> p (s n)"))\
                      .then_inc(raw_s[r], 16)

            with sp.Fori(1, S_WD // RING) as i:
                slab_pair(i)
            sp.wait_ge(otr_s, H)
            sp.dma_start(h_t, x_t).then_inc(x2_in_s, 16)
            with sp.Fori(S_WD // RING, S_FF // RING) as i:
                slab_pair(i)
            sp.wait_ge(mg_s, KD)
            sp.dma_start(p_in, p_t).then_inc(p_in_s, 16)
            with sp.Fori(S_FF // RING, S_PP // RING) as i:
                slab_pair(i)
            for s in range(S_PP, N_SLABS):
                sp.wait_ge(lo_s, LO_PARTS * (s + 1 - RING))
                sp.dma_start(raw[:, s % RING, :], stream[s]).then_inc(raw_s[s % RING], 16)
            for m in range(0, KD, 2):
                sp.wait_ge(fin_s, m + 2)
                sp.dma_start(out[:, m:m + 2, :], h_t[:, m:m + 2, :]).then_inc(out_s, 16)
            sp.wait_ge(out_s, 16 * (KD // 2))

        @block.tensor
        def _(pe):
            mm = nc.tensor.matmul

            def three(o, wh, wl, ah, al, first, last):
                mm(o, wh, ah, start=first, stop=False)
                mm(o, wh, al, start=False, stop=False)
                return mm(o, wl, ah, start=False, stop=last)

            def unit(s, j, src):
                nk = UNITS // tiles_of(s)
                m, k = divmod(j, nk)
                wh, wl = split_view(w_hi, s, nk), split_view(w_lo, s, nk)
                if j == 0:
                    pe.wait_ge(hi_s, HI_PARTS * (s + 1))
                    pe.wait_ge(lo_s, LO_PARTS * (s + 1))
                u = first_tile(s) + m
                if k == 0 and u >= 4:
                    pe.wait_ge(read_s[u % 4], u // 4)
                ah, al = src
                last = three(bank(u), wh[:, k, m * P:(m + 1) * P], wl[:, k, m * P:(m + 1) * P],
                             ah[:, k, :], al[:, k, :], k == 0, k == nk - 1)
                if k == nk - 1:
                    last.then_inc(tile_s, 1)

            def norm_total(r, a):
                pe.wait_ge(acc_s, (r + 1) * (KD - 1))
                mm(extra[:, 0, :], ones, a, start=True, stop=True).then_inc(sqsum_s, 1)

            def small_projection():
                pe.wait_ge(w16h_s, 1)
                pe.wait_ge(w16l_s, 1)
                wh = w16_hi[:].rearrange("p (k n) -> p k n", k=KD)
                wl = w16_lo[:].rearrange("p (k n) -> p k n", k=KD)
                for k in range(KD):
                    last = three(extra[0:16, 1, :], wh[:, k, :], wl[:, k, :], act_hi[:, k, :], act_lo[:, k, :],
                                 k == 0, k == KD - 1)
                last.then_inc(ba_s, 1)

            def turn_projection():
                pe.wait_ge(bat_s, 1)
                for c in range(NC):
                    last = nc.tensor.transpose(extra[:, 1, 16 * c:16 * c + 16], ba_t[0:16, c * P:(c + 1) * P],
                                               ident[0:16, 0:16])
                last.then_inc(batr_s, 1)

            def gate_sums():
                pe.wait_ge(g_s, 1)
                for q, lhs in enumerate((incl, strict, (ones, ones))):
                    for d in range(DIRS):
                        at = (q * DIRS + d) * NC * H
                        last = mm(extra[:, 1, at:at + NC * H].rearrange("p (c h) -> p c h", c=NC),
                                  lhs[d], gate[:, :, d * H:(d + 1) * H], start=True, stop=True)
                last.then_inc(gsum_s, 1)

            def square_sums(i, h, which):
                pe.wait_ge(qksq_s, i + 1)
                for c in range(NC):
                    last = mm(extra[:, which, c * H + h:c * H + h + 1], sq_qk[:, i % 2, c * P:(c + 1) * P], ones[:, 0:1],
                              start=True, stop=True)
                last.then_inc(ss_s, 1)

            def to_tokens(i, src, h):
                pe.wait_ge(silu_s, i + 1 if i < H else i + H + 1)
                if i == 5:
                    pe.wait_ge(qsq_s, 1)
                elif i == 4:
                    pe.wait_ge(kcopy_s, 3)
                elif 2 <= i < H:
                    pe.wait_ge(kcopy_s, i - 1)
                elif i > 5:
                    pe.wait_ge(vcopy_s, i - 5)
                for c in range(NC):
                    last = nc.tensor.transpose(extra[:, 2 + i % 2, c * P:(c + 1) * P],
                                               src[:, h, c * P:(c + 1) * P], ident)
                last.then_inc(tr_s, 1)

            def qkv_aux(i):
                h = i % H
                if i < H:
                    square_sums(i, h, 0)
                    to_tokens(i, k_t, h)
                elif i < 2 * H:
                    if i == H:
                        pe.wait_ge(kcopy_s, 4)
                    square_sums(i, h, 3)
                else:
                    to_tokens(i - H, v_t, h)

            def heads(o, lhs, rhs):
                for h in range(H):
                    last = mm(o[:, h * P:(h + 1) * P], lhs(h), rhs(h), start=True, stop=True)
                return last

            def decay_sums(i):
                pe.wait_ge(gm_s, i + 1)
                if i == 0:
                    pe.wait_ge(ksq_s, 1)
                else:
                    pe.wait_ge(vm_s, upper(i - 1, LEVELS - 1))
                mm(extra[:, 0, :], strict[0], gate_f.rearrange("p h n -> p (h n)"), start=True, stop=False)
                mm(extra[:, 0, :], strict[1], gate_b.rearrange("p h n -> p (h n)"), start=False, stop=True)\
                    .then_inc(dsum_s, 1)

            def products(i, which):
                t = slice(ORDER[i] * P, (ORDER[i] + 1) * P)
                if which == 0:
                    if i == 0:
                        pe.wait_ge(ecol_s, 1)
                        pe.wait_ge(silu_s, H)
                    else:
                        pe.wait_ge(xt_s, level(i - 1, LEVELS - 1))
                    heads(extra[:, 1, :], lambda h: k_t[:, h, t], lambda h: k_t[:, h, t]).then_inc(kk_s, 1)
                else:
                    pe.wait_ge(dexp_s, i + 1)
                    if i == 0:
                        pe.wait_ge(silu_s, 2 * H)
                    heads(extra[:, 0, :], lambda h: k_t[:, h, t], lambda h: q_t[:, h, t]).then_inc(qk_s, 1)

            def level_ax(i, l):
                pe.wait_ge(y_s, upper(i, l))
                if l == 1:
                    pe.wait_ge(p_s, i + 1)
                else:
                    pe.wait_ge(vm_s, upper(i, l - 1))
                heads(extra[:, 0, :], lambda h: a_t[:, h, :], lambda h: y[:, h, :]).then_inc(v_s, 1)

            def level_xax(i, l):
                pe.wait_ge(vm_s, upper(i, l))
                pe.wait_ge(z_s, upper(i, l))
                pe.wait_ge(xt_s, level(i, l - 1))
                heads(extra[:, 1, :], lambda h: z_t[:, h, :], lambda h: ax[:, h, :]).then_inc(xvx_s, 1)

            def turn(i, l):
                pe.wait_ge(xu_s, level(i, l))
                src = inv_t[:, ORDER[i]] if l == 0 else inv
                for h in range(H):
                    last = nc.tensor.transpose(extra[:, 1, h * P:(h + 1) * P], src[:, h, :], ident)
                last.then_inc(turn_s, 1)

            def scan_read(n, d):
                t = slice(chunk_of(n, d) * P, (chunk_of(n, d) + 1) * P)
                b_r, b_o = scan_banks(n, d)
                pe.wait_ge(st_s, pair(n - 1, d))
                pe.wait_ge(oadd_s, pair(n - 1, d))
                if (n, d) == (1, 0):
                    pe.wait_ge(xt_s, level(NC - 1, LEVELS - 1))
                heads(extra[:, b_r, :], lambda h: k_t[:, h, t], lambda h: state[:, d, h, :])
                heads(extra[:, b_o, :], lambda h: q_t[:, h, t], lambda h: state[:, d, h, :]).then_inc(sread_s, 1)

            def scan_solve(n, d):
                pe.wait_ge(trix_s, pair(n, d))
                if n > 0:
                    pe.wait_ge(r_s, pair(n - 1, d))
                elif d == 0:
                    pe.wait_ge(vcopy_s, 4)
                else:
                    pe.wait_ge(st_s, pair(0, 0))
                heads(extra[:, scan_banks(n, d)[0], :], lambda h: tri_x[slot_of(n, d)][:, h, :],
                      lambda h: r_buf[:, d, h, :] if n > 0 else v_tok[:, chunk_of(n, d), h, :]).then_inc(xr_s, 1)

            def scan_write(n, d):
                b_r, b_o = scan_banks(n, d)
                pe.wait_ge(w_s, pair(n, d))
                pe.wait_ge(triqk_s, pair(n, d))
                if n > 0:
                    pe.wait_ge(qs_s, pair(n - 1, d))
                elif d == 1:
                    pe.wait_ge(oadd_s, pair(0, 0))
                heads(extra[:, b_o, :], lambda h: tri_qk[slot_of(n, d)][:, h, :], lambda h: w_buf[:, d, h, :])\
                    .then_inc(in_s, 1)
                if n < NC - 1:
                    pe.wait_ge(wd_s, pair(n, d))
                    heads(extra[:, b_r, :], lambda h: k_tok[:, chunk_of(n, d), h, :], lambda h: w_dec[:, d, h, :])\
                        .then_inc(ds_s, 1)

            def delta(what, *at):
                if what in ("decay", "kk", "qk", "ax", "xax", "turn", "read", "solve", "write"):
                    {"decay": decay_sums, "kk": lambda i: products(i, 0), "qk": lambda i: products(i, 1),
                     "ax": level_ax, "xax": level_xax, "turn": turn, "read": scan_read, "solve": scan_solve,
                     "write": scan_write}[what](*at)

            pe.wait_ge(masks_in_s, 16)
            norm_total(0, acc0)
            n_src, y_src, f_src, hid_src = (act_hi, act_lo), (y_hi, y_lo), (f_hi, f_lo), (hid_hi, hid_lo)
            for s in range(S_FF):
                for j in range(UNITS):
                    if s == 0 and j < KD:
                        pe.wait_ge(nhi_s, j + 1)
                        pe.wait_ge(nlo_s, j + 1)
                    if s == S_WA and j < H:
                        pe.wait_ge(yh_s, j + 1)
                        pe.wait_ge(yl_s, j + 1)
                    if s == S_WD and j < H:
                        pe.wait_ge(yh_s, H + j + 1)
                        pe.wait_ge(yl_s, H + j + 1)
                    if s == S_WO and j < KD:
                        pe.wait_ge(nhi_s, KD + j + 1)
                        pe.wait_ge(nlo_s, KD + j + 1)
                    unit(s, j, y_src if tiles_of(s) == 4 else n_src)
                    if (s, j) == (0, UNITS - 1):
                        small_projection()
                    if (s, j) == (1, 1):
                        turn_projection()
                    if 1 <= s <= 6 and j in (4, 12):
                        qkv_aux(2 * (s - 1) + (j == 12))
                    if (s, j) == (3, 8):
                        gate_sums()
                    for step in DELTA.get(s * UNITS + j, ()):
                        delta(*step)
                    if (s, j) == (22, 6):
                        pe.wait_ge(onorm_s, 1)
                        for h in range(H):
                            for c in range(NC):
                                last = nc.tensor.transpose(extra[:, h, c * P:(c + 1) * P], o_acc[:, c, h, :], ident)
                            last.then_inc(otr_s, 1)

            def ff_group(i, first):
                for b in range(FF_SLABS):
                    pe.wait_ge(hi_s, i * (HI_PARTS * FF_SLABS) + HI_PARTS * (S_FF + b + 1))
                    pe.wait_ge(lo_s, i * (LO_PARTS * FF_SLABS) + LO_PARTS * (S_FF + b + 1))
                    wh, wl = split_view(w_hi, b), split_view(w_lo, b)
                    ah, al = f_src if b < FF_SLABS // 2 else hid_src
                    for m in range(2):
                        u = 2 * b + m
                        pe.wait_ge(read_s[u % 4], i * 4 + (FF_T0 + u) // 4)
                        for k in range(KD):
                            if first and u == 0:
                                pe.wait_ge(nhi_s, 2 * KD + k + 1)
                                pe.wait_ge(nlo_s, 2 * KD + k + 1)
                            if u == FF_SLABS:
                                pe.wait_ge(hh_s, i * 8 + (k + 1))
                                pe.wait_ge(hl_s, i * 8 + (k + 1))
                            last = three(bank(u), wh[:, k, m * P:(m + 1) * P], wl[:, k, m * P:(m + 1) * P],
                                         ah[:, k, :], al[:, k, :], k == 0, k == KD - 1)
                        last.then_inc(tile_s, 1)
                        if first and u == 0:
                            norm_total(1, acc)

            ff_group(0, True)
            with pe.Fori(1, FF_GROUPS) as i:
                ff_group(i, False)

            for k in range(2):
                pe.wait_ge(ph_s, k + 1)
                pe.wait_ge(pl_s, k + 1)
            for j in range(UNITS):
                unit(S_PP, j, y_src)
            for s in range(S_PG, N_SLABS):
                for j in range(UNITS):
                    if s == S_PG and j < KD:
                        pe.wait_ge(nhi_s, 3 * KD + j + 1)
                        pe.wait_ge(nlo_s, 3 * KD + j + 1)
                    unit(s, j, n_src)
                    if (s, j) == (S_PG, 0):
                        norm_total(2, acc)
            norm_total(3, acc)

        @block.scalar
        def _(act):
            A = nc.scalar.activation

            def split_hi(s, q):
                if q == 0:
                    act.wait_ge(raw_s[s % RING], 16 * (s // RING + 1))
                    if s >= RING:
                        act.wait_ge(tile_s, first_tile(s - RING + 1))
                A(part(w_hi, s % RING, q, HI_PARTS), part(raw, s % RING, q, HI_PARTS), ACT.Copy).then_inc(hi_s, 1)

            def square(r, k, sq, src):
                if k >= SQ:
                    act.wait_ge(acc_s, r * (KD - 1) + max(k - SQ, 1))
                elif r > 1 and k == 0:
                    act.wait_ge(rb_s, r)
                A(sq[:, k % SQ, :], src, ACT.Square).then_inc(sq_s, 1)

            def norm_root(r, buf):
                act.wait_ge(ms_s, r + 1)
                A(buf[:, 1, :], buf[:, 0, :], ACT.Sqrt).then_inc(root_s, 1)

            def qkv_tile(i):
                u = i
                act.wait_ge(tile_s, u + 1)
                A(conv_t[:, i % 2, :], bank(u), ACT.Copy, scale=conv_col(i, 1)).then_inc(tap_s, 1)
                wait_read(act, u)
                to = (k_t, q_t, v_t)[i // H][:, i % H, :]
                A(to, conv_t[:, i % 2, :], ACT.Silu).then_inc(silu_s, 1)
                if i < 2 * H:
                    c = i
                    act.wait_ge(silu_s, i + 1)
                    if c > 1:
                        act.wait_ge(ss_s, c - 1)
                    A(sq_qk[:, c % 2, :], to, ACT.Square).then_inc(qksq_s, 1)

            def delta(what, i, l=0):
                if what == "decay":
                    act.wait_ge(dsum_s, i + 1)
                    if i > 0:
                        act.wait_ge(xvx_s, upper(i - 1, LEVELS - 1))
                    A(decay.rearrange("p h n -> p (h n)"), extra[:, 0, :], ACT.Exp).then_inc(dexp_s, 1)
                if what == "turn":
                    act.wait_ge(turn_s, level(i, l))
                    to = inv if l == 0 else inv_t[:, ORDER[i]]
                    A(to.rearrange("p h n -> p (h n)"), extra[:, 1, :], ACT.Copy).then_inc(xt_s, 1)
                if what == "solve":
                    n, d = i, l
                    act.wait_ge(xr_s, pair(n, d))
                    if n > 0:
                        act.wait_ge(in_s, pair(n - 1, d))
                        act.wait_ge(ds_s, pair(n - 1, d))
                    for to, by, done in ((w_buf, c1, w_s), (w_dec, c1_end, wd_s)):
                        if done is wd_s and n == NC - 1:
                            continue
                        for h in range(H):
                            last = A(to[:, d, h, :], extra[:, scan_banks(n, d)[0], h * P:(h + 1) * P], ACT.Copy,
                                     scale=by[:, chunk_of(n, d), d, h:h + 1])
                        last.then_inc(done, 1)

            def finish_tile(s, m):
                u = first_tile(s) + m
                if s < S_BXC:
                    qkv_tile(u)
                elif s < S_WA and (s - S_BXC) % 3 == 0:
                    act.wait_ge(tile_s, u + 1)
                    if s > S_BXC:
                        wait_read(act, first_tile(S_BXC + 1) + m)
                    A(b_sb[:, m, :], bank(u), ACT.Copy).then_inc(read_s[u % 4], 1)
                elif s < S_WA and (s - S_BXC) % 3 == 2:
                    i = 2 * ((s - S_BXC) // 3) + m
                    wait_read(act, u)
                    A(y_hi[:, i, :], ya[:, m, :], ACT.Copy).then_inc(yh_s, 1)
                elif S_WA <= s < S_GA:
                    act.wait_ge(tile_s, u + 1)
                    if s == S_WA and m == 0:
                        act.wait_ge(yl_s, H)
                    A(mixed[:, u - first_tile(S_WA), :], bank(u), ACT.Copy).then_inc(read_s[u % 4], 1)
                elif S_GA <= s < S_Z:
                    i = u - first_tile(S_GA)
                    act.wait_ge(tile_s, u + 1)
                    if i > 0:
                        act.wait_ge(sigau_s, i)
                    A(sig_a, bank(u), ACT.Sigmoid).then_inc(read_s[u % 4], 1)
                elif S_Z <= s < S_GD:
                    act.wait_ge(tile_s, u + 1)
                    A(z_silu[:, u - first_tile(S_Z), :], bank(u), ACT.Silu).then_inc(read_s[u % 4], 1)
                elif S_GD <= s < S_WD:
                    act.wait_ge(tile_s, u + 1)
                    if s == S_GD and m == 0:
                        act.wait_ge(sread_s, pair(NC - 2, 1))
                    A(sig_d[:, u - first_tile(S_GD), :], bank(u), ACT.Sigmoid).then_inc(read_s[u % 4], 1)
                elif S_WD <= s < S_WO:
                    i = u - first_tile(S_WD)
                    act.wait_ge(mg_s, i + 1)
                    act.wait_ge(tile_s, first_tile(S_WD))
                    A(act_hi[:, i, :], mg_f[:, i % 2, :], ACT.Copy).then_inc(nhi_s, 1)
                elif S_WO <= s < S_FF:
                    i = u - first_tile(S_WO)
                    wait_read(act, u)
                    A(f_hi[:, i, :], h_t[:, i, :], ACT.Copy, scale=cols[:, C_GFFN + i:C_GFFN + i + 1])\
                        .then_inc(nhi_s, 1)
                    square(1, i, sq_t, h_t[:, i, :])

            for k in range(KD):
                act.wait_ge(x_in_s[k // 2], 16)
                square(0, k, sq_in, x_in[:, k, :])
            norm_root(0, norm0)
            for q in range(HI_PARTS):
                split_hi(0, q)
            act.wait_ge(cols_in_s, 16)
            A(w16_hi[:], cols[:, C_W16:C_W16 + KD * 16], ACT.Copy).then_inc(w16h_s, 1)
            for k in range(KD):
                act.wait_ge(nf_s, k + 1)
                A(act_hi[:, k, :], n_f[:, k % 4, :], ACT.Copy).then_inc(nhi_s, 1)

            for s in range(S_FF):
                for j in range(UNITS):
                    if j in (0, 5):
                        split_hi(s + 1, j // 5)
                    m = tile_ends(s, j)
                    if m is not None:
                        finish_tile(s, m)
                    if (s, j) == (1, 3):
                        act.wait_ge(bac_s, 1)
                        A(beta[:], ba[:, :, 0:8], ACT.Sigmoid).then_inc(beta_s, 1)
                        A(tiny[:, 5, 0:8], cols[:, C_ALOG:C_ALOG + 8], ACT.Exp).then_inc(aexp_s, 1)
                        act.wait_ge(abs_s, 1)
                        A(tiny[:, 1, :], tiny[:, 0, :], ACT.Exp, scale=-1.0).then_inc(exp_s, 1)
                    if 1 <= s <= 2 and j in (4, 12):
                        i = 2 * (s - 1) + (j == 12)
                        act.wait_ge(tr_s, i + 1)
                        A(k_tok[:, :, i, :], extra[:, 2 + i % 2, :].rearrange("p (c n) -> p c n", c=NC), ACT.Copy)\
                            .then_inc(kcopy_s, 1)
                    if (s, j) == (2, 13):
                        act.wait_ge(ksq_s, 1)
                        A(k_cols[:, 1, :], k_cols[:, 0, :], ACT.Sqrt).then_inc(kroot_s, 1)
                    if (s, j) == (3, 9):
                        act.wait_ge(gsum_s, 1)
                        A(e_cols[:].rearrange("p q d c h -> p (q d c h)"), extra[:, 1, 0:3 * DIRS * NC * H], ACT.Exp)\
                            .then_inc(ecol_s, 1)
                    for step in DELTA.get(s * UNITS + j, ()):
                        delta(*step)
                    if (s, j) == (20, 10):
                        act.wait_ge(oadd_s, pair(NC - 1, 1))
                        for c in range(NC):
                            for h in range(H):
                                if c + h:
                                    act.wait_ge(ac_s, c * H + h)
                                last = A(o_junk, o_acc[:, c, h, :], ACT.Square,
                                         accum_out=o_sq[:, c * H + h:c * H + h + 1])
                                last.then_inc(ac_s, 1)
                    if (s, j) == (21, 3):
                        act.wait_ge(omean_s, 1)
                        A(norm_t[:, 1, :], norm_t[:, 0, :], ACT.Sqrt).then_inc(oroot_s, 1)
                    if (s, j) == (22, 7):
                        for h in range(H):
                            act.wait_ge(yd_s, h + 1)
                            A(y_hi[:, h, :], yd_f[:, h % 2, :], ACT.Copy).then_inc(yh_s, 1)

            def ff_group(i, first):
                for b in range(FF_SLABS):
                    r = (b + 1) % RING
                    act.wait_ge(raw_s[r], i * (16 * FF_SLABS // RING) + 16 * ((S_FF + b + 1) // RING + 1))
                    act.wait_ge(tile_s, i * 16 + (FF_T0 + 2 * b))
                    for q in range(HI_PARTS):
                        A(part(w_hi, r, q, HI_PARTS), part(raw, r, q, HI_PARTS), ACT.Copy).then_inc(hi_s, 1)
                    if first and b == 0:
                        norm_root(1, sq_t)
                    if first and b == 2:
                        act.wait_ge(p_in_s, 16)
                        for k in range(2):
                            A(y_hi[:, k, :], p_in[:, k, :], ACT.Copy).then_inc(ph_s, 1)
                    if b < FF_SLABS // 2:
                        for m in range(2):
                            u = 2 * b + m
                            act.wait_ge(read_s[u % 4], i * 4 + ((FF_T0 + u) // 4 + 1))
                            if not first:
                                act.wait_ge(tile_s, i * 16 + FF_T0)
                            A(hid_hi[:, 2 * b + m, :], relu_t[:, m, :], ACT.Square).then_inc(hh_s, 1)
                            if not first or b > 0:
                                act.wait_ge(hl_s, i * 8 + (2 * b + m - 1))
                            A(hid_f[:, m, :], relu_t[:, m, :], ACT.Square).then_inc(hf_s, 1)

            ff_group(0, True)
            with act.Fori(1, FF_GROUPS) as i:
                ff_group(i, False)

            for k in range(KD):
                wait_read(act, first_tile(S_PP) - KD + k)
                A(act_hi[:, k, :], h_t[:, k, :], ACT.Copy, scale=cols[:, C_GPLE + k:C_GPLE + k + 1])\
                    .then_inc(nhi_s, 1)
                square(2, k, sq_t, h_t[:, k, :])
                u = first_tile(S_PP) + k
                act.wait_ge(tile_s, u + 1)
                A(ple[:, k, :], bank(u), ACT.Copy).then_inc(read_s[u % 4], 1)
                if k == 0:
                    for q in range(HI_PARTS):
                        split_hi(S_PG, q)
            norm_root(2, sq_t)
            for q in range(HI_PARTS):
                split_hi(S_PG + 1, q)
            for s in range(S_PG, N_SLABS):
                if S_PG < s < N_SLABS - 1:
                    for q in range(HI_PARTS):
                        split_hi(s + 1, q)
                for m in range(2):
                    i = 2 * (s - S_PG) + m
                    wait_read(act, first_tile(s) + m)
                    A(sig_p[:, m, :], sig_p[:, m, :], ACT.Sigmoid).then_inc(gp_s, 1)
                    act.wait_ge(hp_s, i + 1)
                    square(3, i, sq_t, h_t[:, i, :])
            norm_root(3, sq_t)

        @block.vector
        def _(dve):
            V = nc.vector
            steps = [0]

            def link(ins):
                steps[0] += 1
                ins.then_inc(dv_s, 1)
                dve.wait_ge(dv_s, steps[0])

            def split_lo(s, q):
                dve.wait_ge(hi_s, HI_PARTS * s + q * HI_PARTS // LO_PARTS + 1)
                V.tensor_tensor(part(w_lo, s % RING, q, LO_PARTS), part(raw, s % RING, q, LO_PARTS),
                                part(w_hi, s % RING, q, LO_PARTS).bitcast(F32), ALU.subtract).then_inc(lo_s, 1)

            def rsqrt_steps(x, root, t, to):
                link(V.reciprocal(root, root))
                link(V.tensor_tensor(t, root, root, ALU.mult))
                link(V.scalar_tensor_tensor(t, t, -0.5, x, ALU.mult, ALU.mult))
                return V.scalar_tensor_tensor(to, t, 1.5, root, ALU.add, ALU.mult)

            def norm_rstd(r, buf, to):
                dve.wait_ge(sqsum_s, r + 1)
                V.tensor_scalar(buf[:, 0, :], extra[:, 0, :], 1.0 / D, EPS, ALU.mult, ALU.add).then_inc(ms_s, 1)
                dve.wait_ge(root_s, r + 1)
                rsqrt_steps(buf[:, 0, :], buf[:, 1, :], buf[:, 2, :], to).then_inc(rb_s, 1)
                dve.wait_ge(rb_s, r + 1)

            def qkv_tile(i):
                dve.wait_ge(tap_s, i + 1)
                c = conv_t[:, i % 2, :]
                link(V.scalar_tensor_tensor(c[:, 1:TOK], bank(i)[:, 0:TOK - 1], conv_col(i, 0), c[:, 1:TOK],
                                            ALU.mult, ALU.add))
                V.scalar_tensor_tensor(c[:, 0:TOK - 1], bank(i)[:, 1:TOK], conv_col(i, 2), c[:, 0:TOK - 1],
                                       ALU.mult, ALU.add).then_inc(read_s[i % 4], 1)

            def finish_tile(s, m):
                u = first_tile(s) + m
                if s < S_BXC:
                    qkv_tile(u)
                elif s < S_WA:
                    g, what = divmod(s - S_BXC, 3)
                    i = 2 * g + m
                    if what == 1:
                        dve.wait_ge(tile_s, u + 1)
                        wait_read(dve, first_tile(s - 1) + m)
                        V.tensor_tensor(bx[:, m, :], b_sb[:, m, :], bank(u), ALU.mult).then_inc(read_s[u % 4], 1)
                        wait_read(dve, u)
                        if g:
                            dve.wait_ge(yh_s, m + 1)
                            dve.wait_ge(yl_s, m + 1)
                        taps = [cols[:, C_CONVA + 4 * q + i:C_CONVA + 4 * q + i + 1] for q in range(3)]
                        y = ya[:, m, :]
                        link(V.tensor_scalar(y, bx[:, m, :], taps[1], None, ALU.mult))
                        link(V.scalar_tensor_tensor(y[:, 1:TOK], bx[:, m, 0:TOK - 1], taps[0], y[:, 1:TOK],
                                                    ALU.mult, ALU.add))
                        link(V.scalar_tensor_tensor(y[:, 0:TOK - 1], bx[:, m, 1:TOK], taps[2], y[:, 0:TOK - 1],
                                                    ALU.mult, ALU.add))
                    if what == 2:
                        dve.wait_ge(tile_s, u + 1)
                        V.tensor_tensor(ya[:, m, :], ya[:, m, :], bank(u), ALU.mult).then_inc(read_s[u % 4], 1)
                        dve.wait_ge(yh_s, i + 1)
                        V.tensor_tensor(y_lo[:, i, :], ya[:, m, :], y_hi[:, i, :].bitcast(F32), ALU.subtract)\
                            .then_inc(yl_s, 1)
                elif S_GA <= s < S_Z:
                    i = u - first_tile(S_GA)
                    wait_read(dve, u)
                    wait_read(dve, first_tile(S_WA) + i)
                    V.tensor_tensor(mixed[:, i, :], mixed[:, i, :], sig_a, ALU.mult).then_inc(sigau_s, 1)
                elif S_WD <= s < S_WO:
                    i = u - first_tile(S_WD)
                    dve.wait_ge(tile_s, u + 1)
                    if i >= 2:
                        dve.wait_ge(nhi_s, KD + i - 1)
                        dve.wait_ge(nlo_s, KD + i - 1)
                    if i == 0:
                        for q in range(4):
                            wait_read(dve, first_tile(S_WD) - 1 - q)
                    V.tensor_tensor(mg_f[:, i % 2, :], bank(u), sig_d[:, i, :], ALU.mult).then_inc(read_s[u % 4], 1)
                    wait_read(dve, u)
                    V.tensor_tensor(mg_f[:, i % 2, :], mg_f[:, i % 2, :], mixed[:, i, :], ALU.add).then_inc(mg_s, 1)
                    dve.wait_ge(nhi_s, KD + i + 1)
                    V.tensor_tensor(act_lo[:, i, :], mg_f[:, i % 2, :], act_hi[:, i, :].bitcast(F32), ALU.subtract)\
                        .then_inc(nlo_s, 1)
                elif S_WO <= s < S_FF:
                    i = u - first_tile(S_WO)
                    dve.wait_ge(tile_s, u + 1)
                    dve.wait_ge(x2_in_s, 16)
                    V.tensor_tensor(h_t[:, i, :], h_t[:, i, :], bank(u), ALU.add).then_inc(read_s[u % 4], 1)
                    dve.wait_ge(nhi_s, 2 * KD + i + 1)
                    V.scalar_tensor_tensor(f_lo[:, i, :], h_t[:, i, :], cols[:, C_GFFN + i:C_GFFN + i + 1],
                                           f_hi[:, i, :].bitcast(F32), ALU.mult, ALU.subtract).then_inc(nlo_s, 1)

            def spread(col):
                return col.unsqueeze(2).broadcast_to([P, col.shape[1], P])

            def norm_lo(k):
                dve.wait_ge(nhi_s, k + 1)
                V.tensor_tensor(act_lo[:, k, :], n_f[:, k % 4, :], act_hi[:, k, :].bitcast(F32), ALU.subtract)\
                    .then_inc(nlo_s, 1)

            def log_decays():
                dve.wait_ge(batr_s, 1)
                V.tensor_copy(ba[:].rearrange("p c n -> p (c n)"), extra[:, 1, 0:NC * 16]).then_inc(bac_s, 1)
                dve.wait_ge(bac_s, 1)
                x, e, r, t, y, q = (tiny[:, i, :] for i in range(6))
                al = gate[:].rearrange("p c n -> p (c n)")
                dt = cols[:, C_DTB:C_DTB + 8].unsqueeze(1).broadcast_to([P, NC, 8])
                link(V.tensor_tensor(gate[:], ba[:, :, 8:16], dt, ALU.add))
                V.scalar_tensor_tensor(x, al, -1.0, al, ALU.mult, ALU.max).then_inc(abs_s, 1)
                dve.wait_ge(exp_s, 1)
                link(V.tensor_scalar(r, e, 2.0, None, ALU.add))
                link(V.reciprocal(t, r))
                link(V.tensor_tensor(t, t, e, ALU.mult))
                link(V.tensor_tensor(y, t, t, ALU.mult))
                link(V.tensor_scalar(r, y, 1.0 / 17, None, ALU.mult))
                for odd in (15, 13, 11, 9, 7, 5, 3):
                    link(V.scalar_tensor_tensor(r, r, 1.0 / odd, y, ALU.add, ALU.mult))
                link(V.scalar_tensor_tensor(r, r, 1.0, t, ALU.add, ALU.mult))
                link(V.tensor_scalar(al, al, 0.0, None, ALU.max))
                link(V.scalar_tensor_tensor(al, r, 2.0, al, ALU.mult, ALU.add))
                dve.wait_ge(aexp_s, 1)
                ea = tiny[:, 5, 0:8].unsqueeze(1).broadcast_to([P, NC, 8])
                V.scalar_tensor_tensor(gate[:], gate[:], -1.0, ea, ALU.mult, ALU.mult).then_inc(g_s, 1)
                dve.wait_ge(g_s, 1)

            def key_columns():
                dve.wait_ge(ss_s, H)
                sq, root, rec, length, inv_sq = (k_cols[:, i, :] for i in range(5))
                V.tensor_scalar(sq, extra[:, 0, 0:NC * H], EPS, None, ALU.add).then_inc(ksq_s, 1)
                dve.wait_ge(ksq_s, 1)
                link(V.reciprocal(inv_sq, sq))
                dve.wait_ge(kroot_s, 1)
                link(V.reciprocal(rec, root))
                link(V.tensor_tensor(rec, rec, sq, ALU.mult))
                link(V.tensor_tensor(rec, rec, root, ALU.add))
                link(V.tensor_scalar(length, rec, 0.5, None, ALU.mult))
                dve.wait_ge(beta_s, 1)
                for d in range(DIRS):
                    link(V.tensor_tensor(c1[:, :, d, :], beta[:, :, d * H:(d + 1) * H],
                                         inv_sq.rearrange("p (c h) -> p c h", c=NC), ALU.mult))
                for l in range(LEVELS):
                    even, odd = (cols[:, C_PARITY + side * LEVELS + l:C_PARITY + side * LEVELS + l + 1]
                                 for side in range(2))
                    to = c_lvl[:, l, :].rearrange("p (c h) -> p c h", c=NC)
                    link(V.tensor_scalar(to, c1[:, :, 0, :], even, None, ALU.mult))
                    link(V.scalar_tensor_tensor(to, c1[:, :, 1, :], odd, to, ALU.mult, ALU.add))

            def blocks(i, l):
                for h in range(H):
                    c = ORDER[i] * H + h
                    last = V.scalar_tensor_tensor(y[:, h, :], inv[:, h, :], c_lvl[:, l, c:c + 1], tri[l],
                                                  ALU.mult, ALU.mult)
                last.then_inc(y_s, 1)

            def make_k(i):
                dve.wait_ge(kk_s, i + 1)
                dve.wait_ge(dexp_s, i + 1)
                link(V.tensor_tensor(a_t, heads_of(extra[:, 1, :]), decay, ALU.mult))
                for h in range(H):
                    c = ORDER[i] * H + h
                    last = V.scalar_tensor_tensor(y[:, h, :], a_t[:, h, :], c_lvl[:, 0, c:c + 1], off[0],
                                                  ALU.mult, ALU.mult)
                link(last)
                V.tensor_tensor(inv_t[:, ORDER[i]], over_heads(ident), y, ALU.subtract).then_inc(xu_s, 1)

            def make_p(i):
                dve.wait_ge(qk_s, i + 1)
                V.tensor_tensor(qk[:, ORDER[i]], heads_of(extra[:, 0, :]), decay, ALU.mult).then_inc(p_s, 1)

            def turned(i, l):
                if l == 0:
                    dve.wait_ge(xt_s, level(i, 0))
                    dve.wait_ge(xu_s, level(i, 0))
                    blocks(i, 1)

            def mask_ax(i, l):
                dve.wait_ge(v_s, upper(i, l))
                V.tensor_tensor(ax, heads_of(extra[:, 0, :]), over_heads(off[l]), ALU.mult).then_inc(vm_s, 1)

            def update_inverse(i, l):
                dve.wait_ge(xvx_s, upper(i, l))
                V.tensor_tensor(inv, inv, heads_of(extra[:, 1, :]), ALU.subtract).then_inc(xu_s, 1)
                if l < LEVELS - 1:
                    dve.wait_ge(xu_s, level(i, l))
                    blocks(i, l + 1)

            def scan_read(n, d):
                dve.wait_ge(sread_s, pair(n - 1, d))
                c = chunk_of(n, d)
                b_r, b_o = scan_banks(n, d)
                for h in range(H):
                    last = V.scalar_tensor_tensor(r_buf[:, d, h, :], extra[:, b_r, h * P:(h + 1) * P],
                                                  neg_run[:, d, c, h:h + 1], v_tok[:, c, h, :], ALU.mult, ALU.add)
                last.then_inc(r_s, 1)
                if n >= NC // 2:
                    dve.wait_ge(oadd_s, pair(NC - 1 - n, 1 - d))
                for h in range(H):
                    run = e_cols[:, 0, d, c, h:h + 1]
                    if n < NC // 2:
                        last = V.tensor_scalar(o_acc[:, c, h, :], extra[:, b_o, h * P:(h + 1) * P], run, None, ALU.mult)
                    else:
                        last = V.scalar_tensor_tensor(o_acc[:, c, h, :], extra[:, b_o, h * P:(h + 1) * P], run,
                                                      o_acc[:, c, h, :], ALU.mult, ALU.add)
                last.then_inc(qs_s, 1)

            def scan_write(n, d):
                c = chunk_of(n, d)
                b_r, b_o = scan_banks(n, d)
                dve.wait_ge(in_s, pair(n, d))
                if n == 0:
                    V.tensor_copy(o_acc[:, c], heads_of(extra[:, b_o, :])).then_inc(oadd_s, 1)
                else:
                    dve.wait_ge(qs_s, pair(n - 1, d))
                    V.tensor_tensor(o_acc[:, c], o_acc[:, c], heads_of(extra[:, b_o, :]), ALU.add).then_inc(oadd_s, 1)
                if n < NC - 1:
                    dve.wait_ge(ds_s, pair(n, d))
                    if n == 0:
                        V.tensor_copy(state[:, d], heads_of(extra[:, b_r, :])).then_inc(st_s, 1)
                    else:
                        for h in range(H):
                            last = V.scalar_tensor_tensor(state[:, d, h, :], state[:, d, h, :],
                                                          e_cols[:, 2, d, c, h:h + 1], extra[:, b_r, h * P:(h + 1) * P],
                                                          ALU.mult, ALU.add)
                        last.then_inc(st_s, 1)

            def delta(what, *at):
                if what in ("make_k", "make_p", "turn", "ax", "xax", "read", "write"):
                    {"make_k": make_k, "make_p": make_p, "turn": turned, "ax": mask_ax, "xax": update_inverse,
                     "read": scan_read, "write": scan_write}[what](*at)

            def output_norm():
                dve.wait_ge(ac_s, NC * H)
                dve.wait_ge(qsq_s, 1)
                link(V.tensor_scalar(norm_t[:, 5, :], q_sq[:], EPS, EPS * P, ALU.add, ALU.mult))
                V.scalar_tensor_tensor(norm_t[:, 0, :], o_sq[:], 1.0 / P, norm_t[:, 5, :], ALU.mult, ALU.add)\
                    .then_inc(omean_s, 1)
                dve.wait_ge(oroot_s, 1)
                x, root, t, to = (norm_t[:, i, :] for i in range(4))
                link(rsqrt_steps(x, root, t, to))
                flat = o_acc.rearrange("p c h n -> p (c h) n")
                V.tensor_tensor(flat, flat, spread(norm_t[:, 3, :]), ALU.mult).then_inc(onorm_s, 1)

            for k in range(1, KD):
                dve.wait_ge(sq_s, k + 1)
                if k > 1:
                    dve.wait_ge(acc_s, k - 1)
                V.tensor_tensor(acc0, sq_in[:, 0, :] if k == 1 else acc0, sq_in[:, k % SQ, :], ALU.add)\
                    .then_inc(acc_s, 1)
            norm_rstd(0, norm0, rb0)
            dve.wait_ge(cols_in_s, 16)
            for k in range(KD):
                if k >= 4:
                    dve.wait_ge(nhi_s, k - 3)
                V.scalar_tensor_tensor(n_f[:, k % 4, :], x_in[:, k, :], cols[:, C_GMIX + k:C_GMIX + k + 1], rb0,
                                       ALU.mult, ALU.mult).then_inc(nf_s, 1)
                if k == 0:
                    for q in range(LO_PARTS):
                        split_lo(0, q)
                if k > 0:
                    norm_lo(k - 1)
            norm_lo(KD - 1)
            dve.wait_ge(w16h_s, 1)
            V.tensor_tensor(w16_lo[:], cols[:, C_W16:C_W16 + KD * 16], w16_hi[:].bitcast(F32), ALU.subtract)\
                .then_inc(w16l_s, 1)

            for s in range(S_FF):
                for j in range(UNITS):
                    if j in (0, 3, 6, 9):
                        split_lo(s + 1, j // 3)
                    if (s, j) == (1, 0):
                        dve.wait_ge(ba_s, 1)
                        V.tensor_copy(ba_t[0:16, :], extra[0:16, 1, :]).then_inc(bat_s, 1)
                    m = tile_ends(s, j)
                    if m is not None:
                        finish_tile(s, m)
                    if (s, j) == (1, 2):
                        log_decays()
                    if (s, j) == (2, 13):
                        key_columns()
                    if (s, j) == (3, 9):
                        dve.wait_ge(ecol_s, 1)
                        link(V.tensor_scalar(neg_run[:], e_cols[:, 0], -1.0, None, ALU.mult))
                        for d in range(DIRS):
                            link(V.tensor_tensor(c1_end[:, :, d, :], c1[:, :, d, :], e_cols[:, 1, d], ALU.mult))
                    if 5 <= s <= 6 and j in (4, 12):
                        i = 2 * (s - 3) + (j == 12)
                        dve.wait_ge(tr_s, i + 1)
                        V.tensor_tensor(v_tok[:, :, i - H, :], extra[:, 2 + i % 2, :].rearrange("p (c n) -> p c n", c=NC),
                                        spread(k_cols[:, 3, :].rearrange("p (c h) -> p c h", c=NC)[:, :, i - H]),
                                        ALU.mult).then_inc(vcopy_s, 1)
                    if (s, j) == (4, 13):
                        dve.wait_ge(ss_s, 2 * H)
                        V.tensor_copy(q_sq[:], extra[:, 3, 0:NC * H]).then_inc(qsq_s, 1)
                    for step in DELTA.get(s * UNITS + j, ()):
                        delta(*step)
                    if (s, j) == (21, 2):
                        output_norm()
                    if (s, j) == (22, 7):
                        for h in range(H):
                            dve.wait_ge(otr_s, h + 1)
                            wait_read(dve, first_tile(S_Z) + h)
                            if h >= 2:
                                dve.wait_ge(yh_s, H + h - 1)
                                dve.wait_ge(yl_s, H + h - 1)
                            V.scalar_tensor_tensor(yd_f[:, h % 2, :], extra[:, h, :], cols[:, C_GDN:C_GDN + 1],
                                                   z_silu[:, h, :], ALU.mult, ALU.mult).then_inc(yd_s, 1)
                            dve.wait_ge(yh_s, H + h + 1)
                            V.tensor_tensor(y_lo[:, h, :], yd_f[:, h % 2, :], y_hi[:, h, :].bitcast(F32), ALU.subtract)\
                                .then_inc(yl_s, 1)

            def ff_group(i, first):
                for b in range(FF_SLABS):
                    r = (b + 1) % RING
                    for q in range(LO_PARTS):
                        dve.wait_ge(hi_s, i * (HI_PARTS * FF_SLABS)
                                    + (HI_PARTS * (S_FF + b + 1) + q * HI_PARTS // LO_PARTS + 1))
                        V.tensor_tensor(part(w_lo, r, q, LO_PARTS), part(raw, r, q, LO_PARTS),
                                        part(w_hi, r, q, LO_PARTS).bitcast(F32), ALU.subtract).then_inc(lo_s, 1)
                    if first and b == 0:
                        norm_rstd(1, sq_t, rb)
                    if first and b == 2:
                        for k in range(2):
                            dve.wait_ge(ph_s, k + 1)
                            V.tensor_tensor(y_lo[:, k, :], p_in[:, k, :], y_hi[:, k, :].bitcast(F32), ALU.subtract)\
                                .then_inc(pl_s, 1)
                    for m in range(2):
                        u = 2 * b + m
                        dve.wait_ge(tile_s, i * 16 + (FF_T0 + u + 1))
                        if b < FF_SLABS // 2:
                            if not first or b > 0:
                                dve.wait_ge(hf_s, i * 8 + (u - 1))
                            V.scalar_tensor_tensor(relu_t[:, m, :], bank(u), 0.0, rb, ALU.max, ALU.mult)\
                                .then_inc(read_s[u % 4], 1)
                            dve.wait_ge(hf_s, i * 8 + (u + 1))
                            V.tensor_tensor(hid_lo[:, u, :], hid_f[:, m, :], hid_hi[:, u, :].bitcast(F32), ALU.subtract)\
                                .then_inc(hl_s, 1)
                        else:
                            V.tensor_tensor(h_t[:, u - 8, :], h_t[:, u - 8, :], bank(u), ALU.add)\
                                .then_inc(read_s[u % 4], 1)

            ff_group(0, True)
            with dve.Fori(1, FF_GROUPS) as i:
                ff_group(i, False)

            for k in range(KD):
                dve.wait_ge(nhi_s, 3 * KD + k + 1)
                V.scalar_tensor_tensor(act_lo[:, k, :], h_t[:, k, :], cols[:, C_GPLE + k:C_GPLE + k + 1],
                                       act_hi[:, k, :].bitcast(F32), ALU.mult, ALU.subtract).then_inc(nlo_s, 1)
                if k == 0:
                    for q in range(LO_PARTS):
                        split_lo(S_PG, q)
            norm_rstd(2, sq_t, rb)
            for q in range(LO_PARTS):
                split_lo(S_PG + 1, q)
            for s in range(S_PG, N_SLABS):
                if S_PG < s < N_SLABS - 1:
                    for q in range(LO_PARTS):
                        split_lo(s + 1, q)
                for m in range(2):
                    i = 2 * (s - S_PG) + m
                    u = first_tile(s) + m
                    dve.wait_ge(tile_s, u + 1)
                    V.tensor_tensor(sig_p[:, m, :], bank(u), rb, ALU.mult).then_inc(read_s[u % 4], 1)
                    dve.wait_ge(gp_s, i + 1)
                    wait_read(dve, first_tile(S_PP) + i)
                    link(V.tensor_tensor(sig_p[:, m, :], sig_p[:, m, :], ple[:, i, :], ALU.mult))
                    V.tensor_tensor(h_t[:, i, :], h_t[:, i, :], sig_p[:, m, :], ALU.add).then_inc(hp_s, 1)
            norm_rstd(3, sq_t, rb)
            for k in range(KD):
                V.scalar_tensor_tensor(h_t[:, k, :], h_t[:, k, :], cols[:, C_GFIN + k:C_GFIN + k + 1], rb,
                                       ALU.mult, ALU.mult).then_inc(fin_s, 1)

        @block.gpsimd
        def _(pool):
            G = nc.gpsimd

            def delta(what, i, l=0):
                if what == "gates":
                    if i == 0:
                        pool.wait_ge(masks_in_s, 16)
                        pool.wait_ge(g_s, 1)
                    else:
                        pool.wait_ge(dsum_s, i)
                        pool.wait_ge(xvx_s, upper(i - 1, LEVELS - 1))
                    for d, to in enumerate((gate_f, gate_b)):
                        for h in range(H):
                            last = G.tensor_scalar(to[:, h, :], incl[d], gate[:, ORDER[i], d * H + h:d * H + h + 1],
                                                   None, ALU.mult)
                    last.then_inc(gm_s, 1)
                if what == "turn" and l < LEVELS - 1:
                    if l == 0:
                        pool.wait_ge(xu_s, level(i, 0))
                        pool.wait_ge(p_s, i + 1)
                    else:
                        pool.wait_ge(xt_s, level(i, l))
                    G.tensor_tensor(z_t, inv_t[:, ORDER[i]], over_heads(tri[l + 1]), ALU.mult).then_inc(z_s, 1)
                if what == "tri":
                    n, d = i, l
                    slot, sign = slot_of(n, d), 1 - 2 * d
                    keep = dict(compare_op=ALU.is_ge, fill=0.0, base=0, pattern=[[0, H], [sign, P]],
                                channel_multiplier=-sign)
                    pool.wait_ge(xt_s, level(ORDER.index(chunk_of(n, d)), LEVELS - 1))
                    if (n, d) == (1, 1):
                        pool.wait_ge(xt_s, level(NC - 1, LEVELS - 1))
                    elif n > 1 or d == 1 or n == 1:
                        before = pair(0, 0) if n == 0 else pair(0, 1) if n == 1 else pair(n - 1, d)
                        pool.wait_ge(xr_s, before)
                        pool.wait_ge(in_s, before)
                    G.affine_select(out=tri_x[slot], in_=inv_t[:, chunk_of(n, d)], **keep).then_inc(trix_s, 1)
                    G.affine_select(out=tri_qk[slot], in_=qk[:, chunk_of(n, d)], **keep).then_inc(triqk_s, 1)

            for at in sorted(DELTA):
                for step in DELTA[at]:
                    delta(*step)

            for r in range(1, 4):
                for k in range(1, KD):
                    pool.wait_ge(sq_s, r * KD + k + 1)
                    if k > 1:
                        pool.wait_ge(acc_s, r * (KD - 1) + k - 1)
                    elif r > 1:
                        pool.wait_ge(sqsum_s, r)
                    G.tensor_tensor(acc, sq_t[:, 0, :] if k == 1 else acc, sq_t[:, k % SQ, :], ALU.add)\
                        .then_inc(acc_s, 1)


def _slabs(w, nk, width):
    rows, n = w.shape
    return w.reshape(nk, P, n // width, width).transpose(2, 1, 0, 3).reshape(n // width, P, nk * width)


def _features(a):
    return np.ascontiguousarray(a.T.reshape(-1, P, TOK).transpose(1, 0, 2))


def _masks():
    i = np.arange(P)
    row, col = i[:, None], i[None, :]
    m = np.stack([row == col, row <= col, row >= col, row > col, row < col, row >= 0 * col], axis=1)
    same = [row >> l == col >> l for l in range(LEVELS + 1)]
    levels = [same[l + 1] & ~same[l] for l in range(LEVELS)]
    for l in range(1, LEVELS):
        levels.append(same[l] & np.where(row >> l & 1, row <= col, row >= col))
    return m.astype(np.float32), np.stack(levels, axis=1)


def kernel(**inputs):
    import ml_dtypes
    import concourse.bacc as bacc
    from concourse.bass_utils import run_bass_kernel_spmd

    a = {n: np.asarray(v) for n, v in inputs.items()}
    w_in = a["w_in"][0]
    b_at, c_at, x_at, q_at, k_at, v_at, z_at = (512 * i for i in range(7))
    ga_at = z_at + 512 + 16
    gd_at = ga_at + D

    def part(at, n):
        return _slabs(w_in[:, at:at + n], KD, 256)

    bxc = [part(at + 256 * g, 256) for g in range(2) for at in (b_at, x_at, c_at)]
    ff = []
    w1, w2 = a["w_ff1"][0], a["w_ff2"][0]
    for g in range(FF_GROUPS):
        ff += [_slabs(w1[:, D * g:D * (g + 1)], KD, 256), _slabs(w2[D * g:D * (g + 1)], KD, 256)]
    stream = np.concatenate(
        [part(k_at, 512), part(q_at, 512), part(v_at, 512), *bxc,
         _slabs(a["w_a_out"][0], H, 512), part(ga_at, D), part(z_at, 512), part(gd_at, D),
         _slabs(a["w_dn_out"][0], H, 512), _slabs(a["w_o"][0], KD, 256), *ff,
         _slabs(a["w_ple_proj"][0], 2, 1024), _slabs(a["w_ple_gate"][0], KD, 256)])
    assert stream.shape == (N_SLABS, P, SLAB)

    cols = np.zeros((P, N_COLS), np.float32)

    def put(at, m):
        cols[:, at:at + m.shape[1]] = m

    put(C_GMIX, a["g_mix"][0].reshape(KD, P).T)
    put(C_GFFN, a["g_ffn"][0].reshape(KD, P).T)
    put(C_GPLE, a["g_ple"][0].reshape(KD, P).T)
    put(C_GFIN, a["g_final"].reshape(KD, P).T)
    put(C_CONVA, a["conv_a"][0].reshape(3 * H, P).T)
    put(C_CONVQ, a["conv_qkv"][0].reshape(3 * 3 * H, P).T)
    put(C_GDN, a["g_dn_norm"][0].reshape(1, P).T)
    for at, f, b in ((C_ALOG, "a_log_f", "a_log_b"), (C_DTB, "dt_bias_f", "dt_bias_b")):
        put(at, np.broadcast_to(a[f], (P, H)))
        put(at + H, np.broadcast_to(a[b], (P, H)))
    odd = np.arange(P)[:, None] >> np.arange(LEVELS) & 1
    put(C_PARITY, np.concatenate([1 - odd, odd], axis=1).astype(np.float32))
    put(C_W16, w_in[:, z_at + 512:ga_at].reshape(KD, P, 16).transpose(1, 0, 2).reshape(P, KD * 16))
    masks, levels = _masks()

    arrays = {"x_in_dram": _features(a["x"][0]), "p_in_dram": _features(a["p"][0, 0]), "stream": stream,
              "cols_in": cols, "masks_in": masks, "levels_in": levels.astype(ml_dtypes.bfloat16)}
    nc = bacc.Bacc("TRN2", target_bir_lowering=False, num_devices=1)
    args = [nc.dram_tensor(n, v.shape, mybir.dt.from_np(v.dtype), kind="ExternalInput").ap()
            for n, v in arrays.items()]
    args.append(nc.dram_tensor("out_t", (P, KD, TOK), F32, kind="ExternalOutput").ap())
    encoder_block(nc, *args)
    got = run_bass_kernel_spmd(nc, [arrays], core_ids=[0]).results[0]["out_t"]
    return np.asarray(got).transpose(2, 1, 0).reshape(1, TOK, D)
```

```python
from contextlib import ExitStack

import numpy as np

import concourse.bass as bass
from concourse import mybir

ALU = mybir.AluOpType
ACT = mybir.ActivationFunctionType
F32 = mybir.dt.float32
F32R = mybir.dt.float32r
BF16 = mybir.dt.bfloat16

P = 128
TOK = 512
D = 1024
KD = D // P
H = 4
NC = TOK // P
LEVELS = 7
EPS = 1e-6
DIRS = 2

SLAB = 2048
UNITS = 16
S_PP = 0
S_K, S_Q, S_V = 1, 3, 5
S_BXC = 7
S_WA = 13
S_GA = 15
S_Z = 19
S_GD = 21
S_WD = 25
S_WO = 27
S_FF = 31
FF_GROUPS = 4
FF_SLABS = 8
S_PG = S_FF + FF_GROUPS * FF_SLABS
N_SLABS = S_PG + 4
RING = 2
HI_PARTS, LO_PARTS = 2, 4
SQ = 3

C_GMIX, C_GFFN, C_GPLE, C_GFIN = 0, 8, 16, 24
C_CONVA = 32
C_CONVQ = C_CONVA + 12
C_GDN = C_CONVQ + 36
C_ALOG = C_GDN + 1
C_DTB = C_ALOG + 8
C_PARITY = C_DTB + 8
C_PICK = C_PARITY + 2 * LEVELS
C_W16 = C_PICK + H * H
N_COLS = C_W16 + KD * 16


def tiles_of(s):
    if s in (S_WA, S_WA + 1, S_WD, S_WD + 1):
        return 4
    return 8 if s == S_PP else 2


def first_tile(s):
    return sum(tiles_of(r) for r in range(s))


ORDER = [c for n in range(NC // 2) for c in (n, NC - 1 - n)]
DELTA = {}


def _put(unit, *what):
    DELTA.setdefault(unit, []).append(what)


INV0, INV_UNITS = 5 * UNITS + 4, 51
for _i in range(NC):
    _b = INV0 + _i * INV_UNITS
    _put(_b - 8, "gates", _i, 0)
    _put(_b - (3 if _i else 8), "gates", _i, 1)
    _put(_b, "decay", _i)
    _put(_b + 2, "kk", _i)
    _put(_b + 4, "make_k", _i)
    _put(_b + 4, "qk", _i)
    _put(_b + 6, "make_p", _i)
    _put(_b + 8, "turn", _i, 0)
    for _l in range(1, LEVELS):
        _v = _b + 6 + 6 * _l
        _put(_v, "ax", _i, _l)
        _put(_v + 3, "xax", _i, _l)
        _put(_v + 5, "turn", _i, _l)
_b = INV0 + 2 * INV_UNITS + 2
for _at, _what, _d in ((-1, "tri", 0), (0, "solve", 0), (5, "write", 0), (6, "tri", 1), (9, "solve", 1), (14, "write", 1)):
    _put(_b + _at, _what, 0, _d)
for _n in range(1, NC):
    _b = INV0 + NC * INV_UNITS + 1 + 13 * (_n - 1)
    for _at, _what, _d in ((0, "tri", 0), (0, "read", 0), (1, "tri", 1), (1, "read", 1), (3, "solve", 0), (5, "solve", 1),
                           (7, "write", 0), (9, "write", 1)):
        _put(_b + _at, _what, _n, _d)


def chunk_of(n, d):
    return n if d == 0 else NC - 1 - n


def pair(n, d):
    return DIRS * n + d + 1


HALF = TOK // 2
T_LAST = first_tile(N_SLABS - 1)


def chunks_of(r):
    return range(NC) if r < 3 else range(NC // 2 * (r - 3), NC // 2 * (r - 2))


def tokens_of(r):
    return slice(chunks_of(r)[0] * P, (chunks_of(r)[-1] + 1) * P)


def added(r, k):
    return sum(KD - 2 + (q in (1, 2)) for q in range(r)) + max(k, 1)


def level(i, l):
    return i * LEVELS + l + 1


def upper(i, l):
    return i * (LEVELS - 1) + l


def encoder_block(nc, x_t, p_t, stream, cols_in, masks_in, levels_in, out, ple_kept):
    with ExitStack() as ctx:
        def sb(name, shape, dt=F32):
            return ctx.enter_context(nc.sbuf_tensor(name, shape, dt))

        def sem(name):
            return ctx.enter_context(nc.semaphore(name))

        raw = sb("raw", [P, RING, SLAB])
        w_hi = sb("w_hi", [P, RING, SLAB], F32R)
        w_lo = sb("w_lo", [P, RING, SLAB], F32R)
        act_hi = sb("act_hi", [P, KD, TOK], F32R)
        act_lo = sb("act_lo", [P, KD, TOK], F32R)
        cols = sb("cols", [P, N_COLS])
        masks = sb("masks", [P, 6, P])
        lmask = sb("lmask", [P, 2 * LEVELS - 1, P], BF16)
        beta = sb("beta", [P, NC, DIRS * H])
        gate = sb("gate", [P, NC, DIRS * H])
        e_cols = sb("e_cols", [P, 3, DIRS, NC, H])
        neg_run = sb("neg_run", [P, DIRS, NC, H])
        c1 = sb("c1", [P, NC, DIRS, H])
        c1_end = sb("c1_end", [P, NC, DIRS, H])
        c_lvl = sb("c_lvl", [P, LEVELS, NC * H])
        k_cols = sb("k_cols", [P, 5, NC * H])
        k_sq = sb("k_sq", [P, NC * H])
        q_sq = sb("q_sq", [P, NC * H])
        o_sq = sb("o_sq", [P, NC * H])
        norm_t = sb("norm_t", [P, 6, NC * H])

        KB = 256
        arena_stack = ExitStack()
        arena = arena_stack.enter_context(nc.sbuf_tensor("arena", [P, 118 * KB], F32))

        def carve(start_kb, *shape):
            flat = arena[:, start_kb * KB:start_kb * KB + int(np.prod(shape))]
            names = " ".join(f"a{i}" for i in range(len(shape)))
            sizes = {f"a{i}": shape[i] for i in range(1, len(shape))}
            return flat.rearrange(f"p ({names}) -> p {names}", **sizes) if len(shape) > 1 else flat

        c_odd = carve(67, LEVELS, NC * H)
        x_in = carve(0, KD, TOK)
        n_f = carve(16, 4, TOK)
        sq_in = carve(24, SQ, TOK)
        acc0 = carve(30, TOK)
        tiny = carve(65, 6, NC * DIRS * H)
        ba = carve(66, NC, 16)
        p_in = carve(80, 2, TOK)
        ple_out = carve(70, 4, TOK), carve(90, 4, TOK)
        ba_t = carve(68, TOK)
        k_t = carve(0, H, TOK)
        q_t = carve(8, H, TOK)
        k_tok = carve(16, NC, H, P)
        v_tok = carve(24, NC, H, P)
        inv_t = carve(32, NC, H, P)
        qk = carve(40, NC, H, P)
        q_rows = carve(42, TOK)
        sq_q = carve(44, 2, TOK)
        sq_k = carve(48, NC, P)
        a_t = carve(48, H, P)
        z_t = carve(50, H, P)
        decay = carve(50, H, P)
        inv = carve(52, H, P)
        y = carve(54, H, P)
        ax = carve(56, H, P)
        gate_b = carve(56, H, P)
        gate_f = carve(58, H, P)
        tri_x = (carve(60, H, P), carve(48, H, P))
        tri_qk = (carve(62, H, P), carve(50, H, P))
        r_buf = carve(52, DIRS, H, P)
        w_buf = carve(64, DIRS, H, P)
        w_dec = carve(68, DIRS, H, P)
        state = carve(72, DIRS, H, P)
        sig_a = carve(76, TOK)
        v_t = carve(78, H, TOK)
        o_acc = carve(78, NC, H, P)
        conv_t = carve(86, 2, TOK)
        b_sb = carve(90, 2, TOK)
        bx = carve(94, 2, TOK)
        ya = carve(98, 2, TOK)
        mixed = carve(86, KD, TOK)
        z_silu = carve(110, H, TOK)
        sig_d = carve(0, KD, TOK)
        o_junk = carve(32, NC, P)
        yd_f = carve(56, 2, TOK)
        mg_f = carve(60, 2, TOK)
        h_t = carve(64, KD, TOK)
        relu_t = carve(80, 2, TOK)
        hid_f = carve(84, 2, TOK)
        rb = carve(88, TOK)
        acc = carve(90, TOK)
        sq_t = carve(92, SQ, TOK)
        ple = carve(32, KD, TOK)
        sig_p = carve(48, 2, TOK)
        arena_stack.close()
        f_hi = sb("f_hi", [P, KD, TOK], F32R)
        f_lo = sb("f_lo", [P, KD, TOK], F32R)
        hid_hi = sb("hid_hi", [P, 8, TOK], F32R)
        hid_lo = sb("hid_lo", [P, 8, TOK], F32R)
        w16_hi = sb("w16_hi", [P, KD * 16], F32R)
        w16_lo = sb("w16_lo", [P, KD * 16], F32R)
        sb("arena_rest", [P, 37 * KB])
        y_hi = sb("y_hi", [P, H, TOK], F32R)
        y_lo = sb("y_lo", [P, H, TOK], F32R)

        ident, incl_f, incl_b, strict_f, strict_b, ones = (masks[:, i, :] for i in range(6))
        off = [lmask[:, l, :] for l in range(LEVELS)]
        tri = [None] + [lmask[:, LEVELS + l, :] for l in range(LEVELS - 1)]
        incl = (incl_f, incl_b)
        strict = (strict_f, strict_b)

        dense = ctx.enter_context(nc.psum_tensor("dense", [P, 4, TOK], F32))
        extra = ctx.enter_context(nc.psum_tensor("extra", [P, 4, TOK], F32))

        cols_in_s, masks_in_s, levels_in_s = sem("cols_landed"), sem("masks_landed"), sem("levels_landed")
        x_in_s = [sem(f"x_landed{i}") for i in range(4)]
        x2_in_s, p_in_s, out_s = sem("x_again_landed"), sem("p_landed"), sem("out_stored")
        raw_s = [sem(f"raw_landed{i}") for i in range(RING)]
        hi_s, lo_s, tile_s = sem("w_hi_made"), sem("w_lo_made"), sem("tile_done")
        read_s = [sem(f"tile_read{i}") for i in range(4)]
        sq_s, acc_s, sqsum_s = sem("square_made"), sem("square_added"), sem("squares_summed")
        ms_s, root_s, col_s = sem("mean_made"), sem("root_made"), sem("rstd_made")
        rbps_s, rb_s = sem("rstd_spread"), sem("rstd_copied")
        nf_s, nhi_s, nlo_s, nlp_s = (sem("norm_made"), sem("norm_hi_made"), sem("norm_lo_made"),
                                     sem("norm_lo_made_by_pool"))
        w16h_s, w16l_s, ba_s, bat_s = sem("w16_hi_made"), sem("w16_lo_made"), sem("ba_done"), sem("ba_t_copied")
        batr_s, bac_s = sem("ba_transposed"), sem("ba_copied")
        beta_s, abs_s, exp_s, aexp_s = sem("beta_made"), sem("alpha_abs"), sem("alpha_exp"), sem("a_exp")
        g_s, gsum_s, ecol_s = sem("gate_made"), sem("gate_sums"), sem("decay_columns")
        ksq_s, kroot_s, qsq_s = sem("k_sq_made"), sem("k_root"), sem("q_sq_made")
        tap_s, silu_s, qsquare_s, ss_s, tr_s = (sem("centre_tap"), sem("silu_made"), sem("q_squared"),
                                             sem("q_summed"), sem("kv_transposed"))
        ksquare_s, qrow_s, qturn_s = sem("k_squared"), sem("q_rows_copied"), sem("q_rows_turned")
        kcopy_s, vcopy_s = sem("k_tok_made"), sem("v_tok_made")
        yd_s, yh_s, yl_s = sem("y_dn_made"), sem("y_hi_made"), sem("y_lo_made")
        sigau_s, mg_s = sem("gate_a_applied"), sem("merged")
        gm_s, gb_s, dsum_s, dexp_s = sem("gates_spread"), sem("gates_b_spread"), sem("decay_sums"), sem("decay_exp")
        kk_s, qk_s, p_s = sem("kk_done"), sem("qk_done"), sem("qk_decayed")
        v_s, vm_s, xvx_s, xu_s = sem("ax_done"), sem("ax_masked"), sem("xax_done"), sem("inverse_updated")
        turn_s, xt_s, z_s, y_s = sem("inverse_turned"), sem("turned_copied"), sem("z_made"), sem("y_made")
        trix_s, triqk_s = sem("x_half_made"), sem("qk_half_made")
        sread_s, r_s, qs_s = sem("state_read"), sem("r_made"), sem("qs_added")
        xr_s, w_s, wd_s = sem("solved"), sem("w_made"), sem("w_decayed")
        in_s, ds_s, oadd_s, st_s = sem("intra_done"), sem("ds_done"), sem("o_added"), sem("state_made")
        omean_s, oroot_s, onorm_s, otr_s = (sem("o_mean"), sem("o_root"), sem("o_normed"),
                                            sem("o_transposed"))
        hp_s = sem("ple_added")
        hh_s, hf_s, hl_s = sem("hid_hi_made"), sem("hid_squared"), sem("hid_lo_made")
        ph_s, pl_s, gp_s = sem("p_hi_made"), sem("p_lo_made"), sem("ple_gate")
        spill_s, ple_in_s = sem("ple_stored"), sem("ple_landed")
        gain_s, fin_s, finp_s = sem("final_gain"), sem("final_made"), sem("final_made_by_pool")
        dv_s = sem("vector_steps")
        ac_s = sem("scalar_steps")

        FF_T0 = first_tile(S_FF)
        assert FF_T0 % 4 == 0 and FF_SLABS % RING == 0

        def bank(u):
            return dense[:, u % 4, :]

        def split_view(t, s, nk=KD):
            return t[:, s % RING, :].rearrange("p (k n) -> p k n", k=nk)

        def conv_col(i, tap):
            at = C_CONVQ + tap * 3 * H + (i + H if i < H else i - H if i < 2 * H else i)
            return cols[:, at:at + 1]

        def over_heads(m):
            return m.unsqueeze(1).broadcast_to([P, H, P])

        def heads_of(flat):
            return flat.rearrange("p (h n) -> p h n", h=H)

        def part(t, slot, q, parts):
            return t[:, slot, q * SLAB // parts:(q + 1) * SLAB // parts]

        def scan_banks(n, d):
            return (0, 1) if n > 0 and d == 0 else (2, 3)

        def slot_of(n, d):
            return d if n > 0 else 0

        def wait_read(eng, u):
            eng.wait_ge(read_s[u % 4], u // 4 + 1)

        def tile_ends(s, j):
            nk = UNITS // tiles_of(s)
            return j // nk if j % nk == nk - 1 else None

        def spread_bank(r):
            return 2 if r == 4 else 0

        block = ctx.enter_context(nc.Block())

        @block.sync
        def _(sp):
            sp.dma_start(p_in, p_t).then_inc(p_in_s, 16)
            sp.dma_start(raw[:, 0, :], stream[0]).then_inc(raw_s[0], 16)
            for i in range(4):
                sp.dma_start(x_in[:, 2 * i:2 * i + 2, :], x_t[:, 2 * i:2 * i + 2, :]).then_inc(x_in_s[i], 16)
            sp.dma_start(masks[:], masks_in).then_inc(masks_in_s, 16)
            sp.dma_start(raw[:, 1, :], stream[1]).then_inc(raw_s[1], 16)
            sp.dma_start(cols[:], cols_in).then_inc(cols_in_s, 16)
            sp.dma_start(lmask[:], levels_in).then_inc(levels_in_s, 16)

            def slab_pair(i):
                for r in range(RING):
                    sp.wait_ge(lo_s, i * (RING * LO_PARTS) + LO_PARTS * (r + 1 - RING))
                    sp.dma_start(raw[:, r, :], stream[bass.ds(i * RING + r, 1)].rearrange("s p n -> p (s n)"))\
                      .then_inc(raw_s[r], 16)

            before_x = S_WD // RING + 1
            with sp.Fori(1, before_x) as i:
                slab_pair(i)
            sp.wait_ge(otr_s, H)
            sp.dma_start(h_t, x_t).then_inc(x2_in_s, 16)
            with sp.Fori(before_x, N_SLABS // RING) as i:
                slab_pair(i)
            for s in range(N_SLABS // RING * RING, N_SLABS):
                sp.wait_ge(lo_s, LO_PARTS * (s + 1 - RING))
                sp.dma_start(raw[:, s % RING, :], stream[s]).then_inc(raw_s[s % RING], 16)
            for half in range(2):
                t = slice(half * HALF, (half + 1) * HALF)
                for done, count, at, n in ((fin_s, 3, 0, 3), (finp_s, 1, 5, 1), (fin_s, 5, 3, 2), (finp_s, 3, 6, 2)):
                    sp.wait_ge(done, half * (5 if done is fin_s else 3) + count)
                    sp.dma_start(out[:, at:at + n, t], h_t[:, at:at + n, t]).then_inc(out_s, 16)
            sp.wait_ge(out_s, 16 * 8)
            sp.wait_ge(spill_s, 32)

        @block.tensor
        def _(pe):
            mm = nc.tensor.matmul

            def three(o, wh, wl, ah, al, first, last):
                mm(o, wh, ah, start=first, stop=False)
                mm(o, wh, al, start=False, stop=False)
                return mm(o, wl, ah, start=False, stop=last)

            def unit(s, j, src):
                nk = UNITS // tiles_of(s)
                m, k = divmod(j, nk)
                wh, wl = split_view(w_hi, s, nk), split_view(w_lo, s, nk)
                if j == 0:
                    pe.wait_ge(hi_s, HI_PARTS * (s + 1))
                    pe.wait_ge(lo_s, LO_PARTS * (s + 1))
                u = first_tile(s) + m
                if k == 0 and u >= 4:
                    pe.wait_ge(read_s[u % 4], u // 4)
                ah, al = src
                last = three(bank(u), wh[:, k, m * P:(m + 1) * P], wl[:, k, m * P:(m + 1) * P],
                             ah[:, k, :], al[:, k, :], k == 0, k == nk - 1)
                if k == nk - 1:
                    last.then_inc(tile_s, 1)

            def norm_total(r, a, sq):
                alone = [] if r in (1, 2) else [KD - 1] if r == 0 else [KD - 2, KD - 1]
                pe.wait_ge(acc_s, added(min(r, 3), KD - 1 - len(alone)))
                for c in chunks_of(r):
                    ins = mm(extra[:, c, 0:1], a[:, c * P:(c + 1) * P], ones[:, 0:1], start=True, stop=not alone)
                if alone:
                    pe.wait_ge(sq_s, (r + 1) * KD if r == 0 else 4 * KD + 2 * (r - 3))
                for k in alone:
                    for c in chunks_of(r):
                        ins = mm(extra[:, c, 0:1], sq[:, k % SQ, c * P:(c + 1) * P], ones[:, 0:1],
                                 start=False, stop=k == alone[-1])
                ins.then_inc(sqsum_s, 1)

            def norm_spread(r):
                pe.wait_ge(col_s, r + 1)
                for c in chunks_of(r):
                    last = mm(extra[:, spread_bank(r), c * P:(c + 1) * P],
                              norm_t[:, 3, c:c + 1].broadcast_to([P, P]), ident, start=True, stop=True)
                last.then_inc(rbps_s, 1)

            def small_projection():
                pe.wait_ge(w16h_s, 1)
                pe.wait_ge(w16l_s, 1)
                wh = w16_hi[:].rearrange("p (k n) -> p k n", k=KD)
                wl = w16_lo[:].rearrange("p (k n) -> p k n", k=KD)
                for k in range(KD):
                    last = three(extra[0:16, 1, :], wh[:, k, :], wl[:, k, :], act_hi[:, k, :], act_lo[:, k, :],
                                 k == 0, k == KD - 1)
                last.then_inc(ba_s, 1)

            def turn_projection():
                pe.wait_ge(bat_s, 1)
                for c in range(NC):
                    last = nc.tensor.transpose(extra[:, 1, 16 * c:16 * c + 16], ba_t[0:16, c * P:(c + 1) * P],
                                               ident[0:16, 0:16])
                last.then_inc(batr_s, 1)

            def gate_sums():
                pe.wait_ge(g_s, 1)
                for q, lhs in enumerate((incl, strict, (ones, ones))):
                    for d in range(DIRS):
                        at = (q * DIRS + d) * NC * H
                        last = mm(extra[:, 1, at:at + NC * H].rearrange("p (c h) -> p c h", c=NC),
                                  lhs[d], gate[:, :, d * H:(d + 1) * H], start=True, stop=True)
                last.then_inc(gsum_s, 1)

            def square_sums(h):
                if h == 0:
                    pe.wait_ge(kcopy_s, 4)
                pe.wait_ge(qsquare_s, h + 1)
                mm(extra[0:H, 3, :], cols[:, C_PICK + H * h:C_PICK + H * (h + 1)], sq_q[:, h % 2, :],
                   start=h == 0, stop=h == H - 1).then_inc(ss_s, 1)

            def turn_squares():
                pe.wait_ge(qrow_s, 1)
                for c in range(NC):
                    last = nc.tensor.transpose(extra[:, 3, c * H:(c + 1) * H], q_rows[0:H, c * P:(c + 1) * P],
                                               ident[0:H, 0:H])
                last.then_inc(qturn_s, 1)

            def to_tokens(i, src, h):
                pe.wait_ge(silu_s, i + 1 if i < H else i + H + 1)
                if i == 5:
                    pe.wait_ge(qsq_s, 1)
                elif i == 4:
                    pe.wait_ge(kcopy_s, 3)
                elif 2 <= i < H:
                    pe.wait_ge(kcopy_s, i - 1)
                elif i > 5:
                    pe.wait_ge(vcopy_s, i - 5)
                for c in range(NC):
                    last = nc.tensor.transpose(extra[:, 2 + i % 2, c * P:(c + 1) * P],
                                               src[:, h, c * P:(c + 1) * P], ident)
                last.then_inc(tr_s, 1)

            def qkv_aux(i):
                h = i % H
                if i < H:
                    to_tokens(i, k_t, h)
                elif i < 2 * H:
                    square_sums(h)
                else:
                    to_tokens(i - H, v_t, h)

            def heads(o, lhs, rhs):
                for h in range(H):
                    last = mm(o[:, h * P:(h + 1) * P], lhs(h), rhs(h), start=True, stop=True)
                return last

            def decay_sums(i):
                pe.wait_ge(gm_s, i + 1)
                pe.wait_ge(gb_s, i + 1)
                if i == 0:
                    pe.wait_ge(nf_s, KD)
                else:
                    pe.wait_ge(vm_s, upper(i - 1, LEVELS - 1))
                mm(extra[:, 0, :], strict[0], gate_f.rearrange("p h n -> p (h n)"), start=True, stop=False)
                mm(extra[:, 0, :], strict[1], gate_b.rearrange("p h n -> p (h n)"), start=False, stop=True)\
                    .then_inc(dsum_s, 1)

            def products(i, which):
                t = slice(ORDER[i] * P, (ORDER[i] + 1) * P)
                if which == 0:
                    if i == 0:
                        pe.wait_ge(ecol_s, 1)
                        pe.wait_ge(silu_s, H)
                    else:
                        pe.wait_ge(xt_s, level(i - 1, LEVELS - 1))
                    heads(extra[:, 1, :], lambda h: k_t[:, h, t], lambda h: k_t[:, h, t]).then_inc(kk_s, 1)
                else:
                    pe.wait_ge(dexp_s, i + 1)
                    if i == 0:
                        pe.wait_ge(silu_s, 2 * H)
                    heads(extra[:, 0, :], lambda h: k_t[:, h, t], lambda h: q_t[:, h, t]).then_inc(qk_s, 1)

            def level_ax(i, l):
                pe.wait_ge(y_s, upper(i, l))
                if l == 1:
                    pe.wait_ge(p_s, i + 1)
                else:
                    pe.wait_ge(vm_s, upper(i, l - 1))
                heads(extra[:, 0, :], lambda h: a_t[:, h, :], lambda h: y[:, h, :]).then_inc(v_s, 1)

            def level_xax(i, l):
                pe.wait_ge(vm_s, upper(i, l))
                pe.wait_ge(z_s, upper(i, l))
                pe.wait_ge(xt_s, level(i, l - 1))
                heads(extra[:, 1, :], lambda h: z_t[:, h, :], lambda h: ax[:, h, :]).then_inc(xvx_s, 1)

            def turn(i, l):
                pe.wait_ge(xu_s, level(i, l))
                src = inv_t[:, ORDER[i]] if l == 0 else inv
                for h in range(H):
                    last = nc.tensor.transpose(extra[:, 1, h * P:(h + 1) * P], src[:, h, :], ident)
                last.then_inc(turn_s, 1)

            def scan_read(n, d):
                t = slice(chunk_of(n, d) * P, (chunk_of(n, d) + 1) * P)
                b_r, b_o = scan_banks(n, d)
                pe.wait_ge(st_s, pair(n - 1, d))
                pe.wait_ge(oadd_s, pair(n - 1, d))
                if (n, d) == (1, 0):
                    pe.wait_ge(xt_s, level(NC - 1, LEVELS - 1))
                heads(extra[:, b_r, :], lambda h: k_t[:, h, t], lambda h: state[:, d, h, :])
                heads(extra[:, b_o, :], lambda h: q_t[:, h, t], lambda h: state[:, d, h, :]).then_inc(sread_s, 1)

            def scan_solve(n, d):
                pe.wait_ge(trix_s, pair(n, d))
                if n > 0:
                    pe.wait_ge(r_s, pair(n - 1, d))
                elif d == 0:
                    pe.wait_ge(vcopy_s, 4)
                else:
                    pe.wait_ge(st_s, pair(0, 0))
                heads(extra[:, scan_banks(n, d)[0], :], lambda h: tri_x[slot_of(n, d)][:, h, :],
                      lambda h: r_buf[:, d, h, :] if n > 0 else v_tok[:, chunk_of(n, d), h, :]).then_inc(xr_s, 1)

            def scan_write(n, d):
                b_r, b_o = scan_banks(n, d)
                pe.wait_ge(w_s, pair(n, d))
                pe.wait_ge(triqk_s, pair(n, d))
                if n > 0:
                    pe.wait_ge(qs_s, pair(n - 1, d))
                elif d == 1:
                    pe.wait_ge(oadd_s, pair(0, 0))
                heads(extra[:, b_o, :], lambda h: tri_qk[slot_of(n, d)][:, h, :], lambda h: w_buf[:, d, h, :])\
                    .then_inc(in_s, 1)
                if n < NC - 1:
                    pe.wait_ge(wd_s, pair(n, d))
                    heads(extra[:, b_r, :], lambda h: k_tok[:, chunk_of(n, d), h, :], lambda h: w_dec[:, d, h, :])\
                        .then_inc(ds_s, 1)

            def delta(what, *at):
                if what in ("decay", "kk", "qk", "ax", "xax", "turn", "read", "solve", "write"):
                    {"decay": decay_sums, "kk": lambda i: products(i, 0), "qk": lambda i: products(i, 1),
                     "ax": level_ax, "xax": level_xax, "turn": turn, "read": scan_read, "solve": scan_solve,
                     "write": scan_write}[what](*at)

            n_src, y_src, f_src, hid_src = (act_hi, act_lo), (y_hi, y_lo), (f_hi, f_lo), (hid_hi, hid_lo)
            for k in range(2):
                pe.wait_ge(ph_s, k + 1)
                pe.wait_ge(pl_s, k + 1)
            for j in range(UNITS):
                unit(S_PP, j, y_src)
                if j == 5:
                    pe.wait_ge(masks_in_s, 16)
                    norm_total(0, acc0, sq_in)
                if j == 8:
                    norm_spread(0)
            for s in range(S_K, S_FF):
                for j in range(UNITS):
                    if s == S_K and j < KD:
                        pe.wait_ge(nhi_s, j + 1)
                        pe.wait_ge(nlp_s if j % 2 else nlo_s, j // 2 + 1)
                    if s == S_WA and j < H:
                        pe.wait_ge(yh_s, j + 1)
                        pe.wait_ge(yl_s, j + 1)
                    if s == S_WD and j < H:
                        pe.wait_ge(yh_s, H + j + 1)
                        pe.wait_ge(yl_s, H + j + 1)
                    if s == S_WO and j < KD:
                        pe.wait_ge(nhi_s, KD + j + 1)
                        pe.wait_ge(nlo_s, KD // 2 + j + 1)
                    unit(s, j, y_src if tiles_of(s) == 4 else n_src)
                    if (s, j) == (1, UNITS - 1):
                        small_projection()
                    if (s, j) == (2, 1):
                        turn_projection()
                    if S_K < s <= S_BXC and j in (4, 12):
                        qkv_aux(2 * (s - S_K - 1) + (j == 12))
                    if (s, j) == (4, 8):
                        gate_sums()
                    if (s, j) == (6, 2):
                        turn_squares()
                    for step in DELTA.get(s * UNITS + j, ()):
                        delta(*step)
                    if (s, j) == (23, 6):
                        pe.wait_ge(onorm_s, 1)
                        for h in range(H):
                            for c in range(NC):
                                last = nc.tensor.transpose(extra[:, h, c * P:(c + 1) * P], o_acc[:, c, h, :], ident)
                            last.then_inc(otr_s, 1)

            def ff_group(i, first):
                for b in range(FF_SLABS):
                    pe.wait_ge(hi_s, i * (HI_PARTS * FF_SLABS) + HI_PARTS * (S_FF + b + 1))
                    pe.wait_ge(lo_s, i * (LO_PARTS * FF_SLABS) + LO_PARTS * (S_FF + b + 1))
                    wh, wl = split_view(w_hi, S_FF + b), split_view(w_lo, S_FF + b)
                    ah, al = f_src if b < FF_SLABS // 2 else hid_src
                    for m in range(2):
                        u = 2 * b + m
                        pe.wait_ge(read_s[u % 4], i * 4 + (FF_T0 + u) // 4)
                        for k in range(KD):
                            if first and u == 0:
                                pe.wait_ge(nhi_s, 2 * KD + k + 1)
                                pe.wait_ge(nlo_s, KD // 2 + KD + k + 1)
                            if u == FF_SLABS:
                                pe.wait_ge(hh_s, i * 8 + (k + 1))
                                pe.wait_ge(hl_s, i * 8 + (k + 1))
                            last = three(bank(u), wh[:, k, m * P:(m + 1) * P], wl[:, k, m * P:(m + 1) * P],
                                         ah[:, k, :], al[:, k, :], k == 0, k == KD - 1)
                        last.then_inc(tile_s, 1)
                        if first and u == 0:
                            norm_total(1, acc, sq_t)
                        if first and u == 1:
                            norm_spread(1)

            ff_group(0, True)
            with pe.Fori(1, FF_GROUPS) as i:
                ff_group(i, False)

            for s in range(S_PG, N_SLABS - 1):
                for j in range(UNITS):
                    if s == S_PG and j < KD:
                        pe.wait_ge(nhi_s, 3 * KD + j + 1)
                        pe.wait_ge(nlo_s, KD // 2 + 2 * KD + j + 1)
                    unit(s, j, n_src)
                    if (s, j) == (S_PG, 7):
                        norm_total(2, acc, sq_t)
                    if (s, j) == (S_PG, 12):
                        norm_spread(2)
            for q in range(4):
                half, m = divmod(q, 2)
                u = T_LAST + q
                t = slice(half * HALF, (half + 1) * HALF)
                if q == 0:
                    pe.wait_ge(hi_s, HI_PARTS * N_SLABS)
                    pe.wait_ge(lo_s, LO_PARTS * N_SLABS)
                pe.wait_ge(read_s[u % 4], u // 4)
                for k in range(KD):
                    wh, wl = split_view(w_hi, N_SLABS - 1), split_view(w_lo, N_SLABS - 1)
                    last = three(bank(u)[:, 0:HALF], wh[:, k, m * P:(m + 1) * P], wl[:, k, m * P:(m + 1) * P],
                                 act_hi[:, k, t], act_lo[:, k, t], k == 0, k == KD - 1)
                    if (q, k) == (3, KD - 2):
                        norm_spread(3)
                last.then_inc(tile_s, 1)
                if q == 2:
                    norm_total(3, acc, sq_t)
            norm_total(4, acc, sq_t)
            norm_spread(4)

        @block.scalar
        def _(act):
            A = nc.scalar.activation

            def split_hi(s, q):
                if q == 0:
                    act.wait_ge(raw_s[s % RING], 16 * (s // RING + 1))
                    if s >= RING:
                        act.wait_ge(tile_s, first_tile(s - RING + 1))
                A(part(w_hi, s % RING, q, HI_PARTS), part(raw, s % RING, q, HI_PARTS), ACT.Copy).then_inc(hi_s, 1)

            def square(r, k, sq, src):
                if k >= SQ:
                    act.wait_ge(acc_s, added(r, k - SQ))
                elif r > 1:
                    act.wait_ge(sqsum_s, r)
                A(sq[:, k % SQ, :], src, ACT.Square).then_inc(sq_s, 1)

            def norm_root(r):
                act.wait_ge(ms_s, r + 1)
                at = slice(chunks_of(r)[0], chunks_of(r)[-1] + 1)
                A(norm_t[:, 1, at], norm_t[:, 0, at], ACT.Sqrt).then_inc(root_s, 1)

            def norm_copy(r):
                act.wait_ge(rbps_s, r + 1)
                A(rb[:, tokens_of(r)], extra[:, spread_bank(r), tokens_of(r)], ACT.Copy).then_inc(rb_s, 1)

            def qkv_tile(i):
                u = first_tile(S_K) + i
                act.wait_ge(tile_s, u + 1)
                A(conv_t[:, i % 2, :], bank(u), ACT.Copy, scale=conv_col(i, 1)).then_inc(tap_s, 1)
                wait_read(act, u)
                to = (k_t, q_t, v_t)[i // H][:, i % H, :]
                A(to, conv_t[:, i % 2, :], ACT.Silu).then_inc(silu_s, 1)
                if H <= i < 2 * H:
                    h = i - H
                    act.wait_ge(silu_s, i + 1)
                    if h > 1:
                        act.wait_ge(ss_s, h - 1)
                    A(sq_q[:, h % 2, :], to, ACT.Square).then_inc(qsquare_s, 1)

            def delta(what, i, l=0):
                if what == "gates" and l == 1:
                    if i == 0:
                        act.wait_ge(g_s, 1)
                    else:
                        act.wait_ge(xvx_s, upper(i - 1, LEVELS - 1))
                    for h in range(H):
                        last = A(gate_b[:, h, :], incl[1], ACT.Copy, scale=gate[:, ORDER[i], H + h:H + h + 1])
                    last.then_inc(gb_s, 1)
                if what == "decay":
                    if i == 0:
                        act.wait_ge(gsum_s, 1)
                        A(e_cols[:].rearrange("p q d c h -> p (q d c h)"), extra[:, 1, 0:3 * DIRS * NC * H], ACT.Exp)\
                            .then_inc(ecol_s, 1)
                    act.wait_ge(dsum_s, i + 1)
                    if i > 0:
                        act.wait_ge(xvx_s, upper(i - 1, LEVELS - 1))
                    A(decay.rearrange("p h n -> p (h n)"), extra[:, 0, :], ACT.Exp).then_inc(dexp_s, 1)
                if what == "turn":
                    act.wait_ge(turn_s, level(i, l))
                    to = inv if l == 0 else inv_t[:, ORDER[i]]
                    A(to.rearrange("p h n -> p (h n)"), extra[:, 1, :], ACT.Copy).then_inc(xt_s, 1)
                if what == "solve":
                    n, d = i, l
                    act.wait_ge(xr_s, pair(n, d))
                    if n > 0:
                        act.wait_ge(in_s, pair(n - 1, d))
                        act.wait_ge(ds_s, pair(n - 1, d))
                    for to, by, done in ((w_buf, c1, w_s), (w_dec, c1_end, wd_s)):
                        if done is wd_s and n == NC - 1:
                            continue
                        for h in range(H):
                            last = A(to[:, d, h, :], extra[:, scan_banks(n, d)[0], h * P:(h + 1) * P], ACT.Copy,
                                     scale=by[:, chunk_of(n, d), d, h:h + 1])
                        last.then_inc(done, 1)

            def finish_tile(s, m):
                u = first_tile(s) + m
                if s < S_BXC:
                    qkv_tile(u - first_tile(S_K))
                elif s < S_WA and (s - S_BXC) % 3 == 0:
                    act.wait_ge(tile_s, u + 1)
                    if s > S_BXC:
                        wait_read(act, first_tile(S_BXC + 1) + m)
                    elif m == 0:
                        act.wait_ge(spill_s, 32)
                    A(b_sb[:, m, :], bank(u), ACT.Copy).then_inc(read_s[u % 4], 1)
                elif s < S_WA and (s - S_BXC) % 3 == 2:
                    i = 2 * ((s - S_BXC) // 3) + m
                    wait_read(act, u)
                    A(y_hi[:, i, :], ya[:, m, :], ACT.Copy).then_inc(yh_s, 1)
                elif S_WA <= s < S_GA:
                    act.wait_ge(tile_s, u + 1)
                    if s == S_WA and m == 0:
                        act.wait_ge(yl_s, H)
                    A(mixed[:, u - first_tile(S_WA), :], bank(u), ACT.Copy).then_inc(read_s[u % 4], 1)
                elif S_GA <= s < S_Z:
                    i = u - first_tile(S_GA)
                    act.wait_ge(tile_s, u + 1)
                    if i > 0:
                        act.wait_ge(sigau_s, i)
                    A(sig_a, bank(u), ACT.Sigmoid).then_inc(read_s[u % 4], 1)
                elif S_Z <= s < S_GD:
                    act.wait_ge(tile_s, u + 1)
                    A(z_silu[:, u - first_tile(S_Z), :], bank(u), ACT.Silu).then_inc(read_s[u % 4], 1)
                elif S_GD <= s < S_WD:
                    act.wait_ge(tile_s, u + 1)
                    if s == S_GD and m == 0:
                        act.wait_ge(sread_s, pair(NC - 2, 1))
                    A(sig_d[:, u - first_tile(S_GD), :], bank(u), ACT.Sigmoid).then_inc(read_s[u % 4], 1)
                elif S_WD <= s < S_WO:
                    i = u - first_tile(S_WD)
                    act.wait_ge(mg_s, i + 1)
                    act.wait_ge(tile_s, first_tile(S_WD))
                    A(act_hi[:, i, :], mg_f[:, i % 2, :], ACT.Copy).then_inc(nhi_s, 1)
                elif S_WO <= s < S_FF:
                    i = u - first_tile(S_WO)
                    wait_read(act, u)
                    A(f_hi[:, i, :], h_t[:, i, :], ACT.Copy, scale=cols[:, C_GFFN + i:C_GFFN + i + 1])\
                        .then_inc(nhi_s, 1)
                    square(1, i, sq_t, h_t[:, i, :])

            act.wait_ge(p_in_s, 16)
            for k in range(2):
                A(y_hi[:, k, :], p_in[:, k, :], ACT.Copy).then_inc(ph_s, 1)
            A(norm_t[:, 1, 0:NC], p_in[:, 0, 0:NC], ACT.Square).then_inc(ac_s, 1)
            act.wait_ge(ac_s, 1)
            A(norm_t[:, 2, 0:NC], norm_t[:, 1, 0:NC], ACT.Sqrt).then_inc(ac_s, 1)
            for q in range(HI_PARTS):
                split_hi(S_PP, q)
            for k in range(KD):
                act.wait_ge(x_in_s[k // 2], 16)
                square(0, k, sq_in, x_in[:, k, :])

            def keep(k):
                act.wait_ge(tile_s, k + 1)
                A(ple_out[k // 4][:, k % 4, :], bank(k), ACT.Copy).then_inc(read_s[k % 4], 1)
                if k % 4 == 3:
                    for u in range(k - 3, k + 1):
                        wait_read(act, u)
                    act.dma_start(ple_kept[:, k - 3:k + 1, :], ple_out[k // 4]).then_inc(spill_s, 16)

            keep(0)
            keep(1)
            for q in range(HI_PARTS):
                split_hi(S_K, q)
            norm_root(0)
            keep(2)
            keep(3)
            for k in range(KD):
                act.wait_ge(nf_s, k + 1)
                A(act_hi[:, k, :], n_f[:, k % 4, :], ACT.Copy).then_inc(nhi_s, 1)
                if k < 4:
                    keep(4 + k)
            act.wait_ge(cols_in_s, 16)
            A(w16_hi[:], cols[:, C_W16:C_W16 + KD * 16], ACT.Copy).then_inc(w16h_s, 1)

            for s in range(S_K, S_FF):
                for j in range(UNITS):
                    if j in (0, 3):
                        split_hi(s + 1, j // 3)
                    m = tile_ends(s, j)
                    if m is not None:
                        finish_tile(s, m)
                    if (s, j) == (2, 3):
                        act.wait_ge(bac_s, 1)
                        A(beta[:], ba[:, :, 0:8], ACT.Sigmoid).then_inc(beta_s, 1)
                        A(tiny[:, 5, 0:8], cols[:, C_ALOG:C_ALOG + 8], ACT.Exp).then_inc(aexp_s, 1)
                        act.wait_ge(abs_s, 1)
                        A(tiny[:, 1, :], tiny[:, 0, :], ACT.Exp, scale=-1.0).then_inc(exp_s, 1)
                    if 2 <= s <= 3 and j in (4, 12):
                        i = 2 * (s - 2) + (j == 12)
                        act.wait_ge(tr_s, i + 1)
                        A(k_tok[:, :, i, :], extra[:, 2 + i % 2, :].rearrange("p (c n) -> p c n", c=NC), ACT.Copy)\
                            .then_inc(kcopy_s, 1)
                        act.wait_ge(kcopy_s, i + 1)
                        for c in range(NC):
                            if i > 0:
                                act.wait_ge(ksquare_s, (i - 1) * NC + c + 1)
                            A(sq_k[:, c, :], k_tok[:, c, i, :], ACT.Square,
                              accum_out=k_sq[:, c * H + i:c * H + i + 1]).then_inc(ksquare_s, 1)
                    if (s, j) == (3, 13):
                        act.wait_ge(ksq_s, 1)
                        A(k_cols[:, 1, :], k_cols[:, 0, :], ACT.Sqrt).then_inc(kroot_s, 1)
                    for step in DELTA.get(s * UNITS + j, ()):
                        delta(*step)
                    if (s, j) == (21, 10):
                        act.wait_ge(oadd_s, pair(NC - 1, 1))
                        for c in range(NC):
                            for h in range(H):
                                if c > 0:
                                    act.wait_ge(ac_s, (c - 1) * H + h + 3)
                                last = A(o_junk[:, h, :], o_acc[:, c, h, :], ACT.Square,
                                         accum_out=o_sq[:, c * H + h:c * H + h + 1])
                                last.then_inc(ac_s, 1)
                    if (s, j) == (22, 3):
                        act.wait_ge(omean_s, 1)
                        A(norm_t[:, 1, :], norm_t[:, 0, :], ACT.Sqrt).then_inc(oroot_s, 1)
                    if (s, j) == (23, 10):
                        for h in range(H):
                            act.wait_ge(yd_s, h + 1)
                            A(y_hi[:, h, :], yd_f[:, h % 2, :], ACT.Copy).then_inc(yh_s, 1)

            def ff_group(i, first, last):
                for b in range(FF_SLABS):
                    r = (S_FF + b + 1) % RING
                    act.wait_ge(raw_s[r], i * (16 * FF_SLABS // RING) + 16 * ((S_FF + b + 1) // RING + 1))
                    act.wait_ge(tile_s, i * 16 + (FF_T0 + 2 * b))
                    for q in range(HI_PARTS):
                        A(part(w_hi, r, q, HI_PARTS), part(raw, r, q, HI_PARTS), ACT.Copy).then_inc(hi_s, 1)
                    if first and b == 0:
                        norm_root(1)
                        norm_copy(1)
                    if b < FF_SLABS // 2:
                        for m in range(2):
                            u = 2 * b + m
                            act.wait_ge(read_s[u % 4], i * 4 + ((FF_T0 + u) // 4 + 1))
                            if not first:
                                act.wait_ge(tile_s, i * 16 + FF_T0)
                            A(hid_hi[:, 2 * b + m, :], relu_t[:, m, :], ACT.Square).then_inc(hh_s, 1)
                            if not first or b > 0:
                                act.wait_ge(hl_s, i * 8 + (2 * b + m - 1))
                            A(hid_f[:, m, :], relu_t[:, m, :], ACT.Square).then_inc(hf_s, 1)
                    elif last:
                        for m in range(2):
                            u = 2 * b + m
                            k = u - 8
                            act.wait_ge(read_s[u % 4], i * 4 + ((FF_T0 + u) // 4 + 1))
                            A(act_hi[:, k, :], h_t[:, k, :], ACT.Copy, scale=cols[:, C_GPLE + k:C_GPLE + k + 1])\
                                .then_inc(nhi_s, 1)
                            square(2, k, sq_t, h_t[:, k, :])

            ff_group(0, True, False)
            with act.Fori(1, FF_GROUPS - 1) as i:
                ff_group(i, False, False)
            ff_group(FF_GROUPS - 1, False, True)

            act.wait_ge(tile_s, first_tile(S_PG))
            act.wait_ge(spill_s, 32)
            act.dma_start(ple, ple_kept).then_inc(ple_in_s, 16)
            norm_root(2)
            for q in range(HI_PARTS):
                split_hi(S_PG + 1, q)
            norm_copy(2)
            for s in range(S_PG, N_SLABS - 1):
                if S_PG < s:
                    for q in range(HI_PARTS):
                        split_hi(s + 1, q)
                for m in range(2):
                    i = 2 * (s - S_PG) + m
                    wait_read(act, first_tile(s) + m)
                    A(sig_p[:, m, :], sig_p[:, m, :], ACT.Sigmoid).then_inc(gp_s, 1)
                    act.wait_ge(hp_s, i + 1)
                    square(3, i, sq_t, h_t[:, i, :])
            def gain(k, t):
                A(h_t[:, k, t], h_t[:, k, t], ACT.Copy, scale=cols[:, C_GFIN + k:C_GFIN + k + 1]).then_inc(gain_s, 1)

            act.wait_ge(sq_s, 4 * KD - 2)
            gain(5, slice(0, TOK))
            for q in range(4):
                half, m = divmod(q, 2)
                t = slice(half * HALF, (half + 1) * HALF)
                wait_read(act, T_LAST + q)
                A(sig_p[:, m, t], sig_p[:, m, t], ACT.Sigmoid).then_inc(gp_s, 1)
                act.wait_ge(hp_s, KD - 2 + q + 1)
                act.wait_ge(acc_s, added(3, KD - 2 + m - SQ))
                A(sq_t[:, (KD - 2 + m) % SQ, t], h_t[:, KD - 2 + m, t], ACT.Square).then_inc(sq_s, 1)
                if q == 1:
                    norm_root(3)
                    act.wait_ge(sq_s, 4 * KD)
                    gain(6, t)
                    gain(7, t)
            norm_copy(3)
            norm_root(4)
            act.wait_ge(sq_s, 4 * KD + 2)
            gain(6, t)
            gain(7, t)
            norm_copy(4)

        @block.vector
        def _(dve):
            V = nc.vector
            steps = [0]

            def link(ins):
                steps[0] += 1
                ins.then_inc(dv_s, 1)
                dve.wait_ge(dv_s, steps[0])

            def split_lo(s, q):
                dve.wait_ge(hi_s, HI_PARTS * s + q * HI_PARTS // LO_PARTS + 1)
                V.tensor_tensor(part(w_lo, s % RING, q, LO_PARTS), part(raw, s % RING, q, LO_PARTS),
                                part(w_hi, s % RING, q, LO_PARTS).bitcast(F32), ALU.subtract).then_inc(lo_s, 1)

            def rsqrt_steps(x, root, t, to):
                link(V.reciprocal(root, root))
                link(V.tensor_tensor(t, root, root, ALU.mult))
                link(V.scalar_tensor_tensor(t, t, -0.5, x, ALU.mult, ALU.mult))
                return V.scalar_tensor_tensor(to, t, 1.5, root, ALU.add, ALU.mult)

            def norm_rstd(r):
                dve.wait_ge(sqsum_s, r + 1)
                at = slice(chunks_of(r)[0], chunks_of(r)[-1] + 1)
                x, root, t, to = (norm_t[:, i, at] for i in range(4))
                V.tensor_scalar(x, extra[:, at, 0:1].rearrange("p c o -> p (c o)"), 1.0 / D, EPS,
                                ALU.mult, ALU.add).then_inc(ms_s, 1)
                dve.wait_ge(root_s, r + 1)
                rsqrt_steps(x, root, t, to).then_inc(col_s, 1)

            def qkv_tile(i):
                u = first_tile(S_K) + i
                dve.wait_ge(tap_s, i + 1)
                c = conv_t[:, i % 2, :]
                link(V.scalar_tensor_tensor(c[:, 1:TOK], bank(u)[:, 0:TOK - 1], conv_col(i, 0), c[:, 1:TOK],
                                            ALU.mult, ALU.add))
                V.scalar_tensor_tensor(c[:, 0:TOK - 1], bank(u)[:, 1:TOK], conv_col(i, 2), c[:, 0:TOK - 1],
                                       ALU.mult, ALU.add).then_inc(read_s[u % 4], 1)

            def merged_lo(i):
                dve.wait_ge(nhi_s, KD + i + 1)
                V.tensor_tensor(act_lo[:, i, :], mg_f[:, i % 2, :], act_hi[:, i, :].bitcast(F32), ALU.subtract)\
                    .then_inc(nlo_s, 1)

            def finish_tile(s, m):
                u = first_tile(s) + m
                if s < S_BXC:
                    qkv_tile(u - first_tile(S_K))
                elif s < S_WA:
                    g, what = divmod(s - S_BXC, 3)
                    i = 2 * g + m
                    if what == 1:
                        dve.wait_ge(tile_s, u + 1)
                        wait_read(dve, first_tile(s - 1) + m)
                        V.tensor_tensor(bx[:, m, :], b_sb[:, m, :], bank(u), ALU.mult).then_inc(read_s[u % 4], 1)
                        wait_read(dve, u)
                        if g:
                            dve.wait_ge(yh_s, m + 1)
                            dve.wait_ge(yl_s, m + 1)
                        taps = [cols[:, C_CONVA + 4 * q + i:C_CONVA + 4 * q + i + 1] for q in range(3)]
                        y = ya[:, m, :]
                        link(V.tensor_scalar(y, bx[:, m, :], taps[1], None, ALU.mult))
                        link(V.scalar_tensor_tensor(y[:, 1:TOK], bx[:, m, 0:TOK - 1], taps[0], y[:, 1:TOK],
                                                    ALU.mult, ALU.add))
                        link(V.scalar_tensor_tensor(y[:, 0:TOK - 1], bx[:, m, 1:TOK], taps[2], y[:, 0:TOK - 1],
                                                    ALU.mult, ALU.add))
                    if what == 2:
                        dve.wait_ge(tile_s, u + 1)
                        V.tensor_tensor(ya[:, m, :], ya[:, m, :], bank(u), ALU.mult).then_inc(read_s[u % 4], 1)
                        dve.wait_ge(yh_s, i + 1)
                        V.tensor_tensor(y_lo[:, i, :], ya[:, m, :], y_hi[:, i, :].bitcast(F32), ALU.subtract)\
                            .then_inc(yl_s, 1)
                elif S_GA <= s < S_Z:
                    i = u - first_tile(S_GA)
                    wait_read(dve, u)
                    wait_read(dve, first_tile(S_WA) + i)
                    V.tensor_tensor(mixed[:, i, :], mixed[:, i, :], sig_a, ALU.mult).then_inc(sigau_s, 1)
                elif S_WD <= s < S_WO:
                    i = u - first_tile(S_WD)
                    dve.wait_ge(tile_s, u + 1)
                    if i >= 2:
                        dve.wait_ge(nlo_s, KD // 2 + i - 1)
                    if i == 0:
                        for q in range(4):
                            wait_read(dve, first_tile(S_WD) - 1 - q)
                    V.tensor_tensor(mg_f[:, i % 2, :], bank(u), sig_d[:, i, :], ALU.mult).then_inc(read_s[u % 4], 1)
                    if i > 0:
                        merged_lo(i - 1)
                    if i == KD - 1:
                        merged_lo(i)
                elif S_WO <= s < S_FF:
                    i = u - first_tile(S_WO)
                    dve.wait_ge(tile_s, u + 1)
                    dve.wait_ge(x2_in_s, 16)
                    V.tensor_tensor(h_t[:, i, :], h_t[:, i, :], bank(u), ALU.add).then_inc(read_s[u % 4], 1)
                    dve.wait_ge(nhi_s, 2 * KD + i + 1)
                    V.scalar_tensor_tensor(f_lo[:, i, :], h_t[:, i, :], cols[:, C_GFFN + i:C_GFFN + i + 1],
                                           f_hi[:, i, :].bitcast(F32), ALU.mult, ALU.subtract).then_inc(nlo_s, 1)

            def spread(col):
                return col.unsqueeze(2).broadcast_to([P, col.shape[1], P])

            def norm_lo(k):
                dve.wait_ge(nhi_s, k + 1)
                V.tensor_tensor(act_lo[:, k, :], n_f[:, k % 4, :], act_hi[:, k, :].bitcast(F32), ALU.subtract)\
                    .then_inc(nlo_s, 1)

            def log_decays():
                dve.wait_ge(batr_s, 1)
                V.tensor_copy(ba[:].rearrange("p c n -> p (c n)"), extra[:, 1, 0:NC * 16]).then_inc(bac_s, 1)
                dve.wait_ge(bac_s, 1)
                x, e, r, t, y, q = (tiny[:, i, :] for i in range(6))
                al = gate[:].rearrange("p c n -> p (c n)")
                dt = cols[:, C_DTB:C_DTB + 8].unsqueeze(1).broadcast_to([P, NC, 8])
                link(V.tensor_tensor(gate[:], ba[:, :, 8:16], dt, ALU.add))
                V.scalar_tensor_tensor(x, al, -1.0, al, ALU.mult, ALU.max).then_inc(abs_s, 1)
                dve.wait_ge(exp_s, 1)
                link(V.tensor_scalar(r, e, 2.0, None, ALU.add))
                link(V.reciprocal(t, r))
                link(V.tensor_tensor(t, t, e, ALU.mult))
                link(V.tensor_tensor(y, t, t, ALU.mult))
                link(V.tensor_scalar(r, y, 1.0 / 17, None, ALU.mult))
                for odd in (15, 13, 11, 9, 7, 5, 3):
                    link(V.scalar_tensor_tensor(r, r, 1.0 / odd, y, ALU.add, ALU.mult))
                link(V.scalar_tensor_tensor(r, r, 1.0, t, ALU.add, ALU.mult))
                link(V.tensor_scalar(al, al, 0.0, None, ALU.max))
                link(V.scalar_tensor_tensor(al, r, 2.0, al, ALU.mult, ALU.add))
                dve.wait_ge(aexp_s, 1)
                ea = tiny[:, 5, 0:8].unsqueeze(1).broadcast_to([P, NC, 8])
                V.scalar_tensor_tensor(gate[:], gate[:], -1.0, ea, ALU.mult, ALU.mult).then_inc(g_s, 1)
                dve.wait_ge(g_s, 1)

            def key_columns():
                dve.wait_ge(ksquare_s, NC * H)
                sq, root, rec, length, inv_sq = (k_cols[:, i, :] for i in range(5))
                V.tensor_scalar(sq, k_sq[:], EPS, None, ALU.add).then_inc(ksq_s, 1)
                dve.wait_ge(ksq_s, 1)
                link(V.reciprocal(inv_sq, sq))
                dve.wait_ge(kroot_s, 1)
                link(V.reciprocal(rec, root))
                link(V.tensor_tensor(rec, rec, sq, ALU.mult))
                link(V.tensor_tensor(rec, rec, root, ALU.add))
                link(V.tensor_scalar(length, rec, 0.5, None, ALU.mult))
                dve.wait_ge(beta_s, 1)
                for d in range(DIRS):
                    link(V.tensor_tensor(c1[:, :, d, :], beta[:, :, d * H:(d + 1) * H],
                                         inv_sq.rearrange("p (c h) -> p c h", c=NC), ALU.mult))
                shape = [P, LEVELS, NC, H]
                to, other = (t.rearrange("p l (c h) -> p l c h", h=H) for t in (c_lvl[:], c_odd))
                for d, t in enumerate((to, other)):
                    side = cols[:, C_PARITY + d * LEVELS:C_PARITY + (d + 1) * LEVELS]
                    last = V.tensor_tensor(t, c1[:, :, d, :].unsqueeze(1).broadcast_to(shape),
                                           side.unsqueeze(2).unsqueeze(3).broadcast_to(shape), ALU.mult)
                link(last)
                link(V.tensor_tensor(c_lvl[:], c_lvl[:], c_odd, ALU.add))

            def blocks(i, l):
                for h in range(H):
                    c = ORDER[i] * H + h
                    last = V.scalar_tensor_tensor(y[:, h, :], inv[:, h, :], c_lvl[:, l, c:c + 1], tri[l],
                                                  ALU.mult, ALU.mult)
                last.then_inc(y_s, 1)

            def make_k(i):
                dve.wait_ge(kk_s, i + 1)
                dve.wait_ge(dexp_s, i + 1)
                link(V.tensor_tensor(a_t, heads_of(extra[:, 1, :]), decay, ALU.mult))
                for h in range(H):
                    c = ORDER[i] * H + h
                    last = V.scalar_tensor_tensor(y[:, h, :], a_t[:, h, :], c_lvl[:, 0, c:c + 1], off[0],
                                                  ALU.mult, ALU.mult)
                link(last)
                V.tensor_tensor(inv_t[:, ORDER[i]], over_heads(ident), y, ALU.subtract).then_inc(xu_s, 1)

            def make_p(i):
                dve.wait_ge(qk_s, i + 1)
                V.tensor_tensor(qk[:, ORDER[i]], heads_of(extra[:, 0, :]), decay, ALU.mult).then_inc(p_s, 1)
                if i == 0:
                    dve.wait_ge(ecol_s, 1)
                    link(V.tensor_scalar(neg_run[:], e_cols[:, 0], -1.0, None, ALU.mult))
                    for d in range(DIRS):
                        link(V.tensor_tensor(c1_end[:, :, d, :], c1[:, :, d, :], e_cols[:, 1, d], ALU.mult))

            def turned(i, l):
                if l == 0:
                    dve.wait_ge(xt_s, level(i, 0))
                    dve.wait_ge(xu_s, level(i, 0))
                    blocks(i, 1)

            def mask_ax(i, l):
                dve.wait_ge(v_s, upper(i, l))
                V.tensor_tensor(ax, heads_of(extra[:, 0, :]), over_heads(off[l]), ALU.mult).then_inc(vm_s, 1)

            def update_inverse(i, l):
                dve.wait_ge(xvx_s, upper(i, l))
                V.tensor_tensor(inv, inv, heads_of(extra[:, 1, :]), ALU.subtract).then_inc(xu_s, 1)
                if l < LEVELS - 1:
                    dve.wait_ge(xu_s, level(i, l))
                    blocks(i, l + 1)

            def scan_read(n, d):
                dve.wait_ge(sread_s, pair(n - 1, d))
                c = chunk_of(n, d)
                b_r, b_o = scan_banks(n, d)
                for h in range(H):
                    last = V.scalar_tensor_tensor(r_buf[:, d, h, :], extra[:, b_r, h * P:(h + 1) * P],
                                                  neg_run[:, d, c, h:h + 1], v_tok[:, c, h, :], ALU.mult, ALU.add)
                last.then_inc(r_s, 1)
                if n >= NC // 2:
                    dve.wait_ge(oadd_s, pair(NC - 1 - n, 1 - d))
                for h in range(H):
                    run = e_cols[:, 0, d, c, h:h + 1]
                    if n < NC // 2:
                        last = V.tensor_scalar(o_acc[:, c, h, :], extra[:, b_o, h * P:(h + 1) * P], run, None, ALU.mult)
                    else:
                        last = V.scalar_tensor_tensor(o_acc[:, c, h, :], extra[:, b_o, h * P:(h + 1) * P], run,
                                                      o_acc[:, c, h, :], ALU.mult, ALU.add)
                last.then_inc(qs_s, 1)

            def scan_write(n, d):
                c = chunk_of(n, d)
                b_r, b_o = scan_banks(n, d)
                dve.wait_ge(in_s, pair(n, d))
                if n == 0:
                    V.tensor_copy(o_acc[:, c], heads_of(extra[:, b_o, :])).then_inc(oadd_s, 1)
                else:
                    dve.wait_ge(qs_s, pair(n - 1, d))
                    V.tensor_tensor(o_acc[:, c], o_acc[:, c], heads_of(extra[:, b_o, :]), ALU.add).then_inc(oadd_s, 1)
                if n < NC - 1:
                    dve.wait_ge(ds_s, pair(n, d))
                    if n == 0:
                        V.tensor_copy(state[:, d], heads_of(extra[:, b_r, :])).then_inc(st_s, 1)
                    else:
                        for h in range(H):
                            last = V.scalar_tensor_tensor(state[:, d, h, :], state[:, d, h, :],
                                                          e_cols[:, 2, d, c, h:h + 1], extra[:, b_r, h * P:(h + 1) * P],
                                                          ALU.mult, ALU.add)
                        last.then_inc(st_s, 1)

            def delta(what, *at):
                if what in ("make_k", "make_p", "turn", "ax", "xax", "read", "write"):
                    {"make_k": make_k, "make_p": make_p, "turn": turned, "ax": mask_ax, "xax": update_inverse,
                     "read": scan_read, "write": scan_write}[what](*at)

            def output_norm():
                dve.wait_ge(ac_s, NC * H + 2)
                dve.wait_ge(qsq_s, 1)
                link(V.tensor_scalar(norm_t[:, 5, :], q_sq[:], EPS, EPS * P, ALU.add, ALU.mult))
                V.scalar_tensor_tensor(norm_t[:, 0, :], o_sq[:], 1.0 / P, norm_t[:, 5, :], ALU.mult, ALU.add)\
                    .then_inc(omean_s, 1)
                dve.wait_ge(oroot_s, 1)
                x, root, t, to = (norm_t[:, i, :] for i in range(4))
                link(rsqrt_steps(x, root, t, to))
                flat = o_acc.rearrange("p c h n -> p (c h) n")
                V.tensor_tensor(flat, flat, spread(norm_t[:, 3, :]), ALU.mult).then_inc(onorm_s, 1)

            for k in range(2):
                dve.wait_ge(ph_s, k + 1)
                V.tensor_tensor(y_lo[:, k, :], p_in[:, k, :], y_hi[:, k, :].bitcast(F32), ALU.subtract)\
                    .then_inc(pl_s, 1)
            for q in range(LO_PARTS):
                split_lo(S_PP, q)
            for k in range(1, KD - 1):
                dve.wait_ge(sq_s, k + 1)
                if k > 1:
                    dve.wait_ge(acc_s, k - 1)
                V.tensor_tensor(acc0, sq_in[:, 0, :] if k == 1 else acc0, sq_in[:, k % SQ, :], ALU.add)\
                    .then_inc(acc_s, 1)
            split_lo(S_K, 0)
            split_lo(S_K, 1)
            norm_rstd(0)
            split_lo(S_K, 2)
            split_lo(S_K, 3)
            dve.wait_ge(rbps_s, 1)
            dve.wait_ge(cols_in_s, 16)
            for k in range(KD):
                if k >= 4:
                    dve.wait_ge(nhi_s, k - 3)
                    dve.wait_ge(nlp_s, (k - 3) // 2)
                V.scalar_tensor_tensor(n_f[:, k % 4, :], x_in[:, k, :], cols[:, C_GMIX + k:C_GMIX + k + 1],
                                       extra[:, 0, :], ALU.mult, ALU.mult).then_inc(nf_s, 1)
                if k % 2 == 1:
                    norm_lo(k - 1)
            dve.wait_ge(w16h_s, 1)
            V.tensor_tensor(w16_lo[:], cols[:, C_W16:C_W16 + KD * 16], w16_hi[:].bitcast(F32), ALU.subtract)\
                .then_inc(w16l_s, 1)

            for s in range(S_K, S_FF):
                for j in range(UNITS):
                    if j in (0, 3, 6, 9):
                        split_lo(s + 1, j // 3)
                    if (s, j) == (2, 0):
                        dve.wait_ge(ba_s, 1)
                        V.tensor_copy(ba_t[0:16, :], extra[0:16, 1, :]).then_inc(bat_s, 1)
                    m = tile_ends(s, j)
                    if m is not None:
                        finish_tile(s, m)
                    if (s, j) == (2, 2):
                        log_decays()
                    if (s, j) == (3, 13):
                        key_columns()
                    if 6 <= s <= 7 and j in (4, 12):
                        i = 2 * (s - 4) + (j == 12)
                        dve.wait_ge(tr_s, i + 1)
                        V.tensor_tensor(v_tok[:, :, i - H, :], extra[:, 2 + i % 2, :].rearrange("p (c n) -> p c n", c=NC),
                                        spread(k_cols[:, 3, :].rearrange("p (c h) -> p c h", c=NC)[:, :, i - H]),
                                        ALU.mult).then_inc(vcopy_s, 1)
                    if (s, j) == (5, 13):
                        dve.wait_ge(ss_s, H)
                        V.tensor_copy(q_rows[0:H, :], extra[0:H, 3, :]).then_inc(qrow_s, 1)
                    if (s, j) == (6, 4):
                        dve.wait_ge(qturn_s, 1)
                        V.tensor_copy(q_sq[:], extra[:, 3, 0:NC * H]).then_inc(qsq_s, 1)
                    for step in DELTA.get(s * UNITS + j, ()):
                        delta(*step)
                    if (s, j) == (22, 2):
                        output_norm()
                    if (s, j) == (23, 10):
                        for h in range(H):
                            dve.wait_ge(otr_s, h + 1)
                            wait_read(dve, first_tile(S_Z) + h)
                            if h >= 2:
                                dve.wait_ge(yh_s, H + h - 1)
                                dve.wait_ge(yl_s, H + h - 1)
                            V.scalar_tensor_tensor(yd_f[:, h % 2, :], extra[:, h, :], cols[:, C_GDN:C_GDN + 1],
                                                   z_silu[:, h, :], ALU.mult, ALU.mult).then_inc(yd_s, 1)
                            dve.wait_ge(yh_s, H + h + 1)
                            V.tensor_tensor(y_lo[:, h, :], yd_f[:, h % 2, :], y_hi[:, h, :].bitcast(F32), ALU.subtract)\
                                .then_inc(yl_s, 1)

            def ff_group(i, first, last):
                for b in range(FF_SLABS):
                    r = (S_FF + b + 1) % RING
                    for q in range(LO_PARTS):
                        dve.wait_ge(hi_s, i * (HI_PARTS * FF_SLABS)
                                    + (HI_PARTS * (S_FF + b + 1) + q * HI_PARTS // LO_PARTS + 1))
                        V.tensor_tensor(part(w_lo, r, q, LO_PARTS), part(raw, r, q, LO_PARTS),
                                        part(w_hi, r, q, LO_PARTS).bitcast(F32), ALU.subtract).then_inc(lo_s, 1)
                    if first and b == 0:
                        norm_rstd(1)
                        dve.wait_ge(rb_s, 1)
                    for m in range(2):
                        u = 2 * b + m
                        dve.wait_ge(tile_s, i * 16 + (FF_T0 + u + 1))
                        if b < FF_SLABS // 2:
                            if not first or b > 0:
                                dve.wait_ge(hf_s, i * 8 + (u - 1))
                            V.scalar_tensor_tensor(relu_t[:, m, :], bank(u), 0.0, rb, ALU.max, ALU.mult)\
                                .then_inc(read_s[u % 4], 1)
                            dve.wait_ge(hf_s, i * 8 + (u + 1))
                            V.tensor_tensor(hid_lo[:, u, :], hid_f[:, m, :], hid_hi[:, u, :].bitcast(F32), ALU.subtract)\
                                .then_inc(hl_s, 1)
                        else:
                            k = u - 8
                            V.tensor_tensor(h_t[:, k, :], h_t[:, k, :], bank(u), ALU.add).then_inc(read_s[u % 4], 1)
                            if last:
                                dve.wait_ge(nhi_s, 3 * KD + k + 1)
                                V.scalar_tensor_tensor(act_lo[:, k, :], h_t[:, k, :],
                                                       cols[:, C_GPLE + k:C_GPLE + k + 1],
                                                       act_hi[:, k, :].bitcast(F32), ALU.mult, ALU.subtract)\
                                    .then_inc(nlo_s, 1)

            ff_group(0, True, False)
            with dve.Fori(1, FF_GROUPS - 1) as i:
                ff_group(i, False, False)
            ff_group(FF_GROUPS - 1, False, True)

            norm_rstd(2)
            for q in range(LO_PARTS):
                split_lo(S_PG + 1, q)
            dve.wait_ge(rb_s, 2)
            dve.wait_ge(ple_in_s, 16)
            for s in range(S_PG, N_SLABS - 1):
                if S_PG < s:
                    for q in range(LO_PARTS):
                        split_lo(s + 1, q)
                for m in range(2):
                    i = 2 * (s - S_PG) + m
                    u = first_tile(s) + m
                    dve.wait_ge(tile_s, u + 1)
                    V.tensor_tensor(sig_p[:, m, :], bank(u), rb, ALU.mult).then_inc(read_s[u % 4], 1)
                    dve.wait_ge(gp_s, i + 1)
                    link(V.tensor_tensor(sig_p[:, m, :], sig_p[:, m, :], ple[:, i, :], ALU.mult))
                    V.tensor_tensor(h_t[:, i, :], h_t[:, i, :], sig_p[:, m, :], ALU.add).then_inc(hp_s, 1)
            def finish(half):
                t = slice(half * HALF, (half + 1) * HALF)
                dve.wait_ge(rb_s, 3 + half)
                for k in range(5):
                    V.scalar_tensor_tensor(h_t[:, k, t], h_t[:, k, t], cols[:, C_GFIN + k:C_GFIN + k + 1], rb[:, t],
                                           ALU.mult, ALU.mult).then_inc(fin_s, 1)

            for q in range(4):
                half, m = divmod(q, 2)
                u, k = T_LAST + q, KD - 2 + m
                t = slice(half * HALF, (half + 1) * HALF)
                dve.wait_ge(tile_s, u + 1)
                V.tensor_tensor(sig_p[:, m, t], bank(u)[:, 0:HALF], rb[:, t], ALU.mult).then_inc(read_s[u % 4], 1)
                dve.wait_ge(gp_s, KD - 2 + q + 1)
                link(V.tensor_tensor(sig_p[:, m, t], sig_p[:, m, t], ple[:, k, t], ALU.mult))
                V.tensor_tensor(h_t[:, k, t], h_t[:, k, t], sig_p[:, m, t], ALU.add).then_inc(hp_s, 1)
                if q == 1:
                    norm_rstd(3)
            finish(0)
            norm_rstd(4)
            finish(1)

        @block.gpsimd
        def _(pool):
            G = nc.gpsimd

            def delta(what, i, l=0):
                if what == "gates" and l == 0:
                    if i == 0:
                        pool.wait_ge(g_s, 1)
                    else:
                        pool.wait_ge(dsum_s, i)
                    for h in range(H):
                        last = G.tensor_scalar(gate_f[:, h, :], incl[0], gate[:, ORDER[i], h:h + 1], None, ALU.mult)
                    last.then_inc(gm_s, 1)
                if what == "turn" and l < LEVELS - 1:
                    if l == 0:
                        pool.wait_ge(xu_s, level(i, 0))
                        pool.wait_ge(p_s, i + 1)
                    else:
                        pool.wait_ge(xt_s, level(i, l))
                    G.tensor_tensor(z_t, inv_t[:, ORDER[i]], over_heads(tri[l + 1]), ALU.mult).then_inc(z_s, 1)
                if what == "tri":
                    n, d = i, l
                    slot, sign = slot_of(n, d), 1 - 2 * d
                    keep = dict(compare_op=ALU.is_ge, fill=0.0, base=0, pattern=[[0, H], [sign, P]],
                                channel_multiplier=-sign)
                    pool.wait_ge(xt_s, level(ORDER.index(chunk_of(n, d)), LEVELS - 1))
                    if (n, d) == (1, 1):
                        pool.wait_ge(xt_s, level(NC - 1, LEVELS - 1))
                    elif n > 1 or d == 1 or n == 1:
                        before = pair(0, 0) if n == 0 else pair(0, 1) if n == 1 else pair(n - 1, d)
                        pool.wait_ge(xr_s, before)
                        pool.wait_ge(in_s, before)
                    G.affine_select(out=tri_x[slot], in_=inv_t[:, chunk_of(n, d)], **keep).then_inc(trix_s, 1)
                    G.affine_select(out=tri_qk[slot], in_=qk[:, chunk_of(n, d)], **keep).then_inc(triqk_s, 1)

            for k in range(1, KD, 2):
                pool.wait_ge(nhi_s, k + 1)
                G.tensor_tensor(act_lo[:, k, :], n_f[:, k % 4, :], act_hi[:, k, :].bitcast(F32), ALU.subtract)\
                    .then_inc(nlp_s, 1)

            for at in sorted(DELTA):
                for step in DELTA[at]:
                    delta(*step)

            for i in range(KD):
                wait_read(pool, first_tile(S_WD) + i)
                pool.wait_ge(sigau_s, i + 1)
                G.tensor_tensor(mg_f[:, i % 2, :], mg_f[:, i % 2, :], mixed[:, i, :], ALU.add).then_inc(mg_s, 1)

            for r in range(1, 4):
                for k in range(1, KD - 2 * (r == 3)):
                    pool.wait_ge(sq_s, r * KD + k + 1)
                    if k > 1:
                        pool.wait_ge(acc_s, added(r, k - 1))
                    elif r > 1:
                        pool.wait_ge(sqsum_s, r)
                    G.tensor_tensor(acc, sq_t[:, 0, :] if k == 1 else acc, sq_t[:, k % SQ, :], ALU.add)\
                        .then_inc(acc_s, 1)
            for half in range(2):
                pool.wait_ge(rb_s, 3 + half)
                for k in range(5, KD):
                    pool.wait_ge(gain_s, 1 if k == 5 else k - 4 + 2 * half)
                    t = slice(half * HALF, (half + 1) * HALF)
                    G.tensor_tensor(h_t[:, k, t], h_t[:, k, t], rb[:, t], ALU.mult).then_inc(finp_s, 1)


def _slabs(w, nk, width):
    n = w.shape[1]
    return w.reshape(nk, P, n // width, width).transpose(2, 1, 0, 3).reshape(n // width, P, nk * width)


def _features(a):
    return np.ascontiguousarray(a.T.reshape(-1, P, TOK).transpose(1, 0, 2))


def _masks():
    i = np.arange(P)
    row, col = i[:, None], i[None, :]
    m = np.stack([row == col, row <= col, row >= col, row > col, row < col, row >= 0 * col], axis=1)
    same = [row >> l == col >> l for l in range(LEVELS + 1)]
    levels = [same[l + 1] & ~same[l] for l in range(LEVELS)]
    for l in range(1, LEVELS):
        levels.append(same[l] & np.where(row >> l & 1, row <= col, row >= col))
    return m.astype(np.float32), np.stack(levels, axis=1)


def kernel(**inputs):
    import ml_dtypes
    import concourse.bacc as bacc
    from concourse.bass_utils import run_bass_kernel_spmd

    a = {n: np.asarray(v) for n, v in inputs.items()}
    w_in = a["w_in"][0]
    b_at, c_at, x_at, q_at, k_at, v_at, z_at = (512 * i for i in range(7))
    ga_at = z_at + 512 + 16
    gd_at = ga_at + D

    def part(at, n):
        return _slabs(w_in[:, at:at + n], KD, 256)

    bxc = [part(at + 256 * g, 256) for g in range(2) for at in (b_at, x_at, c_at)]
    ff = []
    w1, w2 = a["w_ff1"][0], a["w_ff2"][0]
    for g in range(FF_GROUPS):
        ff += [_slabs(w1[:, D * g:D * (g + 1)], KD, 256), _slabs(w2[D * g:D * (g + 1)], KD, 256)]
    stream = np.concatenate(
        [_slabs(a["w_ple_proj"][0], 2, 1024), part(k_at, 512), part(q_at, 512), part(v_at, 512), *bxc,
         _slabs(a["w_a_out"][0], H, 512), part(ga_at, D), part(z_at, 512), part(gd_at, D),
         _slabs(a["w_dn_out"][0], H, 512), _slabs(a["w_o"][0], KD, 256), *ff,
         _slabs(a["w_ple_gate"][0], KD, 256)])
    assert stream.shape == (N_SLABS, P, SLAB)

    cols = np.zeros((P, N_COLS), np.float32)

    def put(at, m):
        cols[:, at:at + m.shape[1]] = m

    put(C_GMIX, a["g_mix"][0].reshape(KD, P).T)
    put(C_GFFN, a["g_ffn"][0].reshape(KD, P).T)
    put(C_GPLE, a["g_ple"][0].reshape(KD, P).T)
    put(C_GFIN, a["g_final"].reshape(KD, P).T)
    put(C_CONVA, a["conv_a"][0].reshape(3 * H, P).T)
    put(C_CONVQ, a["conv_qkv"][0].reshape(3 * 3 * H, P).T)
    put(C_GDN, a["g_dn_norm"][0].reshape(1, P).T)
    for at, f, b in ((C_ALOG, "a_log_f", "a_log_b"), (C_DTB, "dt_bias_f", "dt_bias_b")):
        put(at, np.broadcast_to(a[f], (P, H)))
        put(at + H, np.broadcast_to(a[b], (P, H)))
    odd = np.arange(P)[:, None] >> np.arange(LEVELS) & 1
    put(C_PARITY, np.concatenate([1 - odd, odd], axis=1).astype(np.float32))
    put(C_PICK, np.broadcast_to(np.eye(H, dtype=np.float32).reshape(1, H * H), (P, H * H)))
    put(C_W16, w_in[:, z_at + 512:ga_at].reshape(KD, P, 16).transpose(1, 0, 2).reshape(P, KD * 16))
    masks, levels = _masks()

    arrays = {"x_in_dram": _features(a["x"][0]), "p_in_dram": _features(a["p"][0, 0]), "stream": stream,
              "cols_in": cols, "masks_in": masks, "levels_in": levels.astype(ml_dtypes.bfloat16)}
    nc = bacc.Bacc("TRN2", target_bir_lowering=False, num_devices=1)
    args = [nc.dram_tensor(n, v.shape, mybir.dt.from_np(v.dtype), kind="ExternalInput").ap()
            for n, v in arrays.items()]
    args.append(nc.dram_tensor("out_t", (P, KD, TOK), F32, kind="ExternalOutput").ap())
    args.append(nc.dram_tensor("ple_kept", (P, KD, TOK), F32, kind="Internal").ap())
    encoder_block(nc, *args)
    got = run_bass_kernel_spmd(nc, [arrays], core_ids=[0]).results[0]["out_t"]
    return np.asarray(got).transpose(2, 1, 0).reshape(1, TOK, D)
```
